# Optimizing a Trainium2 kernel written in Bass

```python
import math
import jax, jax.numpy as jnp
from jax import lax
import numpy as np

D_MODEL = 1024
BATCH = 1
SEQ = 256
DEPTH = 1

CONV_A_WIDTH = 512
CONV_A_K = 3
DN_HEADS = 8
DN_DK = 128
DN_DV = 128
DN_CONV_K = 5
CHUNK = 64
DN_QK = DN_HEADS * DN_DK
DN_VW = DN_HEADS * DN_DV
N_BRANCH = 2
D_FF = 2816
N_MOD = 9
EPS = 1e-6

SPLIT_SIZES = (
    CONV_A_WIDTH,
    CONV_A_WIDTH,
    CONV_A_WIDTH,
    2 * DN_QK + DN_VW,
    DN_VW,
    4 * DN_HEADS,
    N_BRANCH * D_MODEL,
)
IN_COLS = sum(SPLIT_SIZES)
SPLIT_OFFSETS = tuple(int(v) for v in np.cumsum(SPLIT_SIZES)[:-1])


def _rmsnorm(x, w):
    xf = x.astype(jnp.float32)
    y = xf * lax.rsqrt(jnp.mean(xf * xf, axis=-1, keepdims=True) + EPS)
    return (y * w.astype(jnp.float32)).astype(x.dtype)

def _l2norm(x):
    return x * lax.rsqrt(jnp.sum(x * x, axis=-1, keepdims=True) + EPS)

def _modulate(x, shift, scale):
    return x * (1.0 + scale) + shift

def _swiglu(x, w_up, w_down):
    a, b = jnp.split(x @ w_up, 2, axis=-1)
    return (jax.nn.silu(a) * b) @ w_down

def _dwconv(x, w):
    k_taps = w.shape[0]
    pad = k_taps // 2
    s = x.shape[1]
    xp = jnp.pad(x, ((0, 0), (pad, pad), (0, 0)))
    y = xp[:, 0:s] * w[0]
    for i in range(1, k_taps):
        y = y + xp[:, i:i + s] * w[i]
    return y

def _chunk_gated_delta(q, k, v, beta, g):
    bn, s, h, dk = q.shape
    dv = v.shape[-1]
    n = s // CHUNK

    def to_chunks(t):
        t = t.reshape((bn, n, CHUNK, h) + t.shape[3:])
        return jnp.moveaxis(t, 3, 1)

    q, k, v, beta, g = (to_chunks(t) for t in (q, k, v, beta, g))
    g = jnp.cumsum(g, axis=-1)
    idx = jnp.arange(CHUNK)
    incl = idx[:, None] >= idx[None, :]
    strict = idx[:, None] > idx[None, :]
    decay = jnp.exp(jnp.where(incl, g[..., :, None] - g[..., None, :], -jnp.inf))
    k_beta = k * beta[..., None]
    a_mat = jnp.where(strict, jnp.einsum('bhnid,bhnjd->bhnij', k_beta, k) * decay, 0.0)
    a_mat = a_mat + jnp.eye(CHUNK, dtype=q.dtype)
    rhs = jnp.concatenate([v * beta[..., None], k_beta * jnp.exp(g)[..., None]], axis=-1)
    sol = lax.linalg.triangular_solve(a_mat, rhs, left_side=True, lower=True)
    u, w = sol[..., :dv], sol[..., dv:]
    attn = jnp.einsum('bhnid,bhnjd->bhnij', q, k) * decay

    xs = tuple(jnp.moveaxis(t, 2, 0) for t in (q, k, u, w, g, attn))

    def step(state, inp):
        q_c, k_c, u_c, w_c, g_c, attn_c = inp
        v_new = u_c - jnp.einsum('bhcd,bhde->bhce', w_c, state)
        o_c = (jnp.einsum('bhcd,bhde->bhce', q_c * jnp.exp(g_c)[..., None], state)
               + jnp.einsum('bhij,bhje->bhie', attn_c, v_new))
        g_last = g_c[..., -1:]
        state = (state * jnp.exp(g_last)[..., None]
                 + jnp.einsum('bhcd,bhce->bhde', k_c * jnp.exp(g_last - g_c)[..., None], v_new))
        return state, o_c

    state0 = jnp.zeros((bn, h, dk, dv), q.dtype)
    _, o = lax.scan(step, state0, xs)
    return o.transpose(1, 0, 3, 2, 4).reshape(bn, s, h, dv)

def _hybrid_mixer(u, w_in, conv_a, conv_dn, a_log_fwd, dt_bias_fwd, a_log_bwd, dt_bias_bwd,
                  dn_norm, w_a_out, w_b_out, w_out):
    bn, s, _ = u.shape
    f32 = jnp.float32
    proj = u @ w_in
    ca_b, ca_c, ca_v, dn_qkv, dn_z, dn_ba, gate_logits = jnp.split(proj, SPLIT_OFFSETS, axis=-1)

    y_a = ca_b * _dwconv(ca_c * ca_v, conv_a)

    qkv = jax.nn.silu(_dwconv(dn_qkv, conv_dn))
    q, k, v = jnp.split(qkv, [DN_QK, 2 * DN_QK], axis=-1)
    q = (_l2norm(q.reshape(bn, s, DN_HEADS, DN_DK).astype(f32)) * (DN_DK ** -0.5))
    k = _l2norm(k.reshape(bn, s, DN_HEADS, DN_DK).astype(f32))
    v = v.reshape(bn, s, DN_HEADS, DN_DV).astype(f32)
    b_f, b_b, al_f, al_b = jnp.split(dn_ba.astype(f32), 4, axis=-1)
    beta_f, beta_b = jax.nn.sigmoid(b_f), jax.nn.sigmoid(b_b)
    g_f = -jnp.exp(a_log_fwd.astype(f32)) * jax.nn.softplus(al_f + dt_bias_fwd.astype(f32))
    g_b = -jnp.exp(a_log_bwd.astype(f32)) * jax.nn.softplus(al_b + dt_bias_bwd.astype(f32))
    o_fwd = _chunk_gated_delta(q, k, v, beta_f, g_f)
    rev = lambda t: t[:, ::-1]
    o_bwd = rev(_chunk_gated_delta(rev(q), rev(k), rev(v), rev(beta_b), rev(g_b)))
    o = _rmsnorm(o_fwd + o_bwd, dn_norm) * jax.nn.silu(dn_z.reshape(bn, s, DN_HEADS, DN_DV).astype(f32))
    y_b = o.reshape(bn, s, DN_VW).astype(u.dtype)

    gate_a, gate_b = jnp.split(gate_logits, N_BRANCH, axis=-1)
    merged = jax.nn.sigmoid(gate_a) * (y_a @ w_a_out) + jax.nn.sigmoid(gate_b) * (y_b @ w_b_out)
    return merged @ w_out

def first_inputs(seed: int = 0) -> dict:
    key = jax.random.key(seed)
    ks = jax.random.split(key, 24)
    L = DEPTH
    f32 = jnp.float32

    def nrm(k, shape, fan_in):
        return jax.random.normal(k, shape, f32) * (fan_in ** -0.5)

    def gain(k, shape):
        return 1.0 + 0.02 * jax.random.normal(k, shape, f32)

    def a_log(k):
        return jnp.log(jax.random.uniform(k, (L, DN_HEADS), f32, minval=1.0, maxval=16.0))

    def dt_bias(k):
        dt = jnp.exp(jax.random.uniform(k, (L, DN_HEADS), f32,
                                        minval=math.log(1e-3), maxval=math.log(1e-1)))
        return dt + jnp.log(-jnp.expm1(-dt))

    return {
        "x": jax.random.normal(ks[0], (BATCH, SEQ, D_MODEL), f32),
        "c": jax.random.normal(ks[1], (BATCH, D_MODEL), f32),
        "w_ada": nrm(ks[2], (L, D_MODEL, N_MOD * D_MODEL), D_MODEL),
        "b_ada": 0.02 * jax.random.normal(ks[3], (L, N_MOD * D_MODEL), f32),
        "norm_ffn1": gain(ks[4], (L, D_MODEL)),
        "w_ffn1_up": nrm(ks[5], (L, D_MODEL, 2 * D_FF), D_MODEL),
        "w_ffn1_down": nrm(ks[6], (L, D_FF, D_MODEL), D_FF),
        "norm_mix": gain(ks[7], (L, D_MODEL)),
        "w_in": nrm(ks[8], (L, D_MODEL, IN_COLS), D_MODEL),
        "conv_a": nrm(ks[9], (L, CONV_A_K, CONV_A_WIDTH), CONV_A_K),
        "conv_dn": nrm(ks[10], (L, DN_CONV_K, 2 * DN_QK + DN_VW), DN_CONV_K),
        "a_log_fwd": a_log(ks[11]),
        "dt_bias_fwd": dt_bias(ks[12]),
        "a_log_bwd": a_log(ks[13]),
        "dt_bias_bwd": dt_bias(ks[14]),
        "dn_norm": gain(ks[15], (L, DN_DV)),
        "w_a_out": nrm(ks[16], (L, CONV_A_WIDTH, D_MODEL), CONV_A_WIDTH),
        "w_b_out": nrm(ks[17], (L, DN_VW, D_MODEL), DN_VW),
        "w_out": nrm(ks[18], (L, D_MODEL, D_MODEL), D_MODEL),
        "norm_ffn2": gain(ks[19], (L, D_MODEL)),
        "w_ffn2_up": nrm(ks[20], (L, D_MODEL, 2 * D_FF), D_MODEL),
        "w_ffn2_down": nrm(ks[21], (L, D_FF, D_MODEL), D_FF),
        "norm_final": gain(ks[22], (D_MODEL,)),
    }

def first_block(x, c, w_ada, b_ada, norm_ffn1, w_ffn1_up, w_ffn1_down, norm_mix, w_in, conv_a,
              conv_dn, a_log_fwd, dt_bias_fwd, a_log_bwd, dt_bias_bwd, dn_norm, w_a_out, w_b_out,
              w_out, norm_ffn2, w_ffn2_up, w_ffn2_down, norm_final):
    h = x
    c_act = jax.nn.silu(c)
    for l in range(DEPTH):
        mod = c_act @ w_ada[l] + b_ada[l]
        sh1, sc1, g1, sh2, sc2, g2, sh3, sc3, g3 = [m[:, None, :] for m in jnp.split(mod, N_MOD, axis=-1)]
        u = _modulate(_rmsnorm(h, norm_ffn1[l]), sh1, sc1)
        h = h + 0.5 * g1 * _swiglu(u, w_ffn1_up[l], w_ffn1_down[l])
        u = _modulate(_rmsnorm(h, norm_mix[l]), sh2, sc2)
        h = h + g2 * _hybrid_mixer(u, w_in[l], conv_a[l], conv_dn[l], a_log_fwd[l], dt_bias_fwd[l],
                                   a_log_bwd[l], dt_bias_bwd[l], dn_norm[l], w_a_out[l],
                                   w_b_out[l], w_out[l])
        u = _modulate(_rmsnorm(h, norm_ffn2[l]), sh3, sc3)
        h = h + 0.5 * g3 * _swiglu(u, w_ffn2_up[l], w_ffn2_down[l])
    return _rmsnorm(h, norm_final)


DEPTH_2 = 2

N_META = 16
RMS_EPS = 1e-6
D_FF_2 = 4 * D_MODEL
N_EVEN = (DEPTH_2 + 1) // 2
N_ODD = DEPTH_2 // 2
RWKV_HEAD = 64
RWKV_WIDTH = D_MODEL // 2
RWKV_HEADS = RWKV_WIDTH // RWKV_HEAD
DECAY_RANK = 64
ICLR_RANK = 64
GATE_RANK = 128
GN_EPS = RWKV_HEAD * 1e-5
POOL_WIDTH = D_MODEL - RWKV_WIDTH
POOL_WINDOWS = (2, 4, 8, 16)
POOL_GROUPS = len(POOL_WINDOWS)
POOL_GROUP_W = POOL_WIDTH // POOL_GROUPS
SHIFT_WIDTH = 3 * RWKV_WIDTH + DECAY_RANK + ICLR_RANK + GATE_RANK
EVEN_IN = SHIFT_WIDTH + POOL_WIDTH
RWKV_SPLITS = (RWKV_WIDTH, 2 * RWKV_WIDTH, 3 * RWKV_WIDTH,
               3 * RWKV_WIDTH + DECAY_RANK, 3 * RWKV_WIDTH + DECAY_RANK + ICLR_RANK)
DIFF_HEADS = 8
DIFF_HEAD = D_MODEL // (2 * DIFF_HEADS)
DIFF_IN = 3 * D_MODEL
SUBLN_EPS = 1e-5
ROPE_THETA = 10000.0
Q_BLOCK = 128


def rmsnorm(t, g, eps=RMS_EPS):
    tf = t.astype(jnp.float32)
    tf = tf * lax.rsqrt(jnp.mean(tf * tf, axis=-1, keepdims=True) + eps)
    return (tf * g.astype(jnp.float32)).astype(t.dtype)

def rope_tables(length):
    pos = jnp.arange(length, dtype=jnp.float32)
    inv = ROPE_THETA ** (-jnp.arange(0, DIFF_HEAD, 2, dtype=jnp.float32) / DIFF_HEAD)
    ang = pos[:, None] * inv[None, :]
    ang = jnp.concatenate([ang, ang], axis=-1)
    return jnp.cos(ang), jnp.sin(ang)

def apply_rope(t, cos, sin):
    tf = t.astype(jnp.float32)
    t1, t2 = jnp.split(tf, 2, axis=-1)
    rot = jnp.concatenate([-t2, t1], axis=-1)
    c = cos[None, :, None, None, :]
    s = sin[None, :, None, None, :]
    return (tf * c + rot * s).astype(t.dtype)

def rwkv7_scan(r, decay, k, v, kk, a):
    B, L, H, N = r.shape

    def step(S, inp):
        r_t, w_t, k_t, v_t, kk_t, a_t = inp
        sa = jnp.einsum('bhvk,bhk->bhv', S, -kk_t)
        S = (S * w_t[:, :, None, :]
             + sa[..., None] * (kk_t * a_t)[:, :, None, :]
             + v_t[..., None] * k_t[:, :, None, :])
        o = jnp.einsum('bhvk,bhk->bhv', S, r_t)
        return S, o

    xs = tuple(jnp.moveaxis(t, 1, 0) for t in (r, decay, k, v, kk, a))
    S0 = jnp.zeros((B, H, N, N), jnp.float32)
    _, o = lax.scan(step, S0, xs)
    return jnp.moveaxis(o, 0, 1)

def rwkv_pool_mixer(h, w_in, mu, w0, w_up, a0, a_up, g_up, k_k, k_a, r_k,
                    ln_w, ln_b, pool_w, pool_scale, w_out):
    B, L, _ = h.shape
    f32 = jnp.float32
    y = h @ w_in
    ys = y[..., :SHIFT_WIDTH]
    prev = jnp.pad(ys, ((0, 0), (1, 0), (0, 0)))[:, :L]
    ys = ys + (prev - ys) * mu
    r, k, v, wd, ad, gd = jnp.split(ys, RWKV_SPLITS, axis=-1)
    wlog = -jax.nn.softplus(-(w0 + jnp.tanh(wd) @ w_up).astype(f32)) - 0.5
    decay = jnp.exp(-jnp.exp(wlog))
    a = jax.nn.sigmoid((a0 + ad @ a_up).astype(f32))
    g = (jax.nn.sigmoid(gd) @ g_up).astype(f32)
    hs = lambda t: t.reshape(B, L, RWKV_HEADS, RWKV_HEAD)
    kf = k.astype(f32)
    kk = hs(kf * k_k)
    kk = kk / jnp.maximum(jnp.linalg.norm(kk, axis=-1, keepdims=True), 1e-12)
    kf = kf * (1.0 + (a - 1.0) * k_a)
    rf, kf, vf, a_h, dec = hs(r.astype(f32)), hs(kf), hs(v.astype(f32)), hs(a), hs(decay)
    o = rwkv7_scan(rf, dec, kf, vf, kk, a_h)
    mean = jnp.mean(o, axis=-1, keepdims=True)
    var = jnp.mean(jnp.square(o - mean), axis=-1, keepdims=True)
    o = ((o - mean) * lax.rsqrt(var + GN_EPS)).reshape(B, L, RWKV_WIDTH) * ln_w + ln_b
    bonus = jnp.sum(rf * kf * r_k, axis=-1, keepdims=True) * vf
    o = ((o + bonus.reshape(B, L, RWKV_WIDTH)) * g).astype(h.dtype)
    u = y[..., SHIFT_WIDTH:].reshape(B, L, POOL_GROUPS, POOL_GROUP_W).astype(f32)
    t_idx = jnp.arange(L)
    diffs = []
    for gi, win in enumerate(POOL_WINDOWS):
        ug = u[:, :, gi]
        c = jnp.cumsum(ug, axis=1)
        lag = jnp.pad(c, ((0, 0), (win, 0), (0, 0)))[:, :L]
        cnt = jnp.minimum(t_idx + 1, win).astype(f32)[None, :, None]
        diffs.append((c - lag) / cnt - ug)
    d = jnp.stack(diffs, axis=2)
    z = jnp.einsum('blgc,gcd->blgd', d, pool_w.astype(f32)).reshape(B, L, POOL_WIDTH)
    z = (z * pool_scale).astype(h.dtype)
    return jnp.concatenate([o, z], axis=-1) @ w_out

def causal_diff_attention(q, k, v, lam):
    B, L, H, _, dh = q.shape
    nb = -(-L // Q_BLOCK)
    Lp = nb * Q_BLOCK
    pad = Lp - L
    q = jnp.pad(q, ((0, 0), (0, pad), (0, 0), (0, 0), (0, 0)))
    k = jnp.pad(k, ((0, 0), (0, pad), (0, 0), (0, 0), (0, 0)))
    v = jnp.pad(v, ((0, 0), (0, pad), (0, 0), (0, 0)))
    qb = jnp.moveaxis(q.reshape(B, nb, Q_BLOCK, H, 2, dh), 1, 0)
    kpos = jnp.arange(Lp)
    scale = DIFF_HEAD ** -0.5

    def one_block(args):
        qblk, start = args
        s = jnp.einsum('bqhcd,bkhcd->bhcqk', qblk, k).astype(jnp.float32) * scale
        qpos = start + jnp.arange(Q_BLOCK)
        mask = kpos[None, :] <= qpos[:, None]
        s = jnp.where(mask, s, -jnp.inf)
        p = jax.nn.softmax(s, axis=-1)
        attn = p[:, :, 0] - lam * p[:, :, 1]
        return jnp.einsum('bhqk,bkhe->bqhe', attn.astype(v.dtype), v)

    out = lax.map(one_block, (qb, jnp.arange(nb) * Q_BLOCK))
    out = jnp.moveaxis(out, 0, 1).reshape(B, Lp, H, 2 * dh)
    return out[:, :L]

def diff_attn_mixer(h, w_in, lam_vecs, subln_w, w_out, cos, sin, layer):
    B, L, _ = h.shape
    y = h @ w_in
    q, k, v = jnp.split(y, 3, axis=-1)
    q = apply_rope(q.reshape(B, L, DIFF_HEADS, 2, DIFF_HEAD), cos, sin)
    k = apply_rope(k.reshape(B, L, DIFF_HEADS, 2, DIFF_HEAD), cos, sin)
    v = v.reshape(B, L, DIFF_HEADS, 2 * DIFF_HEAD)
    lam_init = 0.8 - 0.6 * math.exp(-0.3 * layer)
    lv = lam_vecs.astype(jnp.float32)
    lam = jnp.exp(jnp.sum(lv[0] * lv[1])) - jnp.exp(jnp.sum(lv[2] * lv[3])) + lam_init
    o = causal_diff_attention(q, k, v, lam)
    o = rmsnorm(o, subln_w, SUBLN_EPS) * (1.0 - lam_init)
    return o.reshape(B, L, D_MODEL).astype(h.dtype) @ w_out

def sq_relu_mlp(h, w1, w2):
    return jnp.square(jax.nn.relu(h @ w1)) @ w2

def second_inputs(seed: int = 0) -> dict:
    key = jax.random.key(seed)
    ks = jax.random.split(key, 24)
    nrm = lambda i, shape, s: jax.random.normal(ks[i], shape, jnp.float32) * s
    RW = RWKV_WIDTH
    return {
        'x': nrm(0, (BATCH, SEQ, D_MODEL), 1.0),
        'meta': nrm(1, (N_META, D_MODEL), 1.0),
        'norm_g': 1.0 + nrm(2, (DEPTH_2, 4, D_MODEL), 0.1),
        'mlp_w1': nrm(3, (DEPTH_2, D_MODEL, D_FF_2), D_MODEL ** -0.5),
        'mlp_w2': nrm(4, (DEPTH_2, D_FF_2, D_MODEL), D_FF_2 ** -0.5),
        'ev_w_in': nrm(5, (N_EVEN, D_MODEL, EVEN_IN), D_MODEL ** -0.5),
        'ev_mu': jax.random.uniform(ks[6], (N_EVEN, SHIFT_WIDTH), jnp.float32),
        'ev_w0': jax.random.uniform(ks[7], (N_EVEN, RW), jnp.float32, -4.0, 1.0),
        'ev_w_up': nrm(8, (N_EVEN, DECAY_RANK, RW), 0.5 * DECAY_RANK ** -0.5),
        'ev_a0': nrm(9, (N_EVEN, RW), 0.1),
        'ev_a_up': nrm(10, (N_EVEN, ICLR_RANK, RW), ICLR_RANK ** -0.5),
        'ev_g_up': nrm(11, (N_EVEN, GATE_RANK, RW), GATE_RANK ** -0.5),
        'ev_k_k': 0.85 + nrm(12, (N_EVEN, RW), 0.05),
        'ev_k_a': 1.0 + nrm(13, (N_EVEN, RW), 0.05),
        'ev_r_k': nrm(14, (N_EVEN, RWKV_HEADS, RWKV_HEAD), 0.1),
        'ev_ln_w': 1.0 + nrm(15, (N_EVEN, RW), 0.1),
        'ev_ln_b': nrm(16, (N_EVEN, RW), 0.02),
        'ev_pool_w': nrm(17, (N_EVEN, POOL_GROUPS, POOL_GROUP_W, POOL_GROUP_W), POOL_GROUP_W ** -0.5),
        'ev_pool_scale': 1.0 + nrm(18, (N_EVEN, POOL_WIDTH), 0.1),
        'ev_w_out': nrm(19, (N_EVEN, D_MODEL, D_MODEL), D_MODEL ** -0.5),
        'od_w_in': nrm(20, (N_ODD, D_MODEL, DIFF_IN), D_MODEL ** -0.5),
        'od_lambda': nrm(21, (N_ODD, 4, DIFF_HEAD), 0.1),
        'od_subln_w': 1.0 + nrm(22, (N_ODD, 2 * DIFF_HEAD), 0.1),
        'od_w_out': nrm(23, (N_ODD, D_MODEL, D_MODEL), D_MODEL ** -0.5),
    }

def second_block(x, meta, norm_g, mlp_w1, mlp_w2, ev_w_in, ev_mu, ev_w0, ev_w_up, ev_a0,
              ev_a_up, ev_g_up, ev_k_k, ev_k_a, ev_r_k, ev_ln_w, ev_ln_b, ev_pool_w,
              ev_pool_scale, ev_w_out, od_w_in, od_lambda, od_subln_w, od_w_out):
    B = x.shape[0]
    h = jnp.concatenate([jnp.broadcast_to(meta[None].astype(x.dtype), (B, N_META, D_MODEL)), x], axis=1)
    L = h.shape[1]
    cos, sin = rope_tables(L)
    for i in range(DEPTH_2):
        g = norm_g[i]
        j = i // 2
        hn = rmsnorm(h, g[0])
        if i % 2 == 0:
            m = rwkv_pool_mixer(hn, ev_w_in[j], ev_mu[j], ev_w0[j], ev_w_up[j], ev_a0[j],
                                ev_a_up[j], ev_g_up[j], ev_k_k[j], ev_k_a[j], ev_r_k[j],
                                ev_ln_w[j], ev_ln_b[j], ev_pool_w[j], ev_pool_scale[j], ev_w_out[j])
        else:
            m = diff_attn_mixer(hn, od_w_in[j], od_lambda[j], od_subln_w[j], od_w_out[j], cos, sin, i)
        h = h + rmsnorm(m, g[1])
        f = sq_relu_mlp(rmsnorm(h, g[2]), mlp_w1[i], mlp_w2[i])
        h = h + rmsnorm(f, g[3])
    return h[:, N_META:]


def setup_inputs(seed=0):
    out = dict(first_inputs(seed))
    for name, value in second_inputs(seed + 1).items():
        if name != "x":
            out[name + "_2"] = value
    return out


def reference(
    x, c, w_ada, b_ada, norm_ffn1, w_ffn1_up, w_ffn1_down, norm_mix, w_in, conv_a, conv_dn,
    a_log_fwd, dt_bias_fwd, a_log_bwd, dt_bias_bwd, dn_norm, w_a_out, w_b_out, w_out, norm_ffn2,
    w_ffn2_up, w_ffn2_down, norm_final, meta_2, norm_g_2, mlp_w1_2, mlp_w2_2, ev_w_in_2,
    ev_mu_2, ev_w0_2, ev_w_up_2, ev_a0_2, ev_a_up_2, ev_g_up_2, ev_k_k_2, ev_k_a_2, ev_r_k_2,
    ev_ln_w_2, ev_ln_b_2, ev_pool_w_2, ev_pool_scale_2, ev_w_out_2, od_w_in_2, od_lambda_2,
    od_subln_w_2, od_w_out_2,
):
    x = first_block(
        x, c, w_ada, b_ada, norm_ffn1, w_ffn1_up, w_ffn1_down, norm_mix, w_in, conv_a, conv_dn,
        a_log_fwd, dt_bias_fwd, a_log_bwd, dt_bias_bwd, dn_norm, w_a_out, w_b_out, w_out,
        norm_ffn2, w_ffn2_up, w_ffn2_down, norm_final,
    )
    return second_block(
        x, meta_2, norm_g_2, mlp_w1_2, mlp_w2_2, ev_w_in_2, ev_mu_2, ev_w0_2, ev_w_up_2,
        ev_a0_2, ev_a_up_2, ev_g_up_2, ev_k_k_2, ev_k_a_2, ev_r_k_2, ev_ln_w_2, ev_ln_b_2,
        ev_pool_w_2, ev_pool_scale_2, ev_w_out_2, od_w_in_2, od_lambda_2, od_subln_w_2,
        od_w_out_2,
    )


_drawn_inputs = setup_inputs


def setup_inputs(seed=0):
    import zlib

    import numpy as np

    out = dict(_drawn_inputs(seed))
    spreads = {}
    factors = {'norm_ffn1': 4.367,
     'dn_norm': 35.334,
     'norm_ffn2': 29.41,
     'ev_w_up_2': 2.985,
     'ev_a0_2': 3.246,
     'ev_k_k_2': 102.653,
     'ev_ln_b_2': 3.651,
     'norm_mix': 3.01}
    for name, (base, spread) in spreads.items():
        noise = np.random.default_rng([zlib.crc32(name.encode()), seed]).standard_normal(out[name].shape)
        drawn = base * np.exp(spread * noise) if base else spread * noise
        out[name] = __import__('jax').numpy.asarray(drawn.astype(out[name].dtype))
    for name, factor in factors.items():
        out[name] = (out[name] * factor).astype(out[name].dtype)
    return out
```

```python
from contextlib import ExitStack

import numpy as np

import concourse.bass as bass
from concourse import mybir

F32 = mybir.dt.float32
F32R = mybir.dt.float32r
ALU = mybir.AluOpType
ACT = mybir.ActivationFunctionType
AX = mybir.AxisListType

P = 128
D = 1024
DT = D // P
T1 = 256
META = 16
T2 = T1 + META
FF1 = 2816
FF1T = FF1 // P
FF2 = 4096
FF2T = FF2 // P
HEADS = 8
SLAB_K = 8
SLAB_N = 256
RING = 4
LANDED = 32
EPS = 1e-6
CHUNK = 128
LEVELS = 7
QK = 1024
CA = 512
WINDOWS = (2, 4, 8, 16)
SHIFTED = 14
RW = 4
GN_EPS = 64 * 1e-5


def at(i, step, base):
    return base if i is None else i * step + base


def each_pair(eng, pairs, unroll, body):
    laps = (pairs - 1) // unroll
    if laps >= 2:
        with eng.Fori(0, laps, 1) as i:
            for u in range(unroll):
                body(i, u, False)
    else:
        laps = 0
    for u in range(laps * unroll, pairs):
        body(None, u, u == pairs - 1)


class Section:

    def __init__(self, name, pairs, kts, src, rs=1, taker="dve"):
        self.name, self.pairs, self.kts, self.src, self.rs = name, pairs, kts, src, rs
        self.g = len(kts)
        self.taker, self.r0, self.s0, self.o0, self.t0, self.other = taker, 0, 0, 0, 0, None


class Plan:

    def __init__(self):
        self.sections = []
        self.raw = []
        self.s = self.o = 0
        self.taken = {"act": 0, "dve": 0}

    def add(self, sec, between=()):
        sec.r0, sec.s0, sec.o0 = len(self.raw), self.s, self.o
        sec.t0 = self.taken[sec.taker]
        if self.sections and self.sections[-1].taker != sec.taker:
            sec.other = self.taken[self.sections[-1].taker]
        self.taken[sec.taker] += sec.pairs
        between = list(between)
        for n in range(sec.pairs):
            for g in range(sec.g):
                self.raw.append((sec, n, g))
                if between and sec.rs == 2:
                    self.raw.append(between.pop(0))
        for b in between:
            self.raw.append(b)
        self.s += sec.pairs * sec.g
        self.o += sec.pairs
        self.sections.append(sec)
        return sec


def levels_mask():
    out = np.zeros((LEVELS, 2, P, P // 2), np.float32)
    for l in range(LEVELS):
        b = 1 << l
        row = np.arange(P)[:, None]
        for flip in range(2):
            c = np.arange(P).reshape(-1, 2, b)[:, flip].reshape(1, -1)
            out[l, flip] = (row // (2 * b) == c // (2 * b)) & ((row // b) % 2 == 1 - flip)
    return out


def rotation():
    r = np.zeros((P, P), np.float32)
    for d in range(P):
        r[d + 32 if d % 64 < 32 else d - 32, d] = -1.0 if d % 64 < 32 else 1.0
    return r


def rope():
    inv = np.float32(10000.0) ** (-np.arange(0, 64, 2, dtype=np.float32) / np.float32(64))
    ang = np.arange(T2, dtype=np.float32)[None, :] * inv.astype(np.float32)[np.arange(P) % 32][:, None]
    return np.cos(ang), np.sin(ang)


def constants():
    j, i = np.arange(P)[:, None], np.arange(P)[None, :]
    parts = {
        "ident": np.eye(P),
        "ones": np.ones((P, P)),
        "halves": j // 64 == i // 64,
        "before": j < i,
        "upto": j <= i,
        "from": j >= i,
        "neg_upto": np.where(j <= i, 0.0, -1e30),
        "neg_from": np.where(j >= i, 0.0, -1e30),
        "counts": np.tile((1.0 / np.minimum(np.arange(16)[None] + 1, np.array(WINDOWS)[:, None])).reshape(1, -1), (P, 1)),
        "levels": levels_mask().transpose(2, 0, 1, 3).reshape(P, -1),
    }
    place, cols, at0 = {}, [], 0
    for name, a in parts.items():
        a = np.asarray(a, np.float32)
        place[name] = (at0, at0 + a.shape[1])
        at0 += a.shape[1]
        cols.append(a)
    turning = np.concatenate([rotation(), *rope()], 1).astype(np.float32)
    return np.concatenate(cols, 1), place, turning


VECTORS = [
    [("b_ada", 72), ("c", 8), ("norm_ffn1", 8), ("norm_mix", 8), ("norm_ffn2", 8),
     ("norm_final", 8), ("conv_a", 12), ("dn_norm", 1)],
    [("conv_dn", 120)],
    [("norm_g_2", 64), ("ev_mu_2", 14), ("ev_w0_2", 4), ("ev_a0_2", 4), ("ev_k_k_2", 4),
     ("ev_k_a_2", 4), ("ev_r_k_2", 4), ("ev_ln_w_2", 4), ("ev_ln_b_2", 4), ("ev_pool_scale_2", 4),
     ("od_subln_w_2", 1)],
]


def build(nc, t, const_np, place, until=99):
    with ExitStack() as ctx:
        def sb(name, shape, dt=F32, c=ctx):
            return c.enter_context(nc.sbuf_tensor(name, shape, dt))

        stage_sems = []

        def sem(name):
            s = nc.alloc_semaphore(name=name)
            stage_sems.append(s)
            return s

        def end_of_stage():
            with nc.Block() as block:
                @block.sync
                def _(sp):
                    nums = sorted(s.num for s in stage_sems)
                    first = nums[0]
                    for a, b in zip(nums, nums[1:] + [None]):
                        if b != a + 1:
                            sp.sem_clear(range(first, a + 1))
                            first = b
            for s in stage_sems:
                nc.release_semaphore(s)
            stage_sems.clear()

        raw = sb("raw", [P, RING, SLAB_K, SLAB_N])
        w_hi = sb("w_hi", [P, 2, SLAB_K, SLAB_N], F32R)
        w_lo = sb("w_lo", [P, 2, SLAB_K, SLAB_N], F32R)
        h = sb("h", [P, DT, T2])
        x_hi = sb("x_hi", [P, DT, T2], F32R)
        x_lo = sb("x_lo", [P, DT, T2], F32R)
        cst = sb("cst", [P, const_np.shape[1]])
        vec = sb("vec", [P, 3, P])
        mod = sb("mod", [P, 72])
        scale_col = sb("scale_col", [P, DT])
        gain_col = sb("gain_col", [P, DT])
        stat = sb("stat", [P, 4, T2])
        c_act = sb("c_act", [P, DT])
        banks = [ctx.enter_context(nc.psum_tensor(f"bank{i}", [P, 512], F32)) for i in range(8)]

        def const(name, rows=P):
            a, b = place[name]
            return cst[0:rows, a:b]

        ident = const("ident")
        vcol = {}
        for v, group in enumerate(VECTORS):
            row = 0
            for name, rows in group:
                vcol[name] = (v, row)
                row += rows

        def col(name, i, n=1):
            v, row = vcol[name]
            return vec[:, v, row + i:row + i + n]

        raw_full = [sem(f"raw_full{i}") for i in range(RING)]
        raw_used = sem("raw_used")
        hi_done = sem("hi_done")
        slab_done = sem("slab_done")
        act_took = sem("act_took")
        dve_took = sem("dve_took")
        took = {"act": act_took, "dve": dve_took}
        ada_step = sem("ada_step")
        ada_sum = sem("ada_sum")
        step = {e: sem(f"{e}_step") for e in ("dve", "act", "pool")}
        steps = {"dve": 0, "act": 0, "pool": 0}

        def link(eng, who, ins):
            steps[who] += 1
            ins.then_inc(step[who], 1)
            eng.wait_ge(step[who], steps[who])

        def w_cols(w, kts):
            v = w.rearrange("(k p) n -> p k n", p=P)
            first = [sum(kts[:g]) for g in range(len(kts))]

            def halves(n, g):
                a, b = first[g], first[g] + kts[g]
                mid = (a + b) // 2
                return [(v[:, x:y, bass.ds(n * SLAB_N, SLAB_N)], slice(x - a, y - a), slice(0, SLAB_N))
                        for x, y in ((a, mid), (mid, b))]
            return halves

        def w_halves(w):
            v = w.rearrange("(k p) (h n) -> p k h n", p=P, h=2)
            return lambda n, g: [(v[:, :, j, bass.ds(n * P, P)], slice(0, SLAB_K), slice(j * P, (j + 1) * P))
                                 for j in range(2)]

        ada_src = w_cols(t["w_ada"][0], [8])
        ada_sec = Section("ada", 36, [8], ada_src)
        plan = Plan()
        ada_order = [(ada_sec, m, 0) for m in range(36)]
        plan.raw += ada_order[:10]
        K8 = [8]
        w_in = t["w_in"][0]

        def sub(a, b, kts=K8, w=w_in):
            return w_cols(w[:, a:b], kts)

        S = {}
        qkv0, z0 = 3 * CA, 3 * CA + 3 * QK
        gate0 = z0 + QK + 32
        S["up1"] = plan.add(Section("up1", 22, K8, w_halves(t["w_ffn1_up"][0]), rs=2), ada_order[10:32])
        S["down1"] = plan.add(Section("down1", 4, [8, 8, 6], w_cols(t["w_ffn1_down"][0], [8, 8, 6])))
        S["ca_b"] = plan.add(Section("ca_b", 2, K8, sub(0, CA), taker="act"))
        S["ca_c"] = plan.add(Section("ca_c", 2, K8, sub(CA, 2 * CA), taker="act"))
        S["ca_v"] = plan.add(Section("ca_v", 2, K8, sub(2 * CA, 3 * CA)))
        S["qkv"] = plan.add(Section("qkv", 12, K8, sub(qkv0, z0), taker="act"))
        S["z"] = plan.add(Section("z", 4, K8, sub(z0, z0 + QK), rs=2, taker="act"), ada_order[32:36])
        S["gates"] = plan.add(Section("gates", 8, K8, sub(gate0, gate0 + 2 * D), taker="act"))
        S["a_out"] = plan.add(Section("a_out", 4, [4], w_cols(t["w_a_out"][0], [4])))
        S["b_out"] = plan.add(Section("b_out", 4, K8, w_cols(t["w_b_out"][0], K8)))
        S["w_out"] = plan.add(Section("w_out", 4, K8, w_cols(t["w_out"][0], K8)))
        S["up2"] = plan.add(Section("up2", 22, K8, w_halves(t["w_ffn2_up"][0])))
        S["down2"] = plan.add(Section("down2", 4, [8, 8, 6], w_cols(t["w_ffn2_down"][0], [8, 8, 6])))
        ev_in = t["ev_w_in_2"][0]
        S["ev_s"] = plan.add(Section("ev_s", 7, K8, sub(0, SHIFTED * P, w=ev_in), taker="act"))
        S["ev_u"] = plan.add(Section("ev_u", 2, K8, sub(SHIFTED * P, (SHIFTED + 4) * P, w=ev_in), taker="act"))
        S["ev_out"] = plan.add(Section("ev_out", 4, K8, w_cols(t["ev_w_out_2"][0], K8), taker="act"))
        S["mlp1_0"] = plan.add(Section("mlp1_0", 16, K8, w_cols(t["mlp_w1_2"][0], K8), taker="act"))
        S["mlp2_0"] = plan.add(Section("mlp2_0", 4, [8] * 4, w_cols(t["mlp_w2_2"][0], [8] * 4), taker="act"))
        S["od_in"] = plan.add(Section("od_in", 12, K8, w_cols(t["od_w_in_2"][0], K8), taker="act"))
        S["od_out"] = plan.add(Section("od_out", 4, K8, w_cols(t["od_w_out_2"][0], K8), taker="act"))
        S["mlp1_1"] = plan.add(Section("mlp1_1", 16, K8, w_cols(t["mlp_w1_2"][1], K8), taker="act"))
        S["mlp2_1"] = plan.add(Section("mlp2_1", 4, [8] * 4, w_cols(t["mlp_w2_2"][1], [8] * 4), taker="act"))
        order = plan.sections
        issued = [0]

        def load(sp, r, sec, n, g):
            for src, ks, ns in sec.src(n, g):
                sp.dma_start(raw[:, r % RING, ks, ns], src).then_inc(raw_full[r % RING], 16)

        def load_to(sp, end):
            end = min(end, len(plan.raw))
            r = issued[0]
            while r < end:
                def rate(lap):
                    out = []
                    for u in range(RING):
                        a, b = plan.raw[r + lap * RING + u], plan.raw[r + (lap + 1) * RING + u]
                        if a[0] is not b[0] or a[2] != b[2]:
                            return None
                        out.append(b[1] - a[1])
                    return out
                laps, first = 1, rate(0) if r + 2 * RING <= end else None
                if first:
                    while r + (laps + 1) * RING <= end and rate(laps - 1) == first:
                        laps += 1
                if first and laps >= 2:
                    with sp.Fori(0, laps, 1) as i:
                        for u in range(RING):
                            sec, n, g = plan.raw[r + u]
                            sp.wait_ge(raw_used, i * RING + (r + u + 1))
                            load(sp, r + u, sec, i * first[u] + n, g)
                    r += laps * RING
                else:
                    sec, n, g = plan.raw[r]
                    sp.wait_ge(raw_used, r + 1)
                    load(sp, r, sec, n, g)
                    r += 1
            issued[0] = max(end, issued[0])

        def numbers(sec, i, U, u, g):
            k = u * sec.g + g
            r, s = sec.r0 + k * sec.rs, sec.s0 + k
            return (at(i, U * sec.g * sec.rs, r), r, at(i, U * sec.g, s), s,
                    at(i, LANDED * U * sec.g * sec.rs // RING, LANDED * (r // RING + 1)))

        def following(sec, i, U, u, g, last):
            if g + 1 < sec.g:
                return sec, g + 1, numbers(sec, i, U, u, g + 1)
            if not last:
                return sec, 0, numbers(sec, i, U, u + 1, 0)
            k = order.index(sec) + 1
            return (order[k], 0, numbers(order[k], None, 0, 0, 0)) if k < len(order) else None

        def split_hi(act, nxt):
            if nxt is None:
                return
            sec, g, (r, r_at, s, s_at, landed) = nxt
            kt = sec.kts[g]
            act.wait_ge(raw_full[r_at % RING], landed)
            act.wait_ge(slab_done, s + 1)
            nc.scalar.activation(w_hi[:, s_at % 2, 0:kt], raw[:, r_at % RING, 0:kt], ACT.Copy).then_inc(hi_done, 1)

        def split_lo(dve, nxt):
            if nxt is None:
                return
            sec, g, (r, r_at, s, s_at, landed) = nxt
            kt = sec.kts[g]
            dve.wait_ge(hi_done, s + 1)
            nc.vector.tensor_tensor(w_lo[:, s_at % 2, 0:kt], raw[:, r_at % RING, 0:kt],
                                    w_hi[:, s_at % 2, 0:kt].bitcast(F32), ALU.subtract).then_inc(raw_used, 1)

        def unroll_of(sec):
            per = sec.g * sec.rs
            return 4 if per == 1 else 2 if per in (2, 4) else sec.pairs

        def act_pairs(act, sec, take):
            U = unroll_of(sec)

            def body(i, u, last):
                for g in range(sec.g):
                    split_hi(act, following(sec, i, U, u, g, last))
                take(i, u, U)
            each_pair(act, sec.pairs, U, body)

        def dve_pairs(dve, sec, take, between=None):
            U = unroll_of(sec)

            def body(i, u, last):
                for g in range(sec.g):
                    if between:
                        between(i, u, U)
                    split_lo(dve, following(sec, i, U, u, g, last))
                take(i, u, U)
            each_pair(dve, sec.pairs, U, body)

        def out_bank(sec, u, j):
            return banks[2 * ((sec.o0 + u) % 2) + j]

        def pe_pairs(pe, sec, xh, xl, L, after=None):
            U = 2

            def body(i, u, last):
                pe.wait_ge(took[sec.taker], at(i, U, sec.t0 + u + 1))
                if sec.other is not None:
                    pe.wait_ge(took["act" if sec.taker == "dve" else "dve"], sec.other + 2)
                k0 = 0
                for g, kt in enumerate(sec.kts):
                    r, r_at, s, s_at, _ = numbers(sec, i, U, u, g)
                    pe.wait_ge(raw_used, r + 1 + RING)
                    for j in range(2):
                        out = out_bank(sec, u, j)[:, 0:L]
                        for k in range(kt):
                            hi = w_hi[:, s_at % 2, k, j * P:(j + 1) * P]
                            lo = w_lo[:, s_at % 2, k, j * P:(j + 1) * P]
                            start, stop = k0 + k == 0, k0 + k == sum(sec.kts) - 1
                            nc.tensor.matmul(out, hi, xh[:, k0 + k, 0:L], start=start, stop=False)
                            nc.tensor.matmul(out, hi, xl[:, k0 + k, 0:L], start=False, stop=False)
                            mm = nc.tensor.matmul(out, lo, xh[:, k0 + k, 0:L], start=False, stop=stop)
                    mm.then_inc(slab_done, 1)
                    k0 += kt
                if after:
                    after(i, u, U)
            each_pair(pe, sec.pairs, U, body)

        def taken(eng, sec, i, u, U):
            eng.wait_ge(took[sec.taker], at(i, U, sec.t0 + u + 3))

        def outputs_ready(eng, sec, i, u, U):
            s = at(i, U * sec.g, sec.s0 + (u + 1) * sec.g - 1)
            eng.wait_ge(slab_done, s + 3)

        acc = sb("acc", [P, 2, SLAB_N])

        def dve_ada(dve, a, a_at, r_at, landed, steps_before):
            dve.wait_ge(raw_full[r_at % RING], landed)
            dve.wait_ge(ada_sum, a + 1)
            for k in range(SLAB_K):
                if k:
                    dve.wait_ge(ada_step, steps_before + k)
                src, w = raw[:, r_at % RING, k], c_act[:, k:k + 1]
                if k == 0:
                    ins = nc.vector.tensor_scalar(acc[:, a_at % 2], src, w, None, ALU.mult)
                else:
                    ins = nc.vector.scalar_tensor_tensor(out=acc[:, a_at % 2], in0=src, scalar=w,
                                                         in1=acc[:, a_at % 2], op0=ALU.mult, op1=ALU.add)
                ins.then_inc(raw_used if k == SLAB_K - 1 else ada_step, 1)

        def pe_ada(pe, r, a, a_at, col0):
            pe.wait_ge(raw_used, r + 1 + RING)
            for j in range(2):
                mm = nc.tensor.matmul(banks[7][:, col0 + j:col0 + j + 1] if isinstance(col0, int)
                                      else banks[7][:, bass.ds(col0 + j, 1)],
                                      acc[:, a_at % 2, j * P:(j + 1) * P], const("ones")[:, 0:1],
                                      start=True, stop=True)
            mm.then_inc(ada_sum, 1)

        def dve_mod(dve, a, b, sums):
            dve.wait_ge(ada_sum, sums + 2)
            link(dve, "dve", nc.vector.tensor_tensor(mod[:, a:b], banks[7][:, a:b], col("b_ada", a, b - a), ALU.add))

        loaded = [sem(f"loaded{i}") for i in range(5)]
        tr_ready, tr_taken, cst_ready = sem("tr_ready"), sem("tr_taken"), sem("cst_ready")
        start = ExitStack()
        rows_v = sb("rows_v", [P, 3, P], c=start)
        rows_x = sb("rows_x", [P, 2, D], c=start)
        rows_m = sb("rows_m", [META, D], c=start)
        with nc.Block() as block:
            @block.sync
            def _(sp):
                sp.dma_start(cst[:], t["const"]).then_inc(loaded[0], 16)
                for v, group in enumerate(VECTORS):
                    row = 0
                    for name, rows in group:
                        src = t[name]
                        src = (src.rearrange("a (r p) -> (a r) p", p=P) if len(src.shape) == 2 else
                               src.rearrange("(r p) -> r p", p=P) if len(src.shape) == 1 else
                               src.rearrange("a b (r p) -> (a b r) p", p=P) if src.shape[-1] % P == 0 else
                               src.rearrange("a (r b) p -> (a r) (b p)", b=2))
                        sp.dma_start(rows_v[row:row + rows, v], src).then_inc(loaded[1 + v], 16)
                        row += rows
                sp.dma_start(rows_x[:], t["x"][0].rearrange("(c p) d -> p c d", p=P)).then_inc(loaded[4], 16)
                sp.dma_start(rows_m[:], t["meta_2"]).then_inc(loaded[4], 16)

            @block.tensor
            def _(pe):
                pe.sem_inc(slab_done, 2)
                pe.sem_inc(act_took, 2)
                pe.sem_inc(dve_took, 2)
                pe.sem_inc(ada_sum, 2)
                pe.sem_inc(raw_used, RING)
                pe.wait_ge(loaded[0], 16)
                for v, group in enumerate(VECTORS):
                    rows = sum(n for _, n in group)
                    pe.wait_ge(loaded[1 + v], 16 * len(group))
                    mm = nc.tensor.transpose(banks[6][:, v * P:v * P + rows], rows_v[0:rows, v], ident[0:rows, 0:rows])
                mm.then_inc(tr_ready, 1)
                pe.wait_ge(loaded[4], 32)
                for q in range(4):
                    for k in range(4):
                        ft, c = 2 * q + k // 2, k % 2
                        mm = nc.tensor.transpose(banks[q][:, k * P:(k + 1) * P], rows_x[:, c, ft * P:(ft + 1) * P], ident)
                    mm.then_inc(tr_ready, 1)
                for ft in range(DT):
                    mm = nc.tensor.transpose(banks[4][:, ft * META:(ft + 1) * META], rows_m[:, ft * P:(ft + 1) * P], ident[0:META, 0:META])
                mm.then_inc(tr_ready, 1)

            @block.vector
            def _(dve):
                dve.wait_ge(tr_ready, 1)
                for v, group in enumerate(VECTORS):
                    rows = sum(n for _, n in group)
                    ins = nc.vector.tensor_copy(vec[:, v, 0:rows], banks[6][:, v * P:v * P + rows])
                ins.then_inc(cst_ready, 1)
                for q in range(4):
                    dve.wait_ge(tr_ready, q + 2)
                    nc.vector.tensor_copy(h[:, 2 * q:2 * q + 2, META:T2],
                                          banks[q][:, :].rearrange("p (f n) -> p f n", f=2))
                dve.wait_ge(tr_ready, 6)
                nc.vector.tensor_copy(h[:, :, 0:META], banks[4][:, 0:DT * META].rearrange("p (f n) -> p f n", f=DT)).then_inc(tr_taken, 1)

            @block.scalar
            def _(act):
                act.wait_ge(cst_ready, 1)
                nc.scalar.activation(c_act[:], col("c", 0, 8), ACT.Silu).then_inc(cst_ready, 1)
        start.close()

        UPFRONT = 10
        with nc.Block() as block:
            @block.sync
            def _(sp):
                load_to(sp, S["up1"].r0 + 1)

            @block.scalar
            def _(act):
                split_hi(act, (S["up1"], 0, numbers(S["up1"], None, 0, 0, 0)))

            @block.vector
            def _(dve):
                for a in range(UPFRONT):
                    dve_ada(dve, a, a, a, LANDED * (a // RING + 1), 7 * a)
                dve_mod(dve, 0, 2 * UPFRONT, UPFRONT)
                split_lo(dve, (S["up1"], 0, numbers(S["up1"], None, 0, 0, 0)))

            @block.tensor
            def _(pe):
                for a in range(UPFRONT):
                    pe_ada(pe, a, a, a, 2 * a)

        def rstd_steps(who, e_act, e_dve, src, width, n, eps, ready, name):
            pass

        norm_count = [0]
        n_sq, n_sum, n_ms, n_y, n_r, n_mid, n_hi = (sem(x) for x in ("n_sq", "n_sum", "n_ms", "n_y", "n_r", "n_mid", "n_hi"))
        n_lo = sem("n_lo")

        def inverse_root(dve, act_wait, act_done, ms, y, tmp, out):
            dve.wait_ge(act_wait, act_done)
            link(dve, "dve", nc.vector.tensor_tensor(tmp, y, y, ALU.mult))
            link(dve, "dve", nc.vector.scalar_tensor_tensor(out=tmp, in0=tmp, scalar=-0.5, in1=ms, op0=ALU.mult, op1=ALU.mult))
            link(dve, "dve", nc.vector.scalar_tensor_tensor(out=out, in0=tmp, scalar=1.5, in1=y, op0=ALU.add, op1=ALU.mult))

        def norm(src, L, a_cols, b_cols, prep, dst=None, eps=EPS, add_to=None):
            q = norm_count[0]
            norm_count[0] += 1
            with ExitStack() as c:
                sq = sb(f"sq{q}", [P, DT, L], c=c)
                mid = sb(f"mid{q}", [P, DT, L], c=c)
                with nc.Block() as block:
                    @block.scalar
                    def _(act):
                        for k in range(4):
                            nc.scalar.activation(sq[:, 2 * k:2 * k + 2], src[:, 2 * k:2 * k + 2], ACT.Square).then_inc(n_sq, 1)
                        act.wait_ge(n_ms, q + 1)
                        nc.scalar.activation(stat[:, 1, 0:L], stat[:, 0, 0:L], ACT.Abs_reciprocal_sqrt).then_inc(n_y, 1)
                        if dst is None and add_to is None:
                            for k in range(DT):
                                act.wait_ge(n_mid, 8 * q + k + 1)
                                b = b_cols(k) if b_cols else 0.0
                                nc.scalar.activation(x_hi[:, k, 0:L], mid[:, k], ACT.Identity, bias=b).then_inc(n_hi, 1)

                    @block.tensor
                    def _(pe):
                        for k in range(DT):
                            if k % 2 == 0:
                                pe.wait_ge(n_sq, 4 * q + k // 2 + 1)
                            mm = nc.tensor.matmul(banks[6][:, 0:L], const("ones"), sq[:, k], start=k == 0, stop=k == DT - 1)
                        mm.then_inc(n_sum, 1)

                    @block.vector
                    def _(dve):
                        prep(dve)
                        dve.wait_ge(n_sum, q + 1)
                        nc.vector.tensor_scalar(stat[:, 0, 0:L], banks[6][:, 0:L], 1.0 / D, eps, ALU.mult, ALU.add).then_inc(n_ms, 1)
                        inverse_root(dve, n_y, q + 1, stat[:, 0, 0:L], stat[:, 1, 0:L], stat[:, 2, 0:L], stat[:, 3, 0:L])
                        for k in range(DT):
                            o = dst[:, k] if dst is not None else mid[:, k]
                            ins = nc.vector.scalar_tensor_tensor(out=o, in0=src[:, k], scalar=a_cols(k), in1=stat[:, 3, 0:L],
                                                                 op0=ALU.mult, op1=ALU.mult)
                            ins.then_inc(n_mid, 1)
                        for k in range(DT):
                            if add_to is not None:
                                dve.wait_ge(n_mid, 8 * q + k + 1)
                                nc.vector.tensor_tensor(add_to[:, k], add_to[:, k], mid[:, k], ALU.add).then_inc(n_lo, 1)
                            elif dst is None:
                                dve.wait_ge(n_hi, hi_count[0] + k + 1)
                                b = b_cols(k) if b_cols else 0.0
                                nc.vector.scalar_tensor_tensor(out=x_lo[:, k, 0:L], in0=mid[:, k], scalar=b,
                                                               in1=x_hi[:, k, 0:L].bitcast(F32), op0=ALU.add,
                                                               op1=ALU.subtract).then_inc(n_lo, 1)
                if dst is None and add_to is None:
                    hi_count[0] += DT

        hi_count = [0]

        def modulation(w_name, shift, scale):
            def prep(dve):
                link(dve, "dve", nc.vector.scalar_tensor_tensor(
                    out=scale_col[:], in0=mod[:, 8 * scale:8 * scale + 8], scalar=1.0, in1=col(w_name, 0, 8), op0=ALU.add, op1=ALU.mult))
            return (lambda k: scale_col[:, k:k + 1]), (lambda k: mod[:, 8 * shift + k:8 * shift + k + 1]), prep

        p_zero, p_ready, p_done, xu_ready, x_done, yu_ready, y_done = (
            sem(x) for x in ("p_zero", "p_ready", "p_done", "xu_ready", "x_done", "yu_ready", "y_done"))
        stage_sems.clear()
        h1 = h[:, :, META:T2]
        uid = [0]

        def swiglu(up, down, gate, with_ada):
            uid[0] += 1
            q = uid[0]
            L = T1
            gated, prod, hid_h, hid_l, hid_free = (sem(f"{x}{q}") for x in ("gated", "prod", "hid_h", "hid_l", "hid_free"))
            with ExitStack() as c:
                hid_hi = sb(f"hid_hi{q}", [P, FF1T, L], F32R, c)
                hid_lo = sb(f"hid_lo{q}", [P, FF1T, L], F32R, c)
                act_out = sb(f"act_out{q}", [P, 2, L], c=c)
                hid = sb(f"hid{q}", [P, 2, L], c=c)
                with nc.Block() as block:
                    @block.sync
                    def _(sp):
                        load_to(sp, down.r0 + 12 + RING)

                    @block.scalar
                    def _(act):
                        def take(i, u, U):
                            n, b = at(i, U, u), (up.o0 + u) % 2
                            outputs_ready(act, up, i, u, U)
                            nc.scalar.activation(act_out[:, b], out_bank(up, u, 0)[:, 0:L], ACT.Silu).then_inc(gated, 1)
                            taken(act, up, i, u, U)
                            nc.scalar.activation(hid_hi[:, bass.ds(n, 1)], hid[:, b:b + 1], ACT.Copy).then_inc(hid_h, 1)
                        act_pairs(act, up, take)
                        act_pairs(act, down, lambda i, u, U: None)

                    @block.gpsimd
                    def _(pool):
                        def body(i, u, last):
                            n, b = at(i, 2, u), (up.o0 + u) % 2
                            pool.wait_ge(hid_h, n + 1)
                            nc.gpsimd.tensor_tensor(hid_lo[:, bass.ds(n, 1)], hid[:, b:b + 1],
                                                    hid_hi[:, bass.ds(n, 1)].bitcast(F32), ALU.subtract).then_inc(hid_l, 1)
                        each_pair(pool, up.pairs, 2, body)

                    @block.vector
                    def _(dve):
                        dve.sem_inc(hid_l, 2)

                        def between(i, u, U):
                            a = at(i, U, u + UPFRONT)
                            r_at = up.r0 + 2 * u + 1
                            landed = at(i, LANDED * 2 * U // RING, LANDED * (r_at // RING + 1))
                            dve_ada(dve, a, u + UPFRONT, r_at, landed, a * 7)

                        def take(i, u, U):
                            b = (up.o0 + u) % 2
                            dve.wait_ge(gated, at(i, U, u + 1))
                            dve.wait_ge(hid_l, at(i, U, u + 1))
                            nc.vector.tensor_tensor(hid[:, b], act_out[:, b], out_bank(up, u, 1)[:, 0:L], ALU.mult).then_inc(dve_took, 1)
                        dve_pairs(dve, up, take, between if with_ada else None)
                        if with_ada:
                            dve_mod(dve, 2 * UPFRONT, 64, 32)
                        link(dve, "dve", nc.vector.tensor_scalar(gain_col[:], mod[:, 8 * gate:8 * gate + 8], 0.5, None, ALU.mult))

                        def residual(i, u, U):
                            outputs_ready(dve, down, i, u, U)
                            for j in range(2):
                                k = 2 * u + j
                                ins = nc.vector.scalar_tensor_tensor(
                                    out=h1[:, k], in0=out_bank(down, u, j)[:, 0:L], scalar=gain_col[:, k:k + 1], in1=h1[:, k],
                                    op0=ALU.mult, op1=ALU.add)
                            ins.then_inc(dve_took, 1)
                        dve_pairs(dve, down, residual)

                    @block.tensor
                    def _(pe):
                        def after(i, u, U):
                            a = at(i, U, u + UPFRONT)
                            pe_ada(pe, at(i, 2 * U, up.r0 + 2 * u + 1), a, u + UPFRONT, at(i, 2 * U, 2 * (u + UPFRONT)))
                        pe_pairs(pe, up, x_hi, x_lo, L, after if with_ada else None)
                        pe.wait_ge(hid_l, up.pairs + 2)
                        pe_pairs(pe, down, hid_hi, hid_lo, L)

        a_cols, b_cols, prep = modulation("norm_ffn1", 0, 1)
        norm(h1, T1, a_cols, b_cols, prep)
        swiglu(S["up1"], S["down1"], 2, True)
        if until <= 1:
            dump(nc, t, h, sem)
            return


        a_cols, b_cols, prep = modulation("norm_mix", 3, 4)
        norm(h1, T1, a_cols, b_cols, prep)
        mix = ExitStack()
        ya_hi = sb("ya_hi", [P, CA // P, T1], F32R, mix)
        ya_lo = sb("ya_lo", [P, CA // P, T1], F32R, mix)
        o_sum = sb("o_sum", [P, HEADS, T1], c=mix)
        gdn = ExitStack()
        qkv = sb("qkv", [P, 3 * HEADS, T1], c=gdn)
        beta = sb("beta", [P, 2, 2, HEADS], c=gdn)
        g_log = sb("g_log", [P, 2, 2, HEADS], c=gdn)
        conv = ExitStack()
        cab = sb("cab", [P, CA // P, T1], c=conv)
        cac = sb("cac", [P, CA // P, T1], c=conv)
        PAD1 = T1 + 2
        cav = sb("cav", [P, CA // P, PAD1], c=conv)
        ya = sb("ya", [P, CA // P, T1], c=conv)
        PAD5 = T1 + 4
        win = sb("win", [P, 2, 2, PAD5], c=conv)
        wsum = sb("wsum", [P, 2, 2, T1], c=conv)
        w_ba = sb("w_ba", [P, DT, 32], c=conv)
        w_ba_hi = sb("w_ba_hi", [P, DT, 32], F32R, conv)
        w_ba_lo = sb("w_ba_lo", [P, DT, 32], F32R, conv)
        heads_row = sb("heads_row", [1, 2, 2, HEADS], c=conv)
        heads_all = sb("heads_all", [P, 2, 2, HEADS], c=conv)
        ba = sb("ba", [P, 2, 4 * HEADS], c=conv)
        sp_t = sb("sp_t", [P, 6, 2, 2 * HEADS], c=conv)
        small = sem("mix_small")
        ca_act, cv_ready, conv_step, conv_done = sem("ca_act"), sem("cv_ready"), sem("conv_step"), sem("conv_done")
        qkv_in, qkv_out, ba_sem, ba_hi_done, ba_act = (sem(x) for x in ("qkv_in", "qkv_out", "ba_sem", "ba_hi_done", "ba_act"))
        ya_done, pads, ba_exp = sem("ya_done"), sem("pads"), sem("ba_exp")

        with nc.Block() as block:
            @block.sync
            def _(sp):
                sp.dma_start(w_ba[:], w_in[:, gate0 - 32:gate0].rearrange("(k p) n -> p k n", p=P)).then_inc(small, 16)
                for k, name in enumerate(("dt_bias_fwd", "dt_bias_bwd", "a_log_fwd", "a_log_bwd")):
                    sp.dma_start(heads_row[:, k // 2, k % 2], t[name]).then_inc(small, 16)
                load_to(sp, S["qkv"].r0 + 12 + RING)

            @block.scalar
            def _(act):
                def copy_to(dst, name):
                    sec = S[name]

                    def take(i, u, U):
                        outputs_ready(act, sec, i, u, U)
                        for j in range(2):
                            ins = nc.scalar.activation(dst[:, 2 * u + j], out_bank(sec, u, j)[:, 0:T1], ACT.Copy)
                        ins.then_inc(act_took, 1)
                    return take
                act_pairs(act, S["ca_b"], copy_to(cab, "ca_b"))
                act_pairs(act, S["ca_c"], copy_to(cac, "ca_c"))
                act_pairs(act, S["ca_v"], lambda i, u, U: None)
                act.wait_ge(small, 80)
                nc.scalar.activation(w_ba_hi[:], w_ba[:], ACT.Copy).then_inc(ba_hi_done, 1)
                sec = S["qkv"]
                act.wait_ge(pads, 1)

                def silu(i, n, b, n_at):
                    act.wait_ge(conv_done, n + 1)
                    nc.scalar.activation(qkv[:, bass.ds(n * 2, 2)], wsum[:, b], ACT.Silu).then_inc(qkv_out, 1)

                def take(i, u, U):
                    b = u % 2
                    outputs_ready(act, sec, i, u, U)
                    for j in range(2):
                        ins = nc.scalar.activation(win[:, b, j, 2:2 + T1], out_bank(sec, u, j)[:, 0:T1], ACT.Copy)
                    ins.then_inc(act_took, 1)
                    silu(i, at(i, U, u), b, u)
                act_pairs(act, sec, take)
                act.wait_ge(ya_done, 1)
                nc.scalar.activation(ya_hi[:], ya[:], ACT.Copy).then_inc(ya_done, 1)
                act.wait_ge(ba_sem, 1)
                nc.scalar.activation(heads_all[:], banks[6][:, 128:160].rearrange("p (a b c) -> p a b c", a=2, b=2), ACT.Copy).then_inc(ba_act, 1)
                nc.scalar.activation(ba[:, 0], banks[6][:, 0:32], ACT.Copy)
                nc.scalar.activation(ba[:, 1], banks[6][:, 32:64], ACT.Copy).then_inc(ba_act, 1)
                act.wait_ge(ba_act, 2)
                nc.scalar.activation(beta[:], ba[:, :, 0:16].rearrange("p c (d h) -> p c d h", d=2), ACT.Sigmoid)
                nc.scalar.activation(heads_all[:, 1], heads_all[:, 1], ACT.Exp).then_inc(ba_act, 1)
                act.wait_ge(ba_exp, 1)
                nc.scalar.activation(sp_t[:, 2], sp_t[:, 1], ACT.Exp, scale=-1.0).then_inc(ba_act, 1)

            @block.vector
            def _(dve):
                nc.vector.memset(cav[:], 0.0).then_inc(cv_ready, 1)
                nc.vector.memset(win[:], 0.0).then_inc(pads, 1)
                dve_pairs(dve, S["ca_b"], lambda i, u, U: None)
                dve_pairs(dve, S["ca_c"], lambda i, u, U: None)
                dve.wait_ge(cv_ready, 1)
                sec = S["ca_v"]

                def product(i, u, U):
                    outputs_ready(dve, S["ca_v"], i, u, U)
                    taken(dve, S["ca_c"], None, 1, 0)
                    for j in range(2):
                        k = 2 * u + j
                        ins = nc.vector.tensor_tensor(cav[:, k, 1:1 + T1], out_bank(S["ca_v"], u, j)[:, 0:T1], cac[:, k], ALU.mult)
                    ins.then_inc(dve_took, 1)
                dve_pairs(dve, sec, product)
                taken(dve, sec, None, 1, 0)
                for tap in range(3):
                    for k in range(4):
                        w = col("conv_a", 4 * tap + k)
                        if tap == 0:
                            ins = nc.vector.tensor_scalar(ya[:, k], cav[:, k, 0:T1], w, None, ALU.mult)
                        else:
                            ins = nc.vector.scalar_tensor_tensor(out=ya[:, k], in0=cav[:, k, tap:tap + T1], scalar=w, in1=ya[:, k],
                                                                 op0=ALU.mult, op1=ALU.add)
                    link(dve, "dve", ins)
                nc.vector.tensor_tensor(ya[:], ya[:], cab[:], ALU.mult).then_inc(ya_done, 1)
                dve.wait_ge(ba_hi_done, 1)
                nc.vector.tensor_tensor(w_ba_lo[:], w_ba[:], w_ba_hi[:].bitcast(F32), ALU.subtract).then_inc(ba_hi_done, 1)
                sec = S["qkv"]

                def taps(i, u, U):
                    b, n = u % 2, at(i, U, u)
                    taken(dve, sec, i, u, U)
                    dve.wait_ge(qkv_out, at(i, U, u + 1))
                    for tap in range(5):
                        if tap:
                            dve.wait_ge(conv_step, n * 4 + tap)
                        for j in range(2):
                            v, row = vcol["conv_dn"]
                            w = (vec[:, v, row + 24 * tap + 2 * u + j:row + 24 * tap + 2 * u + j + 1] if i is None else
                                 vec[:, v, bass.ds(i * (2 * U) + (row + 24 * tap + 2 * u + j), 1)])
                            if tap == 0:
                                ins = nc.vector.tensor_scalar(wsum[:, b, j], win[:, b, j, 0:T1], w, None, ALU.mult)
                            else:
                                ins = nc.vector.scalar_tensor_tensor(out=wsum[:, b, j], in0=win[:, b, j, tap:tap + T1], scalar=w,
                                                                     in1=wsum[:, b, j], op0=ALU.mult, op1=ALU.add)
                        ins.then_inc(conv_done if tap == 4 else conv_step, 1)
                dve.sem_inc(qkv_out, 2)
                dve_pairs(dve, sec, taps)
                dve.wait_ge(ya_done, 2)
                nc.vector.tensor_tensor(ya_lo[:], ya[:], ya_hi[:].bitcast(F32), ALU.subtract)
                dve.wait_ge(ba_act, 3)
                al, x, neg = sp_t[:, 0], sp_t[:, 0], sp_t[:, 1]
                bias = heads_all[:, 0].rearrange("p d h -> p (d h)")[:, None, :].broadcast_to([P, 2, 2 * HEADS])
                rate = heads_all[:, 1].rearrange("p d h -> p (d h)")[:, None, :].broadcast_to([P, 2, 2 * HEADS])
                link(dve, "dve", nc.vector.tensor_tensor(x, ba[:, :, 16:32], bias, ALU.add))
                link(dve, "dve", nc.vector.tensor_scalar(neg, x, -1.0, None, ALU.mult))
                nc.vector.tensor_tensor(neg, neg, x, ALU.max).then_inc(ba_exp, 1)
                dve.wait_ge(ba_act, 4)
                e, s, s2, poly = sp_t[:, 2], sp_t[:, 3], sp_t[:, 4], sp_t[:, 5]
                link(dve, "dve", nc.vector.tensor_scalar(s, e, 2.0, None, ALU.add))
                link(dve, "dve", nc.vector.reciprocal(s, s))
                link(dve, "dve", nc.vector.tensor_tensor(s, s, e, ALU.mult))
                link(dve, "dve", nc.vector.tensor_tensor(s2, s, s, ALU.mult))
                link(dve, "dve", nc.vector.tensor_scalar(poly, s2, 2.0 / 19, 2.0 / 17, ALU.mult, ALU.add))
                for k in (15, 13, 11, 9, 7, 5, 3, 1):
                    link(dve, "dve", nc.vector.tensor_tensor(poly, poly, s2, ALU.mult))
                    link(dve, "dve", nc.vector.tensor_scalar(poly, poly, 2.0 / k, None, ALU.add))
                link(dve, "dve", nc.vector.tensor_tensor(poly, poly, s, ALU.mult))
                link(dve, "dve", nc.vector.scalar_tensor_tensor(out=poly, in0=x, scalar=0.0, in1=poly, op0=ALU.max, op1=ALU.add))
                nc.vector.scalar_tensor_tensor(out=g_log[:].rearrange("p c d h -> p c (d h)"), in0=poly, scalar=-1.0, in1=rate,
                                               op0=ALU.mult, op1=ALU.mult)

            @block.tensor
            def _(pe):
                for name in ("ca_b", "ca_c", "ca_v", "qkv"):
                    pe_pairs(pe, S[name], x_hi, x_lo, T1)
                pe.wait_ge(ba_hi_done, 2)
                for c in range(2):
                    out = banks[6][:, 32 * c:32 * c + 32]
                    for k in range(DT):
                        rows = slice(c * P, (c + 1) * P)
                        nc.tensor.matmul(out, x_hi[:, k, rows], w_ba_hi[:, k], start=k == 0, stop=False)
                        nc.tensor.matmul(out, x_lo[:, k, rows], w_ba_hi[:, k], start=False, stop=False)
                        nc.tensor.matmul(out, x_hi[:, k, rows], w_ba_lo[:, k], start=False, stop=k == DT - 1)
                mm = nc.tensor.matmul(banks[6][:, 128:160], const("ones")[0:1], heads_row[:].rearrange("p a b c -> p (a b c)"),
                                      start=True, stop=True)
                mm.then_inc(ba_sem, 1)
        conv.close()

        k_rows = sb("k_rows", [P, 2, HEADS, P], c=gdn)
        v_rows = sb("v_rows", [P, 2, HEADS, P], c=gdn)
        g_cum = sb("g_cum", [P, 2, 2, HEADS], c=gdn)
        g_end = sb("g_end", [P, 2, 2, HEADS], c=gdn)
        g_exp = sb("g_exp", [P, 2, 2, HEADS], c=gdn)
        a_t = sb("a_t", [P, 2, HEADS, P], c=gdn)
        inv = sb("inv", [P, 2, HEADS, P], c=gdn)
        inv_t = sb("inv_t", [P, 2, HEADS, P], c=gdn)
        attn_t = sb("attn_t", [P, 2, HEADS, P], c=gdn)
        prod = sb("prod", [P, 2, HEADS, P], c=gdn)
        dec_t = prod
        q_exp = sb("q_exp", [P, HEADS, P], c=gdn)
        sq = attn_t[:, 0].rearrange("p (a x) n -> p a (x n)", a=4)
        rt = prod[:].rearrange("p c (a x) n -> p (c a) (x n)", a=4).rearrange("p (a b) n -> p a b n", b=2)
        state, k_end, v_new = inv[:, 0], inv[:, 1], prod
        l2_sq, l2_sum, l2_ms, l2_y, l2_done = (sem(x) for x in ("l2_sq", "l2_sum", "l2_ms", "l2_y", "l2_done"))
        rows_ready, rows_taken, cum_ready, cum_taken = (sem(x) for x in ("rows_ready", "rows_taken", "cum_ready", "cum_taken"))
        with nc.Block() as block:
            @block.scalar
            def _(act):
                for q in range(8):
                    if q >= 2:
                        act.wait_ge(l2_sum, q - 1)
                    nc.scalar.activation(sq[:, 2 * (q % 2):2 * (q % 2) + 2], qkv[:, 2 * q:2 * q + 2], ACT.Square).then_inc(l2_sq, 1)
                    if q:
                        act.wait_ge(l2_ms, q)
                        nc.scalar.activation(rt[:, 1], rt[:, 0], ACT.Abs_reciprocal_sqrt).then_inc(l2_y, 1)
                act.wait_ge(l2_ms, 8)
                nc.scalar.activation(rt[:, 1], rt[:, 0], ACT.Abs_reciprocal_sqrt).then_inc(l2_y, 1)
                for q in range(8):
                    act.wait_ge(rows_ready, q + 1)
                    dst, c, hh = (k_rows, v_rows)[q // 4], (q // 2) % 2, 4 * (q % 2)
                    nc.scalar.activation(dst[:, c, hh:hh + 4], banks[q % 4][:].rearrange("p (h n) -> p h n", h=4), ACT.Copy).then_inc(rows_taken, 1)

            @block.tensor
            def _(pe):
                for d, name in enumerate(("upto", "from")):
                    for c in range(2):
                        mm = nc.tensor.matmul(banks[6][:, 16 * d + 8 * c:16 * d + 8 * c + 8], const(name), g_log[:, c, d], start=True, stop=True)
                        mm = nc.tensor.matmul(banks[6][:, 32 + 16 * d + 8 * c:40 + 16 * d + 8 * c], const("ones"), g_log[:, c, d], start=True, stop=True)
                mm.then_inc(cum_ready, 1)
                for q in range(8):
                    pe.wait_ge(l2_sq, q + 1)
                    if q >= 2:
                        pe.wait_ge(l2_ms, q - 1)
                    nc.tensor.matmul(banks[4 + q % 2][:].rearrange("p (a b) -> p a b", a=2), const("ones"), sq[:, 2 * (q % 2):2 * (q % 2) + 2], start=True, stop=True).then_inc(l2_sum, 1)
                pe.wait_ge(l2_done, 8)
                for q in range(8):
                    if q >= 4:
                        pe.wait_ge(rows_taken, q - 3)
                    base, c, hh = (8, 16)[q // 4], (q // 2) % 2, 4 * (q % 2)
                    for k in range(4):
                        mm = nc.tensor.transpose(banks[q % 4][:, k * P:(k + 1) * P], qkv[:, base + hh + k, c * P:(c + 1) * P], ident)
                    mm.then_inc(rows_ready, 1)

            @block.vector
            def _(dve):
                dve.wait_ge(cum_ready, 1)
                flat = lambda x: x.rearrange("p d c h -> p (d c h)")
                link(dve, "dve", nc.vector.tensor_copy(flat(g_cum[:]), banks[6][:, 0:32]))
                nc.vector.tensor_tensor(flat(g_end[:]), banks[6][:, 32:64], flat(g_cum[:]), ALU.subtract).then_inc(cum_taken, 1)
                for q in range(8):
                    dve.wait_ge(l2_sum, q + 1)
                    s = float(P) if q < 4 else 1.0
                    nc.vector.tensor_scalar(rt[:, 0], banks[4 + q % 2][:].rearrange("p (a b) -> p a b", a=2), EPS, s, ALU.add, ALU.mult).then_inc(l2_ms, 1)
                    inverse_root(dve, l2_y, q + 1, rt[:, 0], rt[:, 1], rt[:, 2], rt[:, 3])
                    nc.vector.tensor_tensor(qkv[:, 2 * q:2 * q + 2], qkv[:, 2 * q:2 * q + 2], rt[:, 3], ALU.mult).then_inc(l2_done, 1)
        with nc.Block() as block:
            @block.scalar
            def _(act):
                nc.scalar.activation(g_end[:], g_end[:], ACT.Exp)
                nc.scalar.activation(g_exp[:], g_cum[:], ACT.Exp).then_inc(cum_taken, 1)

            @block.vector
            def _(dve):
                dve.wait_ge(cum_taken, 2)
                nc.vector.tensor_scalar(g_exp[:], g_exp[:], -1.0, None, ALU.mult)


        gb_ready, gb_taken, dec_min, dec_exp, gram_ready, a_done, at_done = (
            sem(x) for x in ("gb_ready", "gb_taken", "dec_min", "dec_exp", "gram_ready", "a_done", "at_done"))
        z_ready, z_done, s_ready, s_done, ks_ready, r_done, o_ready, o_done, qe_ready, qe_done, ke_done = (
            sem(x) for x in ("z_ready", "z_done", "s_ready", "s_done", "ks_ready", "r_done", "o_ready", "o_done", "qe_ready", "qe_done", "ke_done"))
        H2 = HEADS // 2

        def heads4(bank):
            return bank[:].rearrange("p (h n) -> p h n", h=4)

        def joined(x, l, side):
            return x.rearrange("p h (n two b) -> p h n two b", two=2, b=1 << l)[:, :, :, side]

        inverses = [0, 0, 0]

        def grow_inverse(a_t, inv, inv_t, prod, nh, C, flip):
            even, odd = (0, 1) if flip == 0 else (1, 0)
            levels, half = C.bit_length() - 1, C // 2
            L0, Y0, X0 = inverses
            inverses[2] += 2 * (levels - 2)
            inverses[0] += 2 * levels
            inverses[1] += 2 * levels + 2
            level_cols = const("levels").rearrange("p (l f n) -> p l f n", l=LEVELS, f=2)

            def rows_of(side):
                halves = [slice(0, half), slice(half, C)] if half >= 32 else [slice(0, C)]
                return halves if side is None or half < 32 else [halves[side]]

            def by_head(bank, b=None, rows=slice(0, C)):
                v = bank[rows, 0:nh * half]
                return v.rearrange("p (h n b) -> p h n b", h=nh, b=b) if b else v.rearrange("p (h n) -> p h n", h=nh)
            with nc.Block() as block:
                @block.gpsimd
                def _(pool):
                    for l in range(levels):
                        for c in range(2):
                            if l:
                                pool.wait_ge(y_done, Y0 + 2 * l + c + 1)
                            nc.gpsimd.memset(prod[0:C, c], 0.0).then_inc(p_zero, 1)

                @block.tensor
                def _(pe):
                    def product(bank, c, lhs, rhs, done, rows):
                        for k in range(nh):
                            for m in rows:
                                mm = nc.tensor.matmul(bank[m, k * half:(k + 1) * half], lhs[0:C, c, k, m], rhs(c, k), start=True, stop=True)
                        mm.then_inc(done, 1)
                    for l in range(levels):
                        n, last = L0 + 2 * l, l == levels - 1
                        for c in range(2):
                            pe.wait_ge(y_done, Y0 + 2 * l + c + 1)
                            product(banks[c], c, a_t, lambda c, k: joined(inv[0:C, c, k:k + 1], l, even)[:, 0], p_ready, rows_of(odd) if last else rows_of(None))
                        for c in range(2):
                            pe.wait_ge(p_done, n + c + 1)
                            if 0 < l < levels - 1:
                                product(banks[2 + c], c, inv_t, lambda c, k: joined(prod[0:C, c, k:k + 1], l, even)[:, 0], xu_ready, rows_of(None))
                            product(banks[4 + c], c, prod, lambda c, k: joined(inv_t[0:C, c, k:k + 1], l, odd)[:, 0], yu_ready, rows_of(even) if last else rows_of(None))

                @block.vector
                def _(dve):
                    eye = ident[0:C, 0:C][:, None, :].broadcast_to([C, nh, C])
                    for c in range(2):
                        nc.vector.tensor_copy(inv[0:C, c], eye).then_inc(x_done, 1)
                        nc.vector.tensor_copy(inv_t[0:C, c], eye).then_inc(y_done, 1)
                    for l in range(levels):
                        n, b, last = L0 + 2 * l, 1 << l, l == levels - 1
                        rows_p, rows_y = (rows_of(odd)[-1], rows_of(even)[0]) if last and half >= 32 else (slice(0, C), slice(0, C))
                        for c in range(2):
                            dve.wait_ge(p_ready, n + c + 1)
                            dve.wait_ge(p_zero, n + c + 1)
                            mask = level_cols[rows_p, l, flip, 0:half].rearrange("p (n b) -> p n b", b=b)[:, None].broadcast_to([rows_p.stop - rows_p.start, nh, half // b, b])
                            nc.vector.tensor_tensor(joined(prod[rows_p, c], l, even), by_head(banks[c], b, rows_p), mask, ALU.mult).then_inc(p_done, 1)
                        for c in range(2):
                            part = joined(inv[0:C, c], l, even)
                            if l == 0:
                                dve.wait_ge(p_done, n + c + 1)
                                nc.vector.tensor_tensor(part, part, joined(prod[0:C, c], l, even), ALU.subtract).then_inc(x_done, 1)
                            elif not last:
                                dve.wait_ge(xu_ready, X0 + 2 * (l - 1) + c + 1)
                                nc.vector.tensor_tensor(part, part, by_head(banks[2 + c], b), ALU.subtract).then_inc(x_done, 1)
                            dve.wait_ge(yu_ready, n + c + 1)
                            part = joined(inv_t[rows_y, c], l, odd)
                            nc.vector.tensor_tensor(part, part, by_head(banks[4 + c], b, rows_y), ALU.subtract).then_inc(y_done, 1)

        def gb_bank(q):
            return banks[(0, 1, 6, 7)[q]]

        def gdn_direction(d):
            tri, neg = (("upto", "neg_upto"), ("from", "neg_from"))[d]
            first = d
            D4 = 4 * d
            with nc.Block() as block:
                @block.tensor
                def _(pe):
                    for q in range(4):
                        c, hh = q // 2, H2 * (q % 2)
                        for k in range(4):
                            g = g_log[:, c, d, hh + k:hh + k + 1].broadcast_to([P, P])
                            mm = nc.tensor.matmul(gb_bank(q)[:, k * P:(k + 1) * P], g, const(tri), start=True, stop=True)
                        mm.then_inc(gb_ready, 1)
                    for q in range(4):
                        c, hh = q // 2, H2 * (q % 2)
                        if q >= 2:
                            pe.wait_ge(at_done, D4 + q - 1)
                        for k in range(4):
                            kt = qkv[:, HEADS + hh + k, c * P:(c + 1) * P]
                            qt = qkv[:, hh + k, c * P:(c + 1) * P]
                            nc.tensor.matmul(banks[2 + q % 2][:, k * P:(k + 1) * P], kt, kt, start=True, stop=True)
                            mm = nc.tensor.matmul(banks[4 + q % 2][:, k * P:(k + 1) * P], kt, qt, start=True, stop=True)
                        mm.then_inc(gram_ready, 1)

                @block.vector
                def _(dve):
                    for q in range(4):
                        c, hh = q // 2, H2 * (q % 2)
                        dve.wait_ge(gb_ready, D4 + q + 1)
                        for k in range(4):
                            ins = nc.vector.scalar_tensor_tensor(
                                out=dec_t[:, c, hh + k], in0=gb_bank(q)[:, k * P:(k + 1) * P], scalar=g_cum[:, d, c, hh + k:hh + k + 1],
                                in1=const(neg), op0=ALU.subtract, op1=ALU.add)
                        ins.then_inc(gb_taken, 1)
                    for q in range(4):
                        c, hh = q // 2, H2 * (q % 2)
                        dve.wait_ge(dec_exp, D4 + q + 1)
                        dve.wait_ge(gram_ready, D4 + q + 1)
                        for k in range(4):
                            nc.vector.scalar_tensor_tensor(
                                out=a_t[:, c, hh + k], in0=banks[2 + q % 2][:, k * P:(k + 1) * P], scalar=beta[:, c, d, hh + k:hh + k + 1],
                                in1=dec_t[:, c, hh + k], op0=ALU.mult, op1=ALU.mult)
                        nc.vector.tensor_tensor(attn_t[:, c, hh:hh + 4], heads4(banks[4 + q % 2]), dec_t[:, c, hh:hh + 4], ALU.mult).then_inc(at_done, 1)

                @block.scalar
                def _(act):
                    for q in range(4):
                        c, hh = q // 2, H2 * (q % 2)
                        act.wait_ge(gb_taken, D4 + q + 1)
                        nc.scalar.activation(dec_t[:, c, hh:hh + 4], dec_t[:, c, hh:hh + 4], ACT.Exp).then_inc(dec_exp, 1)
                        if c != first:
                            act.wait_ge(gb_ready, D4 + 4)
                            if q % 2 == 1:
                                for half in range(2):
                                    nc.scalar.activation(q_exp[:, 4 * half:4 * half + 4], heads4(gb_bank(2 * c + half)), ACT.Exp).then_inc(qe_ready, 1)

                @block.gpsimd
                def _(pool):
                    pool.wait_ge(qe_ready, 2 * (d + 1))
                    nc.gpsimd.tensor_tensor(q_exp[:], q_exp[:], qkv[:, 0:HEADS, (1 - first) * P:(2 - first) * P], ALU.mult).then_inc(qe_done, 1)

            grow_inverse(a_t, inv, inv_t, prod, HEADS, P, d)
            second = 1 - first
            with nc.Block() as block:
                @block.tensor
                def _(pe):
                    def eight(bank0, lhs, rhs, ready, start=True, stop=True):
                        for k in range(HEADS):
                            mm = nc.tensor.matmul(banks[bank0 + k // 4][:, (k % 4) * P:(k % 4 + 1) * P], lhs(k), rhs(k), start=start, stop=stop)
                            if k % 4 == 3 and ready:
                                mm.then_inc(ready, 1)
                    H = 2 * d
                    eight(0, lambda k: inv_t[:, first, k], lambda k: v_rows[:, first, k], z_ready)
                    for half in range(2):
                        pe.wait_ge(z_done, 2 * H + half + 1)
                        pe.wait_ge(ke_done, H + half + 1)
                        for k in range(4 * half, 4 * half + 4):
                            mm = nc.tensor.matmul(banks[2 + half][:, (k % 4) * P:(k % 4 + 1) * P], k_end[:, k], v_new[:, first, k], start=True, stop=True)
                        mm.then_inc(s_ready, 1)
                    for half in range(2):
                        pe.wait_ge(s_done, H + half + 1)
                        for k in range(4 * half, 4 * half + 4):
                            kt = qkv[:, HEADS + k, second * P:(second + 1) * P]
                            mm = nc.tensor.matmul(banks[4 + half][:, (k % 4) * P:(k % 4 + 1) * P], kt, state[:, k], start=True, stop=True)
                        mm.then_inc(ks_ready, 1)
                    eight(6, lambda k: v_new[:, first, k], lambda k: attn_t[:, first, k], o_ready)
                    for half in range(2):
                        pe.wait_ge(r_done, H + half + 1)
                        for k in range(4 * half, 4 * half + 4):
                            mm = nc.tensor.matmul(banks[half][:, (k % 4) * P:(k % 4 + 1) * P], inv_t[:, second, k], v_new[:, second, k], start=True, stop=True)
                        mm.then_inc(z_ready, 1)
                    for half in range(2):
                        pe.wait_ge(z_done, 2 * H + 2 + half + 1)
                        for k in range(4 * half, 4 * half + 4):
                            out = banks[2 + half][:, (k % 4) * P:(k % 4 + 1) * P]
                            nc.tensor.matmul(out, state[:, k], q_exp[:, k], start=True, stop=False)
                            mm = nc.tensor.matmul(out, v_new[:, second, k], attn_t[:, second, k], start=False, stop=True)
                        mm.then_inc(o_ready, 1)

                @block.gpsimd
                def _(pool):
                    for half in range(2):
                        hs = slice(4 * half, 4 * half + 4)
                        end = g_end[:, d, first, hs][:, :, None].broadcast_to([P, 4, P])
                        nc.gpsimd.tensor_tensor(k_end[:, hs], k_rows[:, first, hs], end, ALU.mult).then_inc(ke_done, 1)

                @block.scalar
                def _(act):
                    for half in range(2):
                        act.wait_ge(s_ready, 2 * d + half + 1)
                        nc.scalar.activation(state[:, 4 * half:4 * half + 4], heads4(banks[2 + half]), ACT.Copy).then_inc(s_done, 1)

                @block.vector
                def _(dve):
                    def betas(c, half):
                        return beta[:, c, d, 4 * half:4 * half + 4][:, :, None].broadcast_to([P, 4, P])

                    def z_to_v(c, half):
                        nc.vector.tensor_tensor(v_new[:, c, 4 * half:4 * half + 4], heads4(banks[half]), betas(c, half), ALU.mult).then_inc(z_done, 1)

                    def outputs(c, half, bank):
                        o = o_sum[:, 4 * half:4 * half + 4, c * P:(c + 1) * P]
                        if d == 0:
                            nc.vector.tensor_copy(o, heads4(bank)).then_inc(o_done, 1)
                        else:
                            nc.vector.tensor_tensor(o, o, heads4(bank), ALU.add).then_inc(o_done, 1)
                    for half in range(2):
                        dve.wait_ge(z_ready, 4 * d + half + 1)
                        z_to_v(first, half)
                    for half in range(2):
                        dve.wait_ge(ks_ready, 2 * d + half + 1)
                        for k in range(4 * half, 4 * half + 4):
                            ins = nc.vector.scalar_tensor_tensor(
                                out=v_new[:, second, k], in0=banks[4 + half][:, (k % 4) * P:(k % 4 + 1) * P],
                                scalar=g_exp[:, d, second, k:k + 1], in1=v_rows[:, second, k], op0=ALU.mult, op1=ALU.add)
                        ins.then_inc(r_done, 1)
                    for half in range(2):
                        dve.wait_ge(o_ready, 4 * d + half + 1)
                        outputs(first, half, banks[6 + half])
                    for half in range(2):
                        dve.wait_ge(z_ready, 4 * d + 2 + half + 1)
                        z_to_v(second, half)
                    for half in range(2):
                        dve.wait_ge(o_ready, 4 * d + 2 + half + 1)
                        outputs(second, half, banks[2 + half])

        gdn_direction(0)
        gdn_direction(1)
        gdn.close()

        fin = ExitStack()
        osq = sb("osq", [P, 4, T1], c=fin)
        ort = sb("ort", [P, 4, 2, T1], c=fin)
        zt = sb("zt", [P, 2, 2, T1], c=fin)
        yb_hi = sb("yb_hi", [P, HEADS, T1], F32R, fin)
        yb_lo = sb("yb_lo", [P, HEADS, T1], F32R, fin)
        gate = sb("gate", [P, 2 * DT, T1], c=fin)
        merged = gate[:, 0:DT]
        tmp_b = sb("tmp_b", [P, 2, 2, T1], c=fin)
        on_sq, on_sum, on_ms, on_y, on_done = (sem(x) for x in ("on_sq", "on_sum", "on_ms", "on_y", "on_done"))
        z_act, yb_done, yb_h, m_done, m_h, m_l, tb_done = (sem(x) for x in ("z_act", "yb_done", "yb_h", "m_done", "m_h", "m_l", "tb_done"))
        with nc.Block() as block:
            @block.sync
            def _(sp):
                load_to(sp, S["w_out"].r0 + 4 + RING)

            @block.scalar
            def _(act):
                for q in range(4):
                    if q >= 2:
                        act.wait_ge(on_sum, q - 1)
                    nc.scalar.activation(osq[:, 2 * (q % 2):2 * (q % 2) + 2], o_sum[:, 2 * q:2 * q + 2], ACT.Square).then_inc(on_sq, 1)
                    if q:
                        act.wait_ge(on_ms, q)
                        nc.scalar.activation(ort[:, 1], ort[:, 0], ACT.Abs_reciprocal_sqrt).then_inc(on_y, 1)
                act.wait_ge(on_ms, 4)
                nc.scalar.activation(ort[:, 1], ort[:, 0], ACT.Abs_reciprocal_sqrt).then_inc(on_y, 1)

                def silu_z(i, u, U):
                    outputs_ready(act, S["z"], i, u, U)
                    if u >= 2:
                        act.wait_ge(yb_done, u - 1)
                    for j in range(2):
                        ins = nc.scalar.activation(zt[:, u % 2, j], out_bank(S["z"], u, j)[:, 0:T1], ACT.Silu)
                    ins.then_inc(act_took, 1)
                act_pairs(act, S["z"], silu_z)
                act.wait_ge(yb_done, 4)
                nc.scalar.activation(yb_hi[:], o_sum[:], ACT.Copy).then_inc(yb_h, 1)

                def sigmoid(i, u, U):
                    outputs_ready(act, S["gates"], i, u, U)
                    for j in range(2):
                        ins = nc.scalar.activation(gate[:, 2 * u + j] if i is None else gate[:, bass.ds(i * (2 * U) + (2 * u + j), 1)],
                                                   out_bank(S["gates"], u, j)[:, 0:T1] if i is None else out_bank(S["gates"], u, j)[:, None, 0:T1], ACT.Sigmoid)
                    ins.then_inc(act_took, 1)
                act_pairs(act, S["gates"], sigmoid)
                act_pairs(act, S["a_out"], lambda i, u, U: None)

                def high(i, u, U):
                    act.wait_ge(m_done, u + 1)
                    nc.scalar.activation(x_hi[:, 2 * u:2 * u + 2, 0:T1], merged[:, 2 * u:2 * u + 2], ACT.Copy).then_inc(m_h, 1)
                act_pairs(act, S["b_out"], high)
                act_pairs(act, S["w_out"], lambda i, u, U: None)

            @block.tensor
            def _(pe):
                for q in range(4):
                    pe.wait_ge(on_sq, q + 1)
                    if q >= 2:
                        pe.wait_ge(on_ms, q - 1)
                    nc.tensor.matmul(banks[4 + q % 2][:].rearrange("p (a b) -> p a b", a=2), const("ones"), osq[:, 2 * (q % 2):2 * (q % 2) + 2], start=True, stop=True).then_inc(on_sum, 1)

                def after(i, u, U):
                    r_at = S["z"].r0 + 2 * u + 1
                    pe_ada(pe, r_at, 32 + u, u, 64 + 2 * u)
                pe_pairs(pe, S["z"], x_hi, x_lo, T1, after)
                pe_pairs(pe, S["gates"], x_hi, x_lo, T1)
                pe_pairs(pe, S["a_out"], ya_hi, ya_lo, T1)
                pe.wait_ge(yb_h, 2)
                pe_pairs(pe, S["b_out"], yb_hi, yb_lo, T1)
                pe.wait_ge(m_l, 4)
                pe_pairs(pe, S["w_out"], x_hi, x_lo, T1)

            @block.vector
            def _(dve):
                for q in range(4):
                    dve.wait_ge(on_sum, q + 1)
                    nc.vector.tensor_scalar(ort[:, 0], banks[4 + q % 2][:].rearrange("p (a b) -> p a b", a=2), 1.0 / P, EPS, ALU.mult, ALU.add).then_inc(on_ms, 1)
                    inverse_root(dve, on_y, q + 1, ort[:, 0], ort[:, 1], ort[:, 2], ort[:, 3])
                    link(dve, "dve", nc.vector.scalar_tensor_tensor(out=o_sum[:, 2 * q:2 * q + 2], in0=o_sum[:, 2 * q:2 * q + 2],
                                                                    scalar=col("dn_norm", 0), in1=ort[:, 3], op0=ALU.mult, op1=ALU.mult))

                def between(i, u, U):
                    r_at = S["z"].r0 + 2 * u + 1
                    dve_ada(dve, 32 + u, u, r_at, LANDED * (r_at // RING + 1), 7 * (32 + u))

                def times_z(i, u, U):
                    taken(dve, S["z"], None, u, 0)
                    nc.vector.tensor_tensor(o_sum[:, 2 * u:2 * u + 2], o_sum[:, 2 * u:2 * u + 2], zt[:, u % 2], ALU.mult).then_inc(yb_done, 1)
                dve_pairs(dve, S["z"], times_z, between)
                dve_mod(dve, 64, 72, 36)
                dve.wait_ge(yb_h, 1)
                nc.vector.tensor_tensor(yb_lo[:], o_sum[:], yb_hi[:].bitcast(F32), ALU.subtract).then_inc(yb_h, 1)
                dve_pairs(dve, S["gates"], lambda i, u, U: None)

                def gated_a(i, u, U):
                    outputs_ready(dve, S["a_out"], i, u, U)
                    taken(dve, S["gates"], None, 7, 0)
                    for j in range(2):
                        k = 2 * u + j
                        ins = nc.vector.tensor_tensor(gate[:, k], gate[:, k], out_bank(S["a_out"], u, j)[:, 0:T1], ALU.mult)
                    ins.then_inc(dve_took, 1)
                dve_pairs(dve, S["a_out"], gated_a)

                def gated_b(i, u, U):
                    outputs_ready(dve, S["b_out"], i, u, U)
                    for j in range(2):
                        k = 2 * u + j
                        ins = nc.vector.tensor_tensor(tmp_b[:, u % 2, j], gate[:, DT + k], out_bank(S["b_out"], u, j)[:, 0:T1], ALU.mult)
                    ins.then_inc(dve_took, 1)
                    taken(dve, S["b_out"], None, u, 0)
                    nc.vector.tensor_tensor(merged[:, 2 * u:2 * u + 2], merged[:, 2 * u:2 * u + 2], tmp_b[:, u % 2], ALU.add).then_inc(m_done, 1)
                    dve.wait_ge(m_h, u + 1)
                    nc.vector.tensor_tensor(x_lo[:, 2 * u:2 * u + 2, 0:T1], merged[:, 2 * u:2 * u + 2], x_hi[:, 2 * u:2 * u + 2, 0:T1].bitcast(F32), ALU.subtract).then_inc(m_l, 1)
                dve_pairs(dve, S["b_out"], gated_b)

                def residual(i, u, U):
                    outputs_ready(dve, S["w_out"], i, u, U)
                    for j in range(2):
                        k = 2 * u + j
                        ins = nc.vector.scalar_tensor_tensor(out=h1[:, k], in0=out_bank(S["w_out"], u, j)[:, 0:T1], scalar=mod[:, 40 + k:41 + k],
                                                             in1=h1[:, k], op0=ALU.mult, op1=ALU.add)
                    ins.then_inc(dve_took, 1)
                dve_pairs(dve, S["w_out"], residual)
        fin.close()
        mix.close()
        if until <= 2:
            dump(nc, t, h, sem)
            return
        a_cols, b_cols, prep = modulation("norm_ffn2", 6, 7)
        norm(h1, T1, a_cols, b_cols, prep)
        swiglu(S["up2"], S["down2"], 8, False)
        norm(h1, T1, lambda k: col("norm_final", k), None, lambda dve: None, dst=h1)
        if until <= 3:
            dump(nc, t, h, sem)
            return

        def g_row(layer, k):
            return lambda ft: col("norm_g_2", (layer * 4 + k) * DT + ft)

        no_prep = lambda dve: None
        end_of_stage()
        norm(h, T2, g_row(0, 0), None, no_prep)
        rw = ExitStack()
        Y = sb("Y", [P, SHIFTED + 4, T2 + 1], c=rw)
        ys = Y[:, :, 1:T2 + 1]
        r_t, k_t, v_t = ys[:, 0:4], ys[:, 4:8], ys[:, 8:12]
        pool_u = ys[:, 14:18]
        log_w = sb("log_w", [P, RW, T2], c=rw)
        log_g = sb("log_g", [P, RW, T2], c=rw)
        nb_t = sb("nb_t", [P, RW, T2], c=rw)
        gate_t = sb("gate_t", [P, RW, T2], c=rw)
        kk_t = sb("kk_t", [P, RW, T2], c=rw)
        e1 = sb("e1", [P, RW, T2], c=rw)
        v_rw = sb("v_rw", [P, 3, 512], c=rw)
        g_fin = sb("g_fin", [P, RW, 5], c=rw)
        state_bd = sb("state_bd", [P, RW, P], c=rw)
        o_rows = sb("o_rows", [P, 3, 512], c=rw)
        pre = ExitStack()
        w_up = sb("w_up", [P, 512], c=pre)
        g_up = sb("g_up", [P, 512], c=pre)
        low = sb("low", [P, 2, T2], c=pre)
        shift = sb("shift", [P, 2, 2, T2], c=pre)
        reset = sb("reset", [P, RW, T2], c=pre)
        e2 = sb("e2", [P, RW, T2], c=pre)
        e3 = sb("e3", [P, RW, T2], c=pre)
        names = ("ev_small", "y_zero", "sh_sub", "sh_done", "lo_act", "lo_mm", "lo_out", "a_mm", "a_out", "g_mm", "g_out",
                 "kk_sq", "kk_sum", "kk_ms", "kk_y", "kk_ok", "bon", "bon_mm", "vr_mm", "vr_out", "ex", "ex_done", "gf_in", "reset_ok")
        q = {n: sem(n) for n in names}
        with nc.Block() as block:
            @block.sync
            def _(sp):
                sp.dma_start(w_up[0:64], t["ev_w_up_2"][0]).then_inc(q["ev_small"], 16)
                sp.dma_start(w_up[64:P], t["ev_a_up_2"][0]).then_inc(q["ev_small"], 16)
                sp.dma_start(g_up[:], t["ev_g_up_2"][0]).then_inc(q["ev_small"], 16)
                load_to(sp, S["ev_u"].r0 + 2 + RING)

            @block.scalar
            def _(act):
                def copy(sec, first):
                    def take(i, u, U):
                        outputs_ready(act, sec, i, u, U)
                        for j in range(2):
                            k = first + 2 * u + j
                            ins = nc.scalar.activation(ys[:, k], out_bank(sec, u, j)[:, 0:T2], ACT.Copy)
                        ins.then_inc(act_took, 1)
                    return take
                act.wait_ge(q["y_zero"], 1)
                act_pairs(act, S["ev_s"], copy(S["ev_s"], 0))
                act_pairs(act, S["ev_u"], copy(S["ev_u"], SHIFTED))
                act.wait_ge(q["sh_done"], 7)
                nc.scalar.activation(low[0:64, 0], ys[0:64, 12], ACT.Tanh)
                nc.scalar.activation(low[64:P, 0], ys[64:P, 12], ACT.Copy)
                nc.scalar.activation(low[:, 1], ys[:, 13], ACT.Sigmoid).then_inc(q["lo_act"], 1)
                for k in range(RW):
                    act.wait_ge(q["lo_mm"], k + 1)
                    nc.scalar.activation(log_w[:, k], banks[k][:, 0:T2], ACT.Sigmoid, bias=col("ev_w0_2", k)).then_inc(q["lo_out"], 1)
                for k in range(RW):
                    act.wait_ge(q["a_mm"], k + 1)
                    nc.scalar.activation(nb_t[:, k], banks[4 + k][:, 0:T2], ACT.Sigmoid, bias=col("ev_a0_2", k)).then_inc(q["a_out"], 1)
                for k in range(RW):
                    act.wait_ge(q["g_mm"], k + 1)
                    nc.scalar.activation(gate_t[:, k], banks[k][:, 0:T2], ACT.Copy).then_inc(q["g_out"], 1)
                act.wait_ge(q["kk_ok"], 1)
                nc.scalar.activation(e1[:], kk_t[:], ACT.Square).then_inc(q["kk_sq"], 1)
                act.wait_ge(q["kk_ms"], 1)
                nc.scalar.activation(e2[:], e1[:], ACT.Abs_reciprocal_sqrt).then_inc(q["kk_y"], 1)
                for c in range(3):
                    act.wait_ge(q["vr_mm"], c + 1)
                    C = min(P, T2 - c * P)
                    nc.scalar.activation(v_rw[0:C, c], banks[c][0:C], ACT.Copy).then_inc(q["vr_out"], 1)
                act.wait_ge(q["ex"], 1)
                nc.scalar.activation(g_fin[:], g_fin[:], ACT.Exp)
                nc.scalar.activation(e1[:], log_g[:], ACT.Exp).then_inc(q["ex_done"], 1)
                nc.scalar.activation(e2[:], log_w[:], ACT.Exp).then_inc(q["ex_done"], 1)
                nc.scalar.activation(e3[:], log_g[:], ACT.Exp, scale=-1.0).then_inc(q["ex_done"], 1)

            @block.vector
            def _(dve):
                nc.vector.memset(Y[:, :, 0:1], 0.0).then_inc(q["y_zero"], 1)
                link(dve, "dve", nc.vector.memset(reset[:], 1.0))
                nc.vector.memset(reset[:, :, 0:T2:64], 0.0).then_inc(q["reset_ok"], 1)
                dve.wait_ge(q["y_zero"], 1)

                def shifted(i, u, U):
                    b = u % 2
                    taken(dve, S["ev_s"], None, u, 0)
                    link(dve, "dve", nc.vector.tensor_tensor(shift[:, b], Y[:, 2 * u:2 * u + 2, 0:T2], ys[:, 2 * u:2 * u + 2], ALU.subtract))
                    for j in range(2):
                        k = 2 * u + j
                        ins = nc.vector.scalar_tensor_tensor(out=ys[:, k], in0=shift[:, b, j], scalar=col("ev_mu_2", k), in1=ys[:, k],
                                                             op0=ALU.mult, op1=ALU.add)
                    ins.then_inc(q["sh_done"], 1)
                dve_pairs(dve, S["ev_s"], shifted)
                dve_pairs(dve, S["ev_u"], lambda i, u, U: None)
                dve.wait_ge(q["sh_done"], 7)
                for k in range(RW):
                    ins = nc.vector.tensor_scalar(kk_t[:, k], k_t[:, k], col("ev_k_k_2", k), None, ALU.mult)
                ins.then_inc(q["kk_ok"], 1)
                dve.wait_ge(q["lo_out"], 4)
                link(dve, "dve", nc.vector.tensor_scalar(log_w[:], log_w[:], -float(np.exp(-0.5)), None, ALU.mult))
                dve.wait_ge(q["reset_ok"], 1)
                flat = lambda x: x[:].rearrange("p a b -> p (a b)")
                link(dve, "dve", nc.vector.tensor_tensor_scan(flat(log_g), flat(reset), flat(log_w), 0.0, ALU.mult, ALU.add))
                nc.vector.tensor_copy(g_fin[:, :, 0:4], log_g[:, :, 63:T2:64])
                nc.vector.tensor_copy(g_fin[:, :, 4:5], log_g[:, :, T2 - 1:T2])
                link(dve, "dve", nc.vector.tensor_tensor(log_w[:], log_g[:], log_w[:], ALU.subtract))
                dve.wait_ge(q["a_out"], 4)
                for k in range(RW):
                    ins = nc.vector.tensor_scalar(e3[:, k], nb_t[:, k], -1.0, col("ev_k_a_2", k), ALU.add, ALU.mult)
                link(dve, "dve", ins)
                link(dve, "dve", nc.vector.scalar_tensor_tensor(out=k_t, in0=e3[:], scalar=1.0, in1=k_t, op0=ALU.add, op1=ALU.mult))
                for k in range(RW):
                    dve.wait_ge(q["kk_sum"], k + 1)
                    ins = nc.vector.tensor_scalar(e1[:, k], banks[4 + k][:, 0:T2], 1e-24, None, ALU.max)
                ins.then_inc(q["kk_ms"], 1)
                inverse_root(dve, q["kk_y"], 1, e1[:], e2[:], e3[:], e3[:])
                link(dve, "dve", nc.vector.tensor_tensor(kk_t[:], kk_t[:], e3[:], ALU.mult))
                link(dve, "dve", nc.vector.scalar_tensor_tensor(out=nb_t[:], in0=kk_t[:], scalar=-1.0, in1=nb_t[:], op0=ALU.mult, op1=ALU.mult))
                for k in range(RW):
                    ins = nc.vector.scalar_tensor_tensor(out=e3[:, k], in0=r_t[:, k], scalar=col("ev_r_k_2", k), in1=k_t[:, k], op0=ALU.mult, op1=ALU.mult)
                ins.then_inc(q["bon"], 1)
                dve.wait_ge(q["vr_out"], 3)
                dve.wait_ge(q["vr_mm"], 3)
                for k in range(RW):
                    dve.wait_ge(q["bon_mm"], k + 1)
                    ins = nc.vector.tensor_tensor(v_t[:, k], v_t[:, k], banks[4 + k][:, 0:T2], ALU.mult)
                ins.then_inc(q["ex"], 1)
                for n, (x, e) in enumerate(((r_t, e1), (kk_t[:], e2), (k_t, e3), (nb_t[:], e3))):
                    dve.wait_ge(q["ex_done"], min(n + 1, 3))
                    nc.vector.tensor_tensor(x, x, e[:], ALU.mult)

            @block.tensor
            def _(pe):
                pe_pairs(pe, S["ev_s"], x_hi, x_lo, T2)
                pe_pairs(pe, S["ev_u"], x_hi, x_lo, T2)
                pe.wait_ge(q["ev_small"], 48)
                pe.wait_ge(q["lo_act"], 1)
                taken(pe, S["ev_u"], None, 1, 0)
                for k in range(RW):
                    nc.tensor.matmul(banks[k][:, 0:T2], w_up[0:64, k * P:(k + 1) * P], low[0:64, 0], start=True, stop=True).then_inc(q["lo_mm"], 1)
                for k in range(RW):
                    nc.tensor.matmul(banks[4 + k][:, 0:T2], w_up[64:P, k * P:(k + 1) * P], low[64:P, 0], start=True, stop=True).then_inc(q["a_mm"], 1)
                for k in range(RW):
                    pe.wait_ge(q["lo_out"], k + 1)
                    nc.tensor.matmul(banks[k][:, 0:T2], g_up[:, k * P:(k + 1) * P], low[:, 1], start=True, stop=True).then_inc(q["g_mm"], 1)
                pe.wait_ge(q["kk_sq"], 1)
                for k in range(RW):
                    pe.wait_ge(q["a_out"], k + 1)
                    nc.tensor.matmul(banks[4 + k][:, 0:T2], const("halves"), e1[:, k], start=True, stop=True).then_inc(q["kk_sum"], 1)
                pe.wait_ge(q["g_out"], 4)
                for c in range(3):
                    C = min(P, T2 - c * P)
                    for k in range(RW):
                        mm = nc.tensor.transpose(banks[c][0:C, k * P:(k + 1) * P], v_t[:, k, c * P:c * P + C], ident)
                    mm.then_inc(q["vr_mm"], 1)
                pe.wait_ge(q["bon"], 1)
                for k in range(RW):
                    nc.tensor.matmul(banks[4 + k][:, 0:T2], const("halves"), e3[:, k], start=True, stop=True).then_inc(q["bon_mm"], 1)
        pre.close()

        ch = ExitStack()
        rb_at, ak_t, rb_t, rk_t, rinv, rinv_t, rprod = (sb(n, [P, 2, RW, P], c=ch) for n in ("rb_at", "ak_t", "rb_t", "rk_t", "rinv", "rinv_t", "rprod"))
        hats = sb("hats", [P, 2, RW, 64], c=ch)
        rows_kb = sb("rows_kb", [P, 2, 512], c=ch)
        rhs_r = sb("rhs_r", [P, 512], c=ch)
        w_r = sb("w_r", [P, 512], c=ch)
        w_end = sb("w_end", [P, RW, 1], c=ch)
        names = ("hat", "gr", "gr_out", "gr_act", "hat2", "kb_mm", "kb_out", "rr", "rr_out", "ww", "ww_out", "oo", "oo_out", "st", "st_out", "bd0")
        m = {n: sem("c_" + n) for n in names}

        def rwkv_chunk(c):
            C = min(P, T2 - c * P)
            cols, c0, c1 = slice(c * P, c * P + C), slice(c * P, c * P + 64), slice(c * P + 64, c * P + P)
            two = C == P
            f_a, f_b = (g_fin[:, :, min(2 * c + x, 4):min(2 * c + x, 4) + 1] for x in range(2))
            pairs = [(nb_t, kk_t), (k_t, kk_t), (nb_t, r_t), (k_t, r_t)]
            with nc.Block() as block:
                @block.gpsimd
                def _(pool):
                    if two:
                        nc.gpsimd.tensor_tensor(hats[:, 0], nb_t[:, :, c0], f_a.broadcast_to([P, RW, 64]), ALU.mult)
                        nc.gpsimd.tensor_tensor(hats[:, 1], k_t[:, :, c0], f_a.broadcast_to([P, RW, 64]), ALU.mult).then_inc(m["hat"], 1)

                @block.tensor
                def _(pe):
                    if two:
                        pe.wait_ge(m["hat"], c + 1)
                    for x, (left, right) in enumerate(pairs):
                        for par in range(2):
                            ps = slice(64 * par, 64 * par + 64)
                            for k in range(RW):
                                out = banks[2 * x + par][0:C, k * P:k * P + C]
                                mm = nc.tensor.matmul(out, left[ps, k, cols], right[ps, k, cols], start=True, stop=True)
                                if two:
                                    mm = nc.tensor.matmul(banks[2 * x + par][0:64, k * P + 64:k * P + P], hats[ps, x % 2, k], right[ps, k, c1], start=True, stop=True)
                            mm.then_inc(m["gr"], 1)

                @block.scalar
                def _(act):
                    for par in range(2):
                        act.wait_ge(m["gr"], 8 * c + par + 1)
                        nc.scalar.activation(rb_at[0:C, par, :, 0:C], heads4(banks[par])[0:C, :, 0:C], ACT.Copy, scale=-1.0).then_inc(m["gr_act"], 1)

                @block.vector
                def _(dve):
                    for x, (dst, mask) in enumerate(((ak_t, "before"), (rb_t, "upto"), (rk_t, "upto"))):
                        for par in range(2):
                            dve.wait_ge(m["gr"], 8 * c + 2 * x + 2 + par + 1)
                            nc.vector.tensor_tensor(dst[0:C, par, :, 0:C], heads4(banks[2 * x + 2 + par])[0:C, :, 0:C],
                                                    const(mask)[0:C, 0:C][:, None, :].broadcast_to([C, RW, C]), ALU.mult).then_inc(m["gr_out"], 1)
            grow_inverse(rb_at[:, :, :, 0:C], rinv[:, :, :, 0:C], rinv_t[:, :, :, 0:C], rprod[:, :, :, 0:C], RW, C, 0)
            has_state, makes_state = c > 0, c < 2
            with nc.Block() as block:
                @block.vector
                def _(dve):
                    if two:
                        fb = f_b.broadcast_to([P, RW, 64])
                        fa = f_a.broadcast_to([P, RW, 64])
                        if has_state:
                            for x in (kk_t[:], r_t):
                                nc.vector.tensor_tensor(x[:, :, c1], x[:, :, c1], fa, ALU.mult)
                        nc.vector.tensor_tensor(w_end[:], f_a, f_b, ALU.mult)
                        for n, x in enumerate((nb_t[:], k_t)):
                            nc.vector.tensor_tensor(x[:, :, c0], hats[:, n], fb, ALU.mult)
                            ins = nc.vector.tensor_tensor(x[:, :, c1], x[:, :, c1], fb, ALU.mult)
                        ins.then_inc(m["hat2"], 1)
                        if c == 0:
                            nc.vector.memset(state_bd[:], 0.0).then_inc(m["bd0"], 1)
                            dve.wait_ge(m["bd0"], 1)
                    dve.wait_ge(m["rr"], c + 1)
                    nc.vector.tensor_copy(rhs_r[0:C], banks[0][0:C]).then_inc(m["rr_out"], 1)
                    dve.wait_ge(m["ww"], c + 1)
                    nc.vector.tensor_copy(w_r[0:C], banks[1][0:C]).then_inc(m["ww_out"], 1)
                    if makes_state:
                        dve.wait_ge(m["st"], c + 1)
                        dve.wait_ge(m["oo"], c + 1)
                        for par in range(2):
                            ps = slice(64 * par, 64 * par + 64)
                            s = state_bd[ps, :, ps]
                            new = heads4(banks[3])[ps, :, ps]
                            if c:
                                link(dve, "dve", nc.vector.tensor_tensor(s, s, w_end[ps].broadcast_to([64, RW, 64]), ALU.mult))
                                link(dve, "dve", nc.vector.tensor_tensor(s, s, new, ALU.add))
                            else:
                                link(dve, "dve", nc.vector.tensor_copy(s, new))

                @block.scalar
                def _(act):
                    if makes_state:
                        for n in range(2):
                            act.wait_ge(m["kb_mm"], 2 * c + n + 1)
                            nc.scalar.activation(rows_kb[:, n], banks[4 + n][:], ACT.Copy).then_inc(m["kb_out"], 1)
                    act.wait_ge(m["oo"], c + 1)
                    nc.scalar.activation(o_rows[0:C, c], banks[2][0:C], ACT.Copy).then_inc(m["oo_out"], 1)

                @block.tensor
                def _(pe):
                    if has_state and two:
                        pe.wait_ge(m["hat2"], c + 1)
                    def head(x, k, par):
                        return x[0:C, par, k, 0:C]
                    def of(x, k, par):
                        return x[0:C, k * P + 64 * par:k * P + 64 * par + 64]
                    for k in range(RW):
                        if has_state:
                            nc.tensor.matmul(banks[0][0:C, k * P:(k + 1) * P], kk_t[:, k, cols], state_bd[:, k], start=True, stop=False, skip_group_check=True)
                        for par in range(2):
                            mm = nc.tensor.matmul(of(banks[0], k, par), head(ak_t, k, par), of(v_rw[:, c], k, par), start=not has_state, stop=True, skip_group_check=True)
                    mm.then_inc(m["rr"], 1)
                    if makes_state:
                        pe.wait_ge(m["hat2"], c + 1)
                        for n, x in enumerate((nb_t, k_t)):
                            for k in range(RW):
                                mm = nc.tensor.transpose(banks[4 + n][:, k * P:(k + 1) * P], x[:, k, cols], ident)
                            mm.then_inc(m["kb_mm"], 1)
                    pe.wait_ge(m["rr_out"], c + 1)
                    for k in range(RW):
                        for par in range(2):
                            mm = nc.tensor.matmul(of(banks[1], k, par), head(rinv_t, k, par), of(rhs_r, k, par), start=True, stop=True)
                    mm.then_inc(m["ww"], 1)
                    pe.wait_ge(m["ww_out"], c + 1)
                    if makes_state:
                        pe.wait_ge(m["kb_out"], 2 * c + 2)
                        for k in range(RW):
                            ks = slice(k * P, (k + 1) * P)
                            nc.tensor.matmul(banks[3][:, ks], rows_kb[:, 0, ks], w_r[:, ks], start=True, stop=False)
                            mm = nc.tensor.matmul(banks[3][:, ks], rows_kb[:, 1, ks], v_rw[:, c, ks], start=False, stop=True)
                        mm.then_inc(m["st"], 1)
                    for k in range(RW):
                        if has_state:
                            nc.tensor.matmul(banks[2][0:C, k * P:(k + 1) * P], r_t[:, k, cols], state_bd[:, k], start=True, stop=False, skip_group_check=True)
                        for par in range(2):
                            nc.tensor.matmul(of(banks[2], k, par), head(rb_t, k, par), of(w_r, k, par), start=not has_state, stop=False, skip_group_check=True)
                            mm = nc.tensor.matmul(of(banks[2], k, par), head(rk_t, k, par), of(v_rw[:, c], k, par), start=False, stop=True, skip_group_check=True)
                    mm.then_inc(m["oo"], 1)

        for c in range(3):
            rwkv_chunk(c)
        ch.close()

        po = ExitStack()
        dev = sb("dev", [P, 3, 512], c=po)
        dev2 = sb("dev2", [P, 3, 512], c=po)
        gn = sb("gn", [P, 6, 3, HEADS], c=po)
        sum_a, sum_b, diff = (sb(n, [P, 4, T2], c=po) for n in ("sum_a", "sum_b", "diff"))
        head16 = sb("head16", [P, 4, 16], c=po)
        pool_w = sb("pool_w", [P, 4, P], c=po)
        cat = sb("cat", [P, DT, T2], c=po)
        names = ("pw", "d2", "ms", "y", "nrm", "tr", "o_done", "pl", "pl_mm", "cat_h", "cat_l", "z_done")
        g = {n: sem("g_" + n) for n in names}
        heads8 = lambda x: x.rearrange("p (h n) -> p h n", h=HEADS)
        with nc.Block() as block:
            @block.sync
            def _(sp):
                sp.dma_start(pool_w[:], t["ev_pool_w_2"][0].rearrange("g c d -> c g d")).then_inc(g["pw"], 16)

            @block.scalar
            def _(act):
                for c in range(3):
                    C = min(P, T2 - c * P)
                    act.wait_ge(g["d2"], c + 1)
                    nc.scalar.activation(dev2[0:C, c], dev[0:C, c], ACT.Square).then_inc(g["y"], 1)
                for c in range(3):
                    C = min(P, T2 - c * P)
                    act.wait_ge(g["ms"], c + 1)
                    nc.scalar.activation(gn[0:C, 3, c], gn[0:C, 2, c], ACT.Abs_reciprocal_sqrt).then_inc(g["y"], 1)
                for k in range(4):
                    act.wait_ge(g["pl_mm"], k + 1)
                    nc.scalar.activation(cat[:, 4 + k], banks[4 + k][:, 0:T2], ACT.Identity, scale=col("ev_pool_scale_2", k)).then_inc(g["z_done"], 1)
                act.wait_ge(g["z_done"], 4)
                nc.scalar.activation(x_hi[:, 4:8], cat[:, 4:8], ACT.Copy).then_inc(g["cat_h"], 1)
                act.wait_ge(g["o_done"], 1)
                nc.scalar.activation(x_hi[:, 0:4], cat[:, 0:4], ACT.Copy).then_inc(g["cat_h"], 1)

            @block.vector
            def _(dve):
                for c in range(3):
                    C = min(P, T2 - c * P)
                    link(dve, "dve", nc.vector.reduce_sum(gn[0:C, 0, c], heads8(o_rows[0:C, c]), AX.X))
                    link(dve, "dve", nc.vector.tensor_scalar(gn[0:C, 0, c], gn[0:C, 0, c], 1.0 / 64, None, ALU.mult))
                    mean = gn[0:C, 0, c][:, :, None].broadcast_to([C, HEADS, 64])
                    nc.vector.tensor_tensor(heads8(dev[0:C, c]), heads8(o_rows[0:C, c]), mean, ALU.subtract).then_inc(g["d2"], 1)
                u = pool_u
                nc.vector.tensor_copy(sum_a[:, :, 0:1], u[:, :, 0:1])
                link(dve, "dve", nc.vector.tensor_tensor(sum_a[:, :, 1:T2], u[:, :, 1:T2], u[:, :, 0:T2 - 1], ALU.add))
                nc.vector.tensor_copy(sum_b[:, 1:4, 0:2], sum_a[:, 1:4, 0:2])
                link(dve, "dve", nc.vector.tensor_tensor(sum_b[:, 1:4, 2:T2], sum_a[:, 1:4, 2:T2], sum_a[:, 1:4, 0:T2 - 2], ALU.add))
                nc.vector.tensor_copy(sum_a[:, 2:4, 0:4], sum_b[:, 2:4, 0:4])
                link(dve, "dve", nc.vector.tensor_tensor(sum_a[:, 2:4, 4:T2], sum_b[:, 2:4, 4:T2], sum_b[:, 2:4, 0:T2 - 4], ALU.add))
                nc.vector.tensor_copy(sum_b[:, 3:4, 0:8], sum_a[:, 3:4, 0:8])
                link(dve, "dve", nc.vector.tensor_tensor(sum_b[:, 3:4, 8:T2], sum_a[:, 3:4, 8:T2], sum_a[:, 3:4, 0:T2 - 8], ALU.add))
                counts = const("counts").rearrange("p (g n) -> p g n", g=4)
                sums = (sum_a, sum_b, sum_a, sum_b)
                for k, win in enumerate(WINDOWS):
                    nc.vector.tensor_tensor(head16[:, k], sums[k][:, k, 0:16], counts[:, k], ALU.mult)
                    ins = nc.vector.scalar_tensor_tensor(out=diff[:, k], in0=sums[k][:, k], scalar=1.0 / win, in1=u[:, k], op0=ALU.mult, op1=ALU.subtract)
                link(dve, "dve", ins)
                nc.vector.tensor_tensor(diff[:, :, 0:16], head16[:], u[:, :, 0:16], ALU.subtract).then_inc(g["pl"], 1)
                for c in range(3):
                    C = min(P, T2 - c * P)
                    dve.wait_ge(g["y"], c + 1)
                    link(dve, "dve", nc.vector.reduce_sum(gn[0:C, 1, c], heads8(dev2[0:C, c]), AX.X))
                    nc.vector.tensor_scalar(gn[0:C, 2, c], gn[0:C, 1, c], 1.0 / 64, GN_EPS, ALU.mult, ALU.add).then_inc(g["ms"], 1)
                for c in range(3):
                    C = min(P, T2 - c * P)
                    inverse_root(dve, g["y"], 3 + c + 1, gn[0:C, 2, c], gn[0:C, 3, c], gn[0:C, 4, c], gn[0:C, 5, c])
                    rstd = gn[0:C, 5, c][:, :, None].broadcast_to([C, HEADS, 64])
                    nc.vector.tensor_tensor(heads8(dev[0:C, c]), heads8(dev[0:C, c]), rstd, ALU.mult).then_inc(g["nrm"], 1)
                dve.wait_ge(g["tr"], 1)
                for k in range(RW):
                    ins = nc.vector.tensor_scalar(cat[:, k], banks[k][:, 0:T2], col("ev_ln_w_2", k), col("ev_ln_b_2", k), ALU.mult, ALU.add)
                link(dve, "dve", ins)
                link(dve, "dve", nc.vector.tensor_tensor(cat[:, 0:4], cat[:, 0:4], v_t, ALU.add))
                nc.vector.tensor_tensor(cat[:, 0:4], cat[:, 0:4], gate_t[:], ALU.mult).then_inc(g["o_done"], 1)
                for n, half in enumerate((slice(4, 8), slice(0, 4))):
                    dve.wait_ge(g["cat_h"], n + 1)
                    if n:
                        dve.wait_ge(g["o_done"], 1)
                    nc.vector.tensor_tensor(x_lo[:, half], cat[:, half], x_hi[:, half].bitcast(F32), ALU.subtract).then_inc(g["cat_l"], 1)

            @block.tensor
            def _(pe):
                pe.wait_ge(g["pw"], 16)
                pe.wait_ge(g["pl"], 1)
                for k in range(4):
                    nc.tensor.matmul(banks[4 + k][:, 0:T2], pool_w[:, k], diff[:, k], start=True, stop=True).then_inc(g["pl_mm"], 1)
                for c in range(3):
                    C = min(P, T2 - c * P)
                    pe.wait_ge(g["nrm"], c + 1)
                    for k in range(RW):
                        mm = nc.tensor.transpose(banks[k][:, c * P:c * P + C], dev[0:C, c, k * P:(k + 1) * P], ident[0:C, 0:C])
                mm.then_inc(g["tr"], 1)
        po.close()
        rw.close()

        def plain(sec, xh, xl, dst):
            with nc.Block() as block:
                @block.sync
                def _(sp):
                    load_to(sp, sec.r0 + sec.pairs * sec.g + RING)

                @block.scalar
                def _(act):
                    def take(i, u, U):
                        outputs_ready(act, sec, i, u, U)
                        for j in range(2):
                            d = dst[:, 2 * u + j] if i is None else dst[:, bass.ds(i * (2 * U) + (2 * u + j), 1)]
                            b = out_bank(sec, u, j)
                            ins = nc.scalar.activation(d, b[:, 0:T2] if i is None else b[:, None, 0:T2], ACT.Copy)
                        ins.then_inc(act_took, 1)
                    act_pairs(act, sec, take)

                @block.vector
                def _(dve):
                    dve_pairs(dve, sec, lambda i, u, U: None)

                @block.tensor
                def _(pe):
                    pe_pairs(pe, sec, xh, xl, T2)

        def mixer_out(sec, layer, tag):
            with ExitStack() as c:
                out = sb(f"mixed{tag}", [P, DT, T2], c=c)
                plain(sec, x_hi, x_lo, out)
                norm(out[:], T2, g_row(layer, 1), None, no_prep, add_to=h)

        def mlp(up, down, layer):
            norm(h, T2, g_row(layer, 2), None, no_prep)
            whole = ExitStack()
            out = sb(f"down_out{layer}", [P, DT, T2], c=whole)
            with ExitStack() as c:
                hid_hi = sb(f"mh_hi{layer}", [P, FF2T, T2], F32R, c)
                hid_lo = sb(f"mh_lo{layer}", [P, FF2T, T2], F32R, c)
                relu = sb(f"relu{layer}", [P, 2, 2, T2], c=c)
                sq = sb(f"relu2{layer}", [P, 2, 2, T2], c=c)
                s_sq, s_hi, s_lo = (sem(f"{x}{layer}") for x in ("mlp_sq", "mlp_hi", "mlp_lo"))
                with nc.Block() as block:
                    @block.sync
                    def _(sp):
                        load_to(sp, up.r0 + up.pairs + RING)

                    @block.scalar
                    def _(act):
                        def take(i, u, U):
                            b, n = u % 2, at(i, U, u)
                            outputs_ready(act, up, i, u, U)
                            for j in range(2):
                                ins = nc.scalar.activation(relu[:, b, j], out_bank(up, u, j)[:, 0:T2], ACT.Relu)
                            ins.then_inc(act_took, 1)
                            taken(act, up, i, u, U)
                            act.wait_ge(s_lo, n + 1)
                            nc.scalar.activation(sq[:, b], relu[:, b], ACT.Square).then_inc(s_sq, 1)
                            act.wait_ge(s_sq, n + 1)
                            nc.scalar.activation(hid_hi[:, bass.ds(n * 2, 2)], sq[:, b], ACT.Copy).then_inc(s_hi, 1)
                        act_pairs(act, up, take)

                    @block.vector
                    def _(dve):
                        dve.sem_inc(s_lo, 2)

                        def low_part(i, u, U):
                            b, n = u % 2, at(i, U, u)
                            dve.wait_ge(s_hi, n + 1)
                            nc.vector.tensor_tensor(hid_lo[:, bass.ds(n * 2, 2)], sq[:, b], hid_hi[:, bass.ds(n * 2, 2)].bitcast(F32), ALU.subtract).then_inc(s_lo, 1)
                        dve_pairs(dve, up, low_part)

                    @block.tensor
                    def _(pe):
                        pe_pairs(pe, up, x_hi, x_lo, T2)
                plain(down, hid_hi, hid_lo, out)
            norm(out[:], T2, g_row(layer, 3), None, no_prep, add_to=h)
            whole.close()

        mixer_out(S["ev_out"], 0, "0")
        if until <= 4:
            dump(nc, t, h, sem)
            return
        mlp(S["mlp1_0"], S["mlp2_0"], 0)
        if until <= 5:
            dump(nc, t, h, sem)
            return

        end_of_stage()
        LAM_INIT = float(0.8 - 0.6 * np.exp(-0.3))
        norm(h, T2, g_row(1, 0), None, no_prep)
        at_ = ExitStack()
        yq = sb("yq", [P, 3 * HEADS, T2], c=at_)
        plain(S["od_in"], x_hi, x_lo, yq)
        turning = sb("turning", [P, P + 2 * T2], c=at_)
        rotate, cos_t, sin_t = turning[:, 0:P], turning[:, P:P + T2], turning[:, P + T2:P + 2 * T2]
        o_at = sb("o_at", [P, HEADS, T2], c=at_)
        v_at = sb("v_at", [P, 3, HEADS, P], c=at_)
        rot_a = sb("rot_a", [P, 2, T2], c=at_)
        lam_row = sb("lam_row", [1, 4, 64], c=at_)
        lam_p = sb("lam_p", [1, 2, 64], c=at_)
        lam_s = sb("lam_s", [1, 4], c=at_)
        lam = sb("lam", [P, 1], c=at_)
        names = ("turn", "lam", "lam_x", "lam_e", "lam_mm", "rot", "rot_a", "rot_d", "vr", "vr_out")
        a = {n: sem("a_" + n) for n in names}
        with nc.Block() as block:
            @block.sync
            def _(sp):
                sp.dma_start(lam_row[:], t["od_lambda_2"]).then_inc(a["lam"], 16)
                sp.dma_start(turning[:], t["turning"]).then_inc(a["turn"], 16)

            @block.tensor
            def _(pe):
                pe.wait_ge(a["turn"], 16)
                for k in range(2 * HEADS):
                    if k >= 4:
                        pe.wait_ge(a["rot_d"], k - 3)
                    nc.tensor.matmul(banks[k % 4][:, 0:T2], rotate, yq[:, k], start=True, stop=True).then_inc(a["rot"], 1)
                for n in range(6):
                    c, half = n // 2, n % 2
                    C = min(P, T2 - c * P)
                    if n >= 2:
                        pe.wait_ge(a["vr_out"], n - 1)
                    for k in range(4):
                        mm = nc.tensor.transpose(banks[4 + n % 2][0:C, k * P:(k + 1) * P], yq[:, 16 + 4 * half + k, c * P:c * P + C], ident)
                    mm.then_inc(a["vr"], 1)
                pe.wait_ge(a["lam_x"], 2)
                nc.tensor.matmul(banks[6][:, 0:1], const("ones")[0:1], lam_s[0:1, 3:4], start=True, stop=True).then_inc(a["lam_mm"], 1)

            @block.vector
            def _(dve):
                dve.wait_ge(a["lam"], 16)
                link(dve, "dve", nc.vector.tensor_tensor(lam_p[:], lam_row[:, 0:4:2], lam_row[:, 1:4:2], ALU.mult))
                nc.vector.reduce_sum(lam_s[:, 0:2], lam_p[:], AX.X).then_inc(a["lam_x"], 1)
                dve.wait_ge(a["lam_e"], 1)
                link(dve, "dve", nc.vector.tensor_tensor(lam_s[:, 2:3], lam_s[:, 1:2], lam_s[:, 0:1], ALU.subtract))
                nc.vector.tensor_scalar(lam_s[:, 3:4], lam_s[:, 2:3], -LAM_INIT, None, ALU.add).then_inc(a["lam_x"], 1)
                for k in range(2 * HEADS):
                    dve.wait_ge(a["rot"], k + 1)
                    link(dve, "dve", nc.vector.tensor_tensor(rot_a[:, k % 2], banks[k % 4][:, 0:T2], sin_t, ALU.mult))
                    dve.wait_ge(a["rot_a"], k + 1)
                    nc.vector.tensor_tensor(yq[:, k], yq[:, k], rot_a[:, k % 2], ALU.add).then_inc(a["rot_d"], 1)
                dve.wait_ge(a["lam_mm"], 1)
                nc.vector.tensor_copy(lam[:], banks[6][:, 0:1])

            @block.gpsimd
            def _(pool):
                for k in range(2 * HEADS):
                    pool.wait_ge(a["rot"], k + 1)
                    nc.gpsimd.tensor_tensor(yq[:, k], yq[:, k], cos_t, ALU.mult).then_inc(a["rot_a"], 1)

            @block.scalar
            def _(act):
                act.wait_ge(a["lam_x"], 1)
                nc.scalar.activation(lam_s[:, 0:2], lam_s[:, 0:2], ACT.Exp).then_inc(a["lam_e"], 1)
                for n in range(6):
                    c, half = n // 2, n % 2
                    C = min(P, T2 - c * P)
                    act.wait_ge(a["vr"], n + 1)
                    nc.scalar.activation(v_at[0:C, c, 4 * half:4 * half + 4], heads4(banks[4 + n % 2])[0:C], ACT.Copy).then_inc(a["vr_out"], 1)

        prob = sb("prob", [P, 2, 2, T2], c=at_)
        attn = sb("attn", [P, 2, T2], c=at_)
        attn_tr = sb("attn_tr", [P, 2, 3, P], c=at_)
        smx = sb("smx", [P, 2, 10], c=at_)
        units = [(head, qt) for head in range(HEADS) for qt in range(3)]
        names = ("sc", "mask", "max", "nmax", "exp", "p0", "attn", "tr", "tr_out", "pv", "o_out")
        u_ = {n: sem("u_" + n) for n in names}
        with nc.Block() as block:
            def dims(n):
                head, qt = units[n]
                C = min(P, T2 - qt * P)
                return head, qt, C, qt * P + C

            @block.tensor
            def _(pe):
                for n in range(len(units) + 2):
                    if n < len(units):
                        head, qt, C, K = dims(n)
                        if n >= 2:
                            pe.wait_ge(u_["exp"], n - 1)
                        for comp in range(2):
                            ps = slice(64 * comp, 64 * comp + 64)
                            mm = nc.tensor.matmul(banks[2 * (n % 2) + comp][0:C, 0:K], yq[ps, head, qt * P:qt * P + C], yq[ps, HEADS + head, 0:K], start=True, stop=True)
                        mm.then_inc(u_["sc"], 1)
                    if 1 <= n <= len(units):
                        head, qt, C, K = dims(n - 1)
                        pe.wait_ge(u_["attn"], n)
                        if n >= 3:
                            pe.wait_ge(u_["tr_out"], n - 2)
                        for kt in range(qt + 1):
                            R = min(P, T2 - kt * P)
                            mm = nc.tensor.transpose(banks[4 + (n - 1) % 2][0:R, kt * P:kt * P + C], attn[0:C, (n - 1) % 2, kt * P:kt * P + R], ident[0:C, 0:C])
                        mm.then_inc(u_["tr"], 1)
                    if n >= 2:
                        head, qt, C, K = dims(n - 2)
                        pe.wait_ge(u_["tr_out"], n - 1)
                        if qt == 0 and head >= 2:
                            pe.wait_ge(u_["o_out"], head - 1)
                        for kt in range(qt + 1):
                            R = min(P, T2 - kt * P)
                            mm = nc.tensor.matmul(banks[6 + head % 2][:, qt * P:qt * P + C], v_at[0:R, kt, head], attn_tr[0:R, (n - 2) % 2, kt, 0:C], start=kt == 0, stop=kt == qt)
                        mm.then_inc(u_["pv"], 1)

            @block.vector
            def _(dve):
                scale = 64 ** -0.5

                def outputs(n):
                    if n >= 0 and units[n][1] == 2:
                        head = units[n][0]
                        dve.wait_ge(u_["pv"], n + 1)
                        nc.vector.tensor_copy(o_at[:, head], banks[6 + head % 2][:, 0:T2]).then_inc(u_["o_out"], 1)

                def combine(n):
                    head, qt, C, K = dims(n)
                    b = n % 2
                    m_ = smx[0:C, b]
                    dve.wait_ge(u_["exp"], n + 1)
                    link(dve, "dve", nc.vector.reciprocal(m_[:, 6:8], m_[:, 4:6]))
                    link(dve, "dve", nc.vector.tensor_tensor(m_[:, 8:9], m_[:, 7:8], lam[0:C], ALU.mult))
                    if n >= 2:
                        dve.wait_ge(u_["tr"], n - 1)
                    link(dve, "dve", nc.vector.tensor_scalar(attn[0:C, b, 0:K], prob[0:C, b, 0, 0:K], m_[:, 6:7], None, ALU.mult))
                    nc.vector.scalar_tensor_tensor(out=attn[0:C, b, 0:K], in0=prob[0:C, b, 1, 0:K], scalar=m_[:, 8:9], in1=attn[0:C, b, 0:K],
                                                   op0=ALU.mult, op1=ALU.add).then_inc(u_["attn"], 1)
                for n in range(len(units)):
                    head, qt, C, K = dims(n)
                    b = n % 2
                    dve.wait_ge(u_["sc"], n + 1)
                    for comp in range(2):
                        bank = banks[2 * b + comp]
                        diag = bank[0:C, qt * P:qt * P + C]
                        ins = nc.vector.tensor_tensor(diag, diag, const("neg_from")[0:C, 0:C], ALU.add)
                    link(dve, "dve", ins)
                    for comp in range(2):
                        ins = nc.vector.reduce_max(smx[0:C, b, comp:comp + 1], banks[2 * b + comp][0:C, 0:K], AX.X)
                    link(dve, "dve", ins)
                    nc.vector.tensor_scalar(smx[0:C, b, 2:4], smx[0:C, b, 0:2], -scale, None, ALU.mult).then_inc(u_["nmax"], 1)
                    if n:
                        combine(n - 1)
                    outputs(n - 3)
                combine(len(units) - 1)
                for n in range(len(units) - 3, len(units)):
                    outputs(n)

            @block.scalar
            def _(act):
                def tr_copy(n):
                    head, qt, C, K = dims(n)
                    act.wait_ge(u_["tr"], n + 1)
                    if n >= 2:
                        act.wait_ge(u_["pv"], n - 1)
                    for kt in range(qt + 1):
                        R = min(P, T2 - kt * P)
                        ins = nc.scalar.activation(attn_tr[0:R, n % 2, kt, 0:C], banks[4 + n % 2][0:R, kt * P:kt * P + C], ACT.Copy)
                    ins.then_inc(u_["tr_out"], 1)
                for n in range(len(units)):
                    head, qt, C, K = dims(n)
                    b = n % 2
                    act.wait_ge(u_["nmax"], n + 1)
                    if n >= 2:
                        act.wait_ge(u_["attn"], n - 1)
                    for comp in range(2):
                        ins = nc.scalar.activation(prob[0:C, b, comp, 0:K], banks[2 * b + comp][0:C, 0:K], ACT.Exp, bias=smx[0:C, b, 2 + comp:3 + comp],
                                                   scale=64 ** -0.5, accum_out=smx[0:C, b, 4 + comp:5 + comp])
                    ins.then_inc(u_["exp"], 1)
                    if n:
                        tr_copy(n - 1)
                tr_copy(len(units) - 1)

        asq = sb("asq", [P, 2, T2], c=at_)
        art = sb("art", [P, 2, 4, T2], c=at_)
        names = ("sq", "sum", "ms", "y", "mid", "hi")
        b_ = {n: sem("b_" + n) for n in names}
        sub_w = sb("sub_w", [P, 1], c=at_)
        with nc.Block() as block:
            @block.scalar
            def _(act):
                def high(k):
                    act.wait_ge(b_["mid"], k + 1)
                    nc.scalar.activation(x_hi[:, k], o_at[:, k], ACT.Copy).then_inc(b_["hi"], 1)
                for k in range(HEADS):
                    if k >= 2:
                        act.wait_ge(b_["sum"], k - 1)
                    nc.scalar.activation(asq[:, k % 2], o_at[:, k], ACT.Square).then_inc(b_["sq"], 1)
                    act.wait_ge(b_["ms"], k + 1)
                    nc.scalar.activation(art[:, k % 2, 1], art[:, k % 2, 0], ACT.Abs_reciprocal_sqrt).then_inc(b_["y"], 1)
                    if k:
                        high(k - 1)
                high(HEADS - 1)

            @block.tensor
            def _(pe):
                for k in range(HEADS):
                    pe.wait_ge(b_["sq"], k + 1)
                    if k >= 2:
                        pe.wait_ge(b_["ms"], k - 1)
                    nc.tensor.matmul(banks[4 + k % 2][:, 0:T2], const("ones"), asq[:, k % 2], start=True, stop=True).then_inc(b_["sum"], 1)

            @block.vector
            def _(dve):
                link(dve, "dve", nc.vector.tensor_scalar(sub_w[:], col("od_subln_w_2", 0), 1.0 - LAM_INIT, None, ALU.mult))
                for k in range(HEADS):
                    s_ = art[:, k % 2]
                    dve.wait_ge(b_["sum"], k + 1)
                    nc.vector.tensor_scalar(s_[:, 0], banks[4 + k % 2][:, 0:T2], 1.0 / P, 1e-5, ALU.mult, ALU.add).then_inc(b_["ms"], 1)
                    inverse_root(dve, b_["y"], k + 1, s_[:, 0], s_[:, 1], s_[:, 2], s_[:, 3])
                    nc.vector.scalar_tensor_tensor(out=o_at[:, k], in0=o_at[:, k], scalar=sub_w[:], in1=s_[:, 3], op0=ALU.mult, op1=ALU.mult).then_inc(b_["mid"], 1)
                for k in range(HEADS):
                    dve.wait_ge(b_["hi"], k + 1)
                    nc.vector.tensor_tensor(x_lo[:, k], o_at[:, k], x_hi[:, k].bitcast(F32), ALU.subtract)
        at_.close()
        mixer_out(S["od_out"], 1, "1")
        if until <= 6:
            dump(nc, t, h, sem)
            return
        mlp(S["mlp1_1"], S["mlp2_1"], 1)
        if until <= 7:
            dump(nc, t, h, sem)
            return

        out_rows = sb("out_rows", [P, 2, D])
        f_tr, f_out, stored = sem("f_tr"), sem("f_out"), sem("stored")
        with nc.Block() as block:
            @block.tensor
            def _(pe):
                for n in range(4):
                    c, half = n // 2, n % 2
                    for k in range(4):
                        mm = nc.tensor.transpose(banks[n][:, k * P:(k + 1) * P], h[:, 4 * half + k, META + c * P:META + (c + 1) * P], ident)
                    mm.then_inc(f_tr, 1)

            @block.vector
            def _(dve):
                for n in range(4):
                    dve.wait_ge(f_tr, n + 1)
                    nc.vector.tensor_copy(out_rows[:, n // 2, 512 * (n % 2):512 * (n % 2) + 512], banks[n][:]).then_inc(f_out, 1)

            @block.sync
            def _(sp):
                rows = t["out"][0].rearrange("(c p) d -> p c d", p=P)
                for n in range(4):
                    cols = slice(512 * (n % 2), 512 * (n % 2) + 512)
                    sp.wait_ge(f_out, n + 1)
                    sp.dma_start(rows[:, n // 2, cols], out_rows[:, n // 2, cols]).then_inc(stored, 16)
                sp.wait_ge(stored, 64)


IN_NAMES = (
    "x", "c", "w_ada", "b_ada", "norm_ffn1", "w_ffn1_up", "w_ffn1_down", "norm_mix", "w_in", "conv_a",
    "conv_dn", "a_log_fwd", "dt_bias_fwd", "a_log_bwd", "dt_bias_bwd", "dn_norm", "w_a_out",
    "w_b_out", "w_out", "norm_ffn2", "w_ffn2_up", "w_ffn2_down", "norm_final", "meta_2",
    "norm_g_2", "mlp_w1_2", "mlp_w2_2", "ev_w_in_2", "ev_mu_2", "ev_w0_2", "ev_w_up_2", "ev_a0_2",
    "ev_a_up_2", "ev_g_up_2", "ev_k_k_2", "ev_k_a_2", "ev_r_k_2", "ev_ln_w_2", "ev_ln_b_2",
    "ev_pool_w_2", "ev_pool_scale_2", "ev_w_out_2", "od_w_in_2", "od_lambda_2", "od_subln_w_2",
    "od_w_out_2",
)


def kernel(**inputs):
    import concourse.bacc as bacc
    from concourse.bass_utils import run_bass_kernel_spmd

    nc = bacc.Bacc("TRN2", target_bir_lowering=False, num_devices=1)
    const_np, place, turning = constants()
    arrays = {name: np.ascontiguousarray(inputs[name]) for name in IN_NAMES}
    arrays["const"], arrays["turning"] = const_np, turning
    t = {name: nc.dram_tensor("in_" + name, a.shape, mybir.dt.from_np(a.dtype), kind="ExternalInput").ap()
         for name, a in arrays.items()}
    t["out"] = nc.dram_tensor("out_0", (1, T1, D), F32, kind="ExternalOutput").ap()
    build(nc, t, const_np, place)
    result = run_bass_kernel_spmd(nc, [{"in_" + name: a for name, a in arrays.items()}], core_ids=[0])
    return result.results[0]["out_0"]
```

```python
from contextlib import ExitStack

import numpy as np

import concourse.bass as bass
from concourse import mybir

F32 = mybir.dt.float32
F32R = mybir.dt.float32r
ALU = mybir.AluOpType
ACT = mybir.ActivationFunctionType
AX = mybir.AxisListType

P = 128
D = 1024
DT = D // P
T1 = 256
META = 16
T2 = T1 + META
FF1 = 2816
FF1T = FF1 // P
FF2 = 4096
FF2T = FF2 // P
HEADS = 8
SLAB_K = 8
SLAB_N = 256
RING = 4
LANDED = 32
EPS = 1e-6
LEVELS = 7
QK = 1024
CA = 512
WINDOWS = (2, 4, 8, 16)
SHIFTED = 14
RW = 4
GN_EPS = 64 * 1e-5


def at(i, step, base):
    return base if i is None else i * step + base


def each_pair(eng, pairs, unroll, body, peeled=0):
    laps = (pairs - 1 - peeled) // unroll
    if laps < 2:
        laps = 0
    for u in range(peeled):
        body(None, u, u == pairs - 1)
    if laps:
        with eng.Fori(0, laps, 1) as i:
            for u in range(peeled, peeled + unroll):
                body(i, u, False)
    for u in range(peeled + laps * unroll, pairs):
        body(None, u, u == pairs - 1)


class Section:

    def __init__(self, name, pairs, kts, src, rs=1, taker="dve"):
        self.name, self.pairs, self.kts, self.src, self.rs = name, pairs, kts, src, rs
        self.g = len(kts)
        self.taker, self.r0, self.s0, self.o0, self.t0, self.other = taker, 0, 0, 0, 0, None


class Plan:

    def __init__(self):
        self.sections = []
        self.raw = []
        self.s = self.o = 0
        self.taken = {"act": 0, "dve": 0}

    def add(self, sec, between=()):
        sec.r0, sec.s0, sec.o0 = len(self.raw), self.s, self.o
        sec.t0 = self.taken[sec.taker]
        if self.sections and self.sections[-1].taker != sec.taker:
            sec.other = self.taken[self.sections[-1].taker]
        self.taken[sec.taker] += sec.pairs
        between = list(between)
        for n in range(sec.pairs):
            for g in range(sec.g):
                self.raw.append((sec, n, g))
                if between and sec.rs == 2:
                    self.raw.append(between.pop(0))
        for b in between:
            self.raw.append(b)
        self.s += sec.pairs * sec.g
        self.o += sec.pairs
        self.sections.append(sec)
        return sec


def levels_mask():
    out = np.zeros((LEVELS, 2, P, P // 2), np.float32)
    for l in range(LEVELS):
        b = 1 << l
        row = np.arange(P)[:, None]
        for flip in range(2):
            c = np.arange(P).reshape(-1, 2, b)[:, flip].reshape(1, -1)
            out[l, flip] = (row // (2 * b) == c // (2 * b)) & ((row // b) % 2 == 1 - flip)
    return out


def rotation():
    r = np.zeros((P, P), np.float32)
    for d in range(P):
        r[d + 32 if d % 64 < 32 else d - 32, d] = -1.0 if d % 64 < 32 else 1.0
    return r


def rope():
    inv = np.float32(10000.0) ** (-np.arange(0, 64, 2, dtype=np.float32) / np.float32(64))
    ang = np.arange(T2, dtype=np.float32)[None, :] * inv.astype(np.float32)[np.arange(P) % 32][:, None]
    return np.cos(ang), np.sin(ang)


def constants():
    j, i = np.arange(P)[:, None], np.arange(P)[None, :]
    parts = {
        "ident": np.eye(P),
        "ones": np.ones((P, P)),
        "halves": j // 64 == i // 64,
        "before": j < i,
        "upto": j <= i,
        "from": j >= i,
        "neg_upto": np.where(j <= i, 0.0, -1e30),
        "neg_from": np.where(j >= i, 0.0, -1e30),
        "counts": np.tile((1.0 / np.minimum(np.arange(16)[None] + 1, np.array(WINDOWS)[:, None])).reshape(1, -1), (P, 1)),
        "levels": levels_mask().transpose(2, 0, 1, 3).reshape(P, -1),
    }
    place, cols, at0 = {}, [], 0
    for name, a in parts.items():
        a = np.asarray(a, np.float32)
        place[name] = (at0, at0 + a.shape[1])
        at0 += a.shape[1]
        cols.append(a)
    turning = np.concatenate([rotation(), *rope()], 1).astype(np.float32)
    return np.concatenate(cols, 1), place, turning


VECTORS = [
    [("b_ada", 72), ("c", 8), ("norm_ffn1", 8), ("norm_mix", 8), ("norm_ffn2", 8),
     ("norm_final", 8), ("conv_a", 12), ("dn_norm", 1)],
    [("conv_dn", 120)],
    [("norm_g_2", 64), ("ev_mu_2", 14), ("ev_w0_2", 4), ("ev_a0_2", 4), ("ev_k_k_2", 4),
     ("ev_k_a_2", 4), ("ev_r_k_2", 4), ("ev_ln_w_2", 4), ("ev_ln_b_2", 4), ("ev_pool_scale_2", 4),
     ("od_subln_w_2", 1)],
]


def build(nc, t, const_np, place):
    with ExitStack() as ctx:
        def sb(name, shape, dt=F32, c=ctx):
            return c.enter_context(nc.sbuf_tensor(name, shape, dt))

        stage_sems = []

        def sem(name):
            s = nc.alloc_semaphore(name=name)
            stage_sems.append(s)
            return s

        def end_of_stage():
            with nc.Block() as block:
                @block.sync
                def _(sp):
                    nums = sorted(s.num for s in stage_sems)
                    first = nums[0]
                    for a, b in zip(nums, nums[1:] + [None]):
                        if b != a + 1:
                            sp.sem_clear(range(first, a + 1))
                            first = b
            for s in stage_sems:
                nc.release_semaphore(s)
            stage_sems.clear()

        raw = sb("raw", [P, RING, SLAB_K, SLAB_N])
        w_hi = sb("w_hi", [P, 2, SLAB_K, SLAB_N], F32R)
        w_lo = sb("w_lo", [P, 2, SLAB_K, SLAB_N], F32R)
        h = sb("h", [P, DT, T2])
        x_hi = sb("x_hi", [P, DT, T2], F32R)
        x_lo = sb("x_lo", [P, DT, T2], F32R)
        cst = sb("cst", [P, const_np.shape[1]])
        vec = sb("vec", [P, 3, P])
        mod = sb("mod", [P, 72])
        scale_col = sb("scale_col", [P, DT])
        gain_col = sb("gain_col", [P, DT])
        stat = sb("stat", [P, 4, T2])
        c_act = sb("c_act", [P, DT])
        banks = [ctx.enter_context(nc.psum_tensor(f"bank{i}", [P, 512], F32)) for i in range(8)]

        def const(name, rows=P):
            a, b = place[name]
            return cst[0:rows, a:b]

        ident = const("ident")
        vcol = {}
        for v, group in enumerate(VECTORS):
            row = 0
            for name, rows in group:
                vcol[name] = (v, row)
                row += rows

        def col(name, i, n=1):
            v, row = vcol[name]
            return vec[:, v, row + i:row + i + n]

        raw_full = [sem(f"raw_full{i}") for i in range(RING)]
        raw_used = sem("raw_used")
        hi_done = sem("hi_done")
        slab_done = sem("slab_done")
        act_took = sem("act_took")
        dve_took = sem("dve_took")
        took = {"act": act_took, "dve": dve_took}
        ada_step = sem("ada_step")
        ada_sum = sem("ada_sum")
        step = {e: sem(f"{e}_step") for e in ("dve", "act", "pool")}
        steps = {"dve": 0, "act": 0, "pool": 0}

        def link(eng, who, ins):
            steps[who] += 1
            ins.then_inc(step[who], 1)
            eng.wait_ge(step[who], steps[who])

        def mark(who, ins):
            steps[who] += 1
            ins.then_inc(step[who], 1)
            return steps[who]

        def w_cols(w, kts):
            v = w.rearrange("(k p) n -> p k n", p=P)
            first = [sum(kts[:g]) for g in range(len(kts))]

            def halves(n, g):
                a, b = first[g], first[g] + kts[g]
                mid = (a + b) // 2
                return [(v[:, x:y, bass.ds(n * SLAB_N, SLAB_N)], slice(x - a, y - a), slice(0, SLAB_N))
                        for x, y in ((a, mid), (mid, b))]
            return halves

        def w_halves(w, n0=0):
            v = w.rearrange("(k p) (h n) -> p k h n", p=P, h=2)
            return lambda n, g: [(v[:, :, j, bass.ds((n + n0) * P, P)], slice(0, SLAB_K), slice(j * P, (j + 1) * P))
                                 for j in range(2)]

        ada_src = w_cols(t["w_ada"][0], [8])
        ada_sec = Section("ada", 36, [8], ada_src)
        plan = Plan()
        UPFRONT, BESIDE_UP = 8, 14
        BESIDE_GDN = (36 - UPFRONT - BESIDE_UP) // 2
        ada_order = [(ada_sec, m, 0) for m in range(36)]
        plan.raw += ada_order[:UPFRONT]
        K8 = [8]
        w_in = t["w_in"][0]

        def sub(a, b, kts=K8, w=w_in):
            return w_cols(w[:, a:b], kts)

        S = {}
        qkv0, z0 = 3 * CA, 3 * CA + 3 * QK
        gate0 = z0 + QK + 32
        beside_gdn = ada_order[UPFRONT + BESIDE_UP:]
        S["up1a"] = plan.add(Section("up1a", BESIDE_UP, K8, w_halves(t["w_ffn1_up"][0]), rs=2), ada_order[UPFRONT:UPFRONT + BESIDE_UP])
        S["up1b"] = plan.add(Section("up1b", FF1T - BESIDE_UP, K8, w_halves(t["w_ffn1_up"][0], BESIDE_UP)))
        S["down1"] = plan.add(Section("down1", 4, [8, 8, 6], w_cols(t["w_ffn1_down"][0], [8, 8, 6])))
        S["ca_b"] = plan.add(Section("ca_b", 2, K8, sub(0, CA), taker="act"))
        S["ca_c"] = plan.add(Section("ca_c", 2, K8, sub(CA, 2 * CA), taker="act"))
        S["ca_v"] = plan.add(Section("ca_v", 2, K8, sub(2 * CA, 3 * CA)))
        S["qkv"] = plan.add(Section("qkv", 12, K8, sub(qkv0, z0), taker="act"))
        gate_parts = ((0, 1), (1, 3), (4, 4))
        for n, (g0, pairs) in enumerate(gate_parts):
            S[f"gates{n}"] = plan.add(Section(f"gates{n}", pairs, K8, sub(gate0 + g0 * SLAB_N, gate0 + (g0 + pairs) * SLAB_N), taker="act"),
                                      () if n else beside_gdn)
        S["z"] = plan.add(Section("z", 4, K8, sub(z0, z0 + QK), taker="act"))
        S["a_out"] = plan.add(Section("a_out", 4, [4], w_cols(t["w_a_out"][0], [4])))
        S["b_out"] = plan.add(Section("b_out", 4, K8, w_cols(t["w_b_out"][0], K8)))
        S["w_out"] = plan.add(Section("w_out", 4, K8, w_cols(t["w_out"][0], K8)))
        S["up2"] = plan.add(Section("up2", 22, K8, w_halves(t["w_ffn2_up"][0])))
        S["down2"] = plan.add(Section("down2", 4, [8, 8, 6], w_cols(t["w_ffn2_down"][0], [8, 8, 6])))
        ev_in = t["ev_w_in_2"][0]
        S["ev_s"] = plan.add(Section("ev_s", 7, K8, sub(0, SHIFTED * P, w=ev_in), taker="act"))
        S["ev_u"] = plan.add(Section("ev_u", 2, K8, sub(SHIFTED * P, (SHIFTED + 4) * P, w=ev_in), taker="act"))
        S["ev_out"] = plan.add(Section("ev_out", 4, K8, w_cols(t["ev_w_out_2"][0], K8), taker="act"))
        S["mlp1_0"] = plan.add(Section("mlp1_0", 16, K8, w_cols(t["mlp_w1_2"][0], K8), taker="act"))
        S["mlp2_0"] = plan.add(Section("mlp2_0", 4, [8] * 4, w_cols(t["mlp_w2_2"][0], [8] * 4), taker="act"))
        S["od_in"] = plan.add(Section("od_in", 12, K8, w_cols(t["od_w_in_2"][0], K8), taker="act"))
        S["od_out"] = plan.add(Section("od_out", 4, K8, w_cols(t["od_w_out_2"][0], K8), taker="act"))
        S["mlp1_1"] = plan.add(Section("mlp1_1", 16, K8, w_cols(t["mlp_w1_2"][1], K8), taker="act"))
        S["mlp2_1"] = plan.add(Section("mlp2_1", 4, [8] * 4, w_cols(t["mlp_w2_2"][1], [8] * 4), taker="act"))
        order = plan.sections
        issued = [0]

        def load(sp, r, sec, n, g):
            for src, ks, ns in sec.src(n, g):
                sp.dma_start(raw[:, r % RING, ks, ns], src).then_inc(raw_full[r % RING], 16)

        def load_to(sp, end):
            end = min(end, len(plan.raw))
            r = issued[0]
            while r < end:
                def rate(lap):
                    out = []
                    for u in range(RING):
                        a, b = plan.raw[r + lap * RING + u], plan.raw[r + (lap + 1) * RING + u]
                        if a[0] is not b[0] or a[2] != b[2]:
                            return None
                        out.append(b[1] - a[1])
                    return out
                laps, first = 1, rate(0) if r + 2 * RING <= end else None
                if first:
                    while r + (laps + 1) * RING <= end and rate(laps - 1) == first:
                        laps += 1
                if first and laps >= 2:
                    with sp.Fori(0, laps, 1) as i:
                        for u in range(RING):
                            sec, n, g = plan.raw[r + u]
                            sp.wait_ge(raw_used, i * RING + (r + u + 1))
                            load(sp, r + u, sec, i * first[u] + n, g)
                    r += laps * RING
                else:
                    sec, n, g = plan.raw[r]
                    sp.wait_ge(raw_used, r + 1)
                    load(sp, r, sec, n, g)
                    r += 1
            issued[0] = max(end, issued[0])

        def numbers(sec, i, U, u, g):
            k = u * sec.g + g
            r, s = sec.r0 + k * sec.rs, sec.s0 + k
            return (at(i, U * sec.g * sec.rs, r), r, at(i, U * sec.g, s), s,
                    at(i, LANDED * U * sec.g * sec.rs // RING, LANDED * (r // RING + 1)))

        def following(sec, i, U, u, g, last):
            if g + 1 < sec.g:
                return sec, g + 1, numbers(sec, i, U, u, g + 1)
            if not last:
                return sec, 0, numbers(sec, i, U, u + 1, 0)
            k = order.index(sec) + 1
            return (order[k], 0, numbers(order[k], None, 0, 0, 0)) if k < len(order) else None

        def split_hi(act, nxt):
            if nxt is None:
                return
            sec, g, (r, r_at, s, s_at, landed) = nxt
            kt = sec.kts[g]
            act.wait_ge(raw_full[r_at % RING], landed)
            act.wait_ge(slab_done, s + 1)
            nc.scalar.activation(w_hi[:, s_at % 2, 0:kt], raw[:, r_at % RING, 0:kt], ACT.Copy).then_inc(hi_done, 1)

        def split_lo(dve, nxt):
            if nxt is None:
                return
            sec, g, (r, r_at, s, s_at, landed) = nxt
            kt = sec.kts[g]
            dve.wait_ge(hi_done, s + 1)
            nc.vector.tensor_tensor(w_lo[:, s_at % 2, 0:kt], raw[:, r_at % RING, 0:kt],
                                    w_hi[:, s_at % 2, 0:kt].bitcast(F32), ALU.subtract).then_inc(raw_used, 1)

        def unroll_of(sec):
            per = sec.g * sec.rs
            return 4 if per == 1 else 2 if per in (2, 4) else sec.pairs

        def split_hi_ahead(act, sec):
            split_hi(act, following(sec, None, unroll_of(sec), 0, 0, sec.pairs == 1))

        def act_pairs(act, sec, take, peeled=1, ahead=False):
            U = unroll_of(sec)

            def body(i, u, last):
                for g in range(sec.g):
                    if not (ahead and i is None and u == 0 and g == 0):
                        split_hi(act, following(sec, i, U, u, g, last))
                    if g == 0 and (i is not None or u):
                        take(i, u - 1, U)
            each_pair(act, sec.pairs, U, body, peeled=peeled)
            take(None, sec.pairs - 1, U)

        def dve_pairs(dve, sec, take, between=None):
            U = unroll_of(sec)

            def body(i, u, last):
                for g in range(sec.g):
                    if between:
                        between(i, u, U)
                    split_lo(dve, following(sec, i, U, u, g, last))
                    if g == 0 and (i is not None or u):
                        take(i, u - 1, U)
            each_pair(dve, sec.pairs, U, body, peeled=1)
            take(None, sec.pairs - 1, U)

        def out_bank(sec, u, j):
            return banks[2 * ((sec.o0 + u) % 2) + j]

        def pe_pairs(pe, sec, xh, xl, L, after=None, norm=None, tile_ready=None):
            if norm:
                tile_ready = lambda k: norm.wait_tile(pe, k)
            U = 2

            def body(i, u, last):
                pe.wait_ge(took[sec.taker], at(i, U, sec.t0 + u + 1))
                if sec.other is not None:
                    pe.wait_ge(took["act" if sec.taker == "dve" else "dve"], sec.other + 2)
                k0 = 0
                for g, kt in enumerate(sec.kts):
                    r, r_at, s, s_at, _ = numbers(sec, i, U, u, g)
                    pe.wait_ge(raw_used, r + 1 + RING)
                    for j in range(2):
                        out = out_bank(sec, u, j)[:, 0:L]
                        for k in range(kt):
                            if tile_ready and i is None and u == 0 and j == 0:
                                tile_ready(k0 + k)
                            hi = w_hi[:, s_at % 2, k, j * P:(j + 1) * P]
                            lo = w_lo[:, s_at % 2, k, j * P:(j + 1) * P]
                            start, stop = k0 + k == 0, k0 + k == sum(sec.kts) - 1
                            nc.tensor.matmul(out, hi, xh[:, k0 + k, 0:L], start=start, stop=False)
                            nc.tensor.matmul(out, hi, xl[:, k0 + k, 0:L], start=False, stop=False)
                            mm = nc.tensor.matmul(out, lo, xh[:, k0 + k, 0:L], start=False, stop=stop)
                    mm.then_inc(slab_done, 1)
                    k0 += kt
                if after:
                    after(i, u, U)
            each_pair(pe, sec.pairs, U, body, peeled=2 if tile_ready and sec.pairs > 2 else 0)

        def taken(eng, sec, i, u, U):
            eng.wait_ge(took[sec.taker], at(i, U, sec.t0 + u + 3))

        def outputs_ready(eng, sec, i, u, U):
            s = at(i, U * sec.g, sec.s0 + (u + 1) * sec.g - 1)
            eng.wait_ge(slab_done, s + 3)

        acc = sb("acc", [P, 3, SLAB_N])
        ADA_STEPS = SLAB_K

        def dve_ada(dve, a, a_at, r, r_at, landed, k0=0, k1=SLAB_K):
            if k0 == 0:
                dve.wait_ge(raw_full[r_at % RING], landed)
                dve.wait_ge(ada_sum, a + 1)
            for k in range(k0, k1):
                src, w = raw[:, r_at % RING, k], c_act[:, k:k + 1]
                part = acc[:, 2 if k % 2 else a_at % 2]
                if k == 1:
                    dve.wait_ge(raw_used, r + RING)
                if k < 2:
                    nc.vector.tensor_scalar(part, src, w, None, ALU.mult).then_inc(ada_step, 1)
                else:
                    dve.wait_ge(ada_step, a * ADA_STEPS + (k - 1))
                    nc.vector.scalar_tensor_tensor(out=part, in0=src, scalar=w, in1=part, op0=ALU.mult, op1=ALU.add).then_inc(ada_step, 1)
            if k1 == SLAB_K:
                dve.wait_ge(ada_step, a * ADA_STEPS + ADA_STEPS)
                nc.vector.tensor_tensor(acc[:, a_at % 2], acc[:, a_at % 2], acc[:, 2], ALU.add).then_inc(raw_used, 1)

        def pe_ada(pe, r, a, a_at, col0):
            pe.wait_ge(raw_used, r + 1 + RING)
            for j in range(2):
                mm = nc.tensor.matmul(banks[7][:, col0 + j:col0 + j + 1] if isinstance(col0, int)
                                      else banks[7][:, bass.ds(col0 + j, 1)],
                                      acc[:, a_at % 2, j * P:(j + 1) * P], const("ones")[:, 0:1],
                                      start=True, stop=True)
            mm.then_inc(ada_sum, 1)

        def dve_mod(dve, a, b, sums):
            dve.wait_ge(ada_sum, sums + 2)
            link(dve, "dve", nc.vector.tensor_tensor(mod[:, a:b], banks[7][:, a:b], col("b_ada", a, b - a), ALU.add))

        loaded = [sem(f"loaded{i}") for i in range(5)]
        tr_ready, tr_taken, cst_ready = sem("tr_ready"), sem("tr_taken"), sem("cst_ready")
        start = ExitStack()
        rows_v = sb("rows_v", [P, 3, P], c=start)
        rows_x = sb("rows_x", [P, 2, D], c=start)
        rows_m = sb("rows_m", [META, D], c=start)
        with nc.Block() as block:
            @block.sync
            def _(sp):
                sp.dma_start(cst[:], t["const"]).then_inc(loaded[0], 16)
                for v, group in enumerate(VECTORS):
                    row = 0
                    for name, rows in group:
                        src = t[name]
                        src = (src.rearrange("a (r p) -> (a r) p", p=P) if len(src.shape) == 2 else
                               src.rearrange("(r p) -> r p", p=P) if len(src.shape) == 1 else
                               src.rearrange("a b (r p) -> (a b r) p", p=P) if src.shape[-1] % P == 0 else
                               src.rearrange("a (r b) p -> (a r) (b p)", b=2))
                        sp.dma_start(rows_v[row:row + rows, v], src).then_inc(loaded[1 + v], 16)
                        row += rows
                load_to(sp, RING)

            @block.tensor
            def _(pe):
                pe.sem_inc(slab_done, 2)
                pe.sem_inc(act_took, 2)
                pe.sem_inc(dve_took, 2)
                pe.sem_inc(ada_sum, 2)
                pe.sem_inc(raw_used, RING)
                pe.wait_ge(loaded[0], 16)
                for v, group in enumerate(VECTORS):
                    rows = sum(n for _, n in group)
                    pe.wait_ge(loaded[1 + v], 16 * len(group))
                    mm = nc.tensor.transpose(banks[6][:, v * P:v * P + rows], rows_v[0:rows, v], ident[0:rows, 0:rows])
                mm.then_inc(tr_ready, 1)
                pe.wait_ge(loaded[4], 32)
                for q in range(4):
                    for k in range(4):
                        ft, c = 2 * q + k // 2, k % 2
                        mm = nc.tensor.transpose(banks[q][:, k * P:(k + 1) * P], rows_x[:, c, ft * P:(ft + 1) * P], ident)
                    mm.then_inc(tr_ready, 1)
                for ft in range(DT):
                    mm = nc.tensor.transpose(banks[4][:, ft * META:(ft + 1) * META], rows_m[:, ft * P:(ft + 1) * P], ident[0:META, 0:META])
                mm.then_inc(tr_ready, 1)

            @block.vector
            def _(dve):
                dve.wait_ge(tr_ready, 1)
                for v, group in enumerate(VECTORS):
                    rows = sum(n for _, n in group)
                    ins = nc.vector.tensor_copy(vec[:, v, 0:rows], banks[6][:, v * P:v * P + rows])
                ins.then_inc(cst_ready, 1)
                for q in range(4):
                    dve.wait_ge(tr_ready, q + 2)
                    nc.vector.tensor_copy(h[:, 2 * q:2 * q + 2, META:T2],
                                          banks[q][:, :].rearrange("p (f n) -> p f n", f=2))
                dve.wait_ge(tr_ready, 6)
                nc.vector.tensor_copy(h[:, :, 0:META], banks[4][:, 0:DT * META].rearrange("p (f n) -> p f n", f=DT)).then_inc(tr_taken, 1)

            @block.scalar
            def _(act):
                act.dma_start(rows_x[:], t["x"][0].rearrange("(c p) d -> p c d", p=P)).then_inc(loaded[4], 16)
                act.dma_start(rows_m[:], t["meta_2"]).then_inc(loaded[4], 16)
                act.wait_ge(cst_ready, 1)
                nc.scalar.activation(c_act[:], col("c", 0, 8), ACT.Silu).then_inc(cst_ready, 1)
        start.close()

        norm_count, lo_count, hi_count = [0], [0], [0]
        n_sq, n_sum, n_ms, n_y, n_mid, n_hi, n_lo = (sem(x) for x in ("n_sq", "n_sum", "n_ms", "n_y", "n_mid", "n_hi", "n_lo"))

        def inverse_root(dve, act_wait, act_done, ms, y, tmp, out):
            dve.wait_ge(act_wait, act_done)
            link(dve, "dve", nc.vector.tensor_tensor(tmp, y, y, ALU.mult))
            link(dve, "dve", nc.vector.scalar_tensor_tensor(out=tmp, in0=tmp, scalar=-0.5, in1=ms, op0=ALU.mult, op1=ALU.mult))
            link(dve, "dve", nc.vector.scalar_tensor_tensor(out=out, in0=tmp, scalar=1.5, in1=y, op0=ALU.add, op1=ALU.mult))

        class Norm:

            def __init__(self, src, L, a_cols, b_cols=None, prep=None, dst=None, add_to=None):
                self.src, self.L, self.a_cols, self.b_cols, self.prep, self.dst, self.add_to = src, L, a_cols, b_cols, prep, dst, add_to
                self.q, self.lo0, self.hi0 = norm_count[0], lo_count[0], hi_count[0]
                norm_count[0] += 1
                lo_count[0] += DT if dst is None else 0
                hi_count[0] += DT if dst is None and add_to is None else 0

            def square(self, act, u, sq):
                nc.scalar.activation(sq[:, 2 * u:2 * u + 2], self.src[:, 2 * u:2 * u + 2], ACT.Square).then_inc(n_sq, 1)

            def total(self, pe, u, sq):
                pe.wait_ge(n_sq, 4 * self.q + u + 1)
                for k in (2 * u, 2 * u + 1):
                    mm = nc.tensor.matmul(banks[6][:, 0:self.L], const("ones"), sq[:, k], start=k == 0, stop=k == DT - 1)
                if u == 3:
                    mm.then_inc(n_sum, 1)

            def on_act(self, act, mid=None, between=None):
                L = self.L
                act.wait_ge(n_ms, self.q + 1)
                nc.scalar.activation(stat[:, 1, 0:L], stat[:, 0, 0:L], ACT.Abs_reciprocal_sqrt).then_inc(n_y, 1)
                if between:
                    between()
                if self.dst is None and self.add_to is None:
                    for k in range(DT):
                        act.wait_ge(n_mid, DT * self.q + k + 1)
                        nc.scalar.activation(x_hi[:, k, 0:L], mid[:, k], ACT.Identity, bias=self.b_cols(k) if self.b_cols else 0.0).then_inc(n_hi, 1)

            def on_dve(self, dve, mid=None):
                L = self.L
                if self.prep:
                    self.prep(dve)
                dve.wait_ge(n_sum, self.q + 1)
                nc.vector.tensor_scalar(stat[:, 0, 0:L], banks[6][:, 0:L], 1.0 / D, EPS, ALU.mult, ALU.add).then_inc(n_ms, 1)
                inverse_root(dve, n_y, self.q + 1, stat[:, 0, 0:L], stat[:, 1, 0:L], stat[:, 2, 0:L], stat[:, 3, 0:L])
                for n in range(DT + 2):
                    if n < DT:
                        o = self.dst[:, n] if self.dst is not None else mid[:, n]
                        nc.vector.scalar_tensor_tensor(out=o, in0=self.src[:, n], scalar=self.a_cols(n), in1=stat[:, 3, 0:L],
                                                       op0=ALU.mult, op1=ALU.mult).then_inc(n_mid, 1)
                    k = n - 2
                    if k < 0 or self.dst is not None:
                        continue
                    if self.add_to is not None:
                        dve.wait_ge(n_mid, DT * self.q + k + 1)
                        nc.vector.tensor_tensor(self.add_to[:, k], self.add_to[:, k], mid[:, k], ALU.add).then_inc(n_lo, 1)
                    else:
                        dve.wait_ge(n_hi, self.hi0 + k + 1)
                        nc.vector.scalar_tensor_tensor(out=x_lo[:, k, 0:L], in0=mid[:, k], scalar=self.b_cols(k) if self.b_cols else 0.0,
                                                       in1=x_hi[:, k, 0:L].bitcast(F32), op0=ALU.add, op1=ALU.subtract).then_inc(n_lo, 1)

            def wait_tile(self, eng, k):
                eng.wait_ge(n_lo, self.lo0 + k + 1)

            def wait_scaled(self, eng, k):
                eng.wait_ge(n_mid, DT * self.q + k + 1)

        def modulation(w_name, shift, scale):
            def prep(dve):
                link(dve, "dve", nc.vector.scalar_tensor_tensor(
                    out=scale_col[:], in0=mod[:, 8 * scale:8 * scale + 8], scalar=1.0, in1=col(w_name, 0, 8), op0=ALU.add, op1=ALU.mult))
            return (lambda k: scale_col[:, k:k + 1]), (lambda k: mod[:, 8 * shift + k:8 * shift + k + 1]), prep

        h1 = h[:, :, META:T2]

        norm_ffn1 = Norm(h1, T1, *modulation("norm_ffn1", 0, 1))
        first_sq = ExitStack()
        sq0 = sb("sq0", [P, DT, T1], c=first_sq)
        with nc.Block() as block:
            @block.sync
            def _(sp):
                load_to(sp, S["up1a"].r0 + 1 + RING)

            @block.scalar
            def _(act):
                for u in range(4):
                    norm_ffn1.square(act, u, sq0)
                split_hi(act, (S["up1a"], 0, numbers(S["up1a"], None, 0, 0, 0)))

            @block.vector
            def _(dve):
                for a in range(UPFRONT):
                    dve_ada(dve, a, a, a, a, LANDED * (a // RING + 1))
                dve_mod(dve, 0, 2 * UPFRONT, UPFRONT)
                split_lo(dve, (S["up1a"], 0, numbers(S["up1a"], None, 0, 0, 0)))

            @block.tensor
            def _(pe):
                for u in range(4):
                    norm_ffn1.total(pe, u, sq0)
                for a in range(UPFRONT):
                    pe_ada(pe, a, a, a, 2 * a)
        first_sq.close()

        p_zero, p_ready, p_done, xu_ready, x_done, yu_ready, y_done = (
            sem(x) for x in ("p_zero", "p_ready", "p_done", "xu_ready", "x_done", "yu_ready", "y_done"))
        stage_sems.clear()
        uid = [0]

        def swiglu(ups, down, gate, norm, then):
            first_pair = [sum(x.pairs for x in ups[:n]) for n in range(len(ups))]
            uid[0] += 1
            q = uid[0]
            L = T1
            gated, hid_h, hid_l = (sem(f"{x}{q}") for x in ("gated", "hid_h", "hid_l"))
            with ExitStack() as c:
                hid_hi = sb(f"hid_hi{q}", [P, FF1T, L], F32R, c)
                hid_lo = sb(f"hid_lo{q}", [P, FF1T, L], F32R, c)
                act_out = sb(f"act_out{q}", [P, 2, L], c=c)
                hid = sb(f"hid{q}", [P, 2, L], c=c)
                mid = sb(f"mid{q}", [P, DT, L], c=c)
                sq = sb(f"sq{q}", [P, DT, L], c=c)
                with nc.Block() as block:
                    @block.sync
                    def _(sp):
                        load_to(sp, down.r0 + 12 + RING)

                    @block.scalar
                    def _(act):
                        def take(up, n0, i, u, U):
                            n, b = at(i, U, n0 + u), (up.o0 + u) % 2
                            outputs_ready(act, up, i, u, U)
                            nc.scalar.activation(act_out[:, b], out_bank(up, u, 0)[:, 0:L], ACT.Silu).then_inc(gated, 1)
                            taken(act, up, i, u, U)
                            nc.scalar.activation(hid_hi[:, bass.ds(n, 1)], hid[:, b:b + 1], ACT.Copy).then_inc(hid_h, 1)
                        norm.on_act(act, mid, lambda: split_hi_ahead(act, ups[0]))
                        for up, n0 in zip(ups, first_pair):
                            act_pairs(act, up, lambda i, u, U: take(up, n0, i, u, U), ahead=n0 == 0)

                        def square(i, u, U):
                            taken(act, down, None, u, 0)
                            then.square(act, u, sq)
                        act_pairs(act, down, square)

                    @block.gpsimd
                    def _(pool):
                        def body(i, u, last):
                            n, b = at(i, 2, u), (ups[0].o0 + u) % 2
                            pool.wait_ge(hid_h, n + 1)
                            nc.gpsimd.tensor_tensor(hid_lo[:, bass.ds(n, 1)], hid[:, b:b + 1],
                                                    hid_hi[:, bass.ds(n, 1)].bitcast(F32), ALU.subtract).then_inc(hid_l, 1)
                        each_pair(pool, FF1T, 2, body)

                    @block.vector
                    def _(dve):
                        dve.sem_inc(hid_l, 2)
                        norm.on_dve(dve, mid)

                        def between(i, u, U):
                            a = at(i, U, u + UPFRONT)
                            r_at = ups[0].r0 + 2 * u + 1
                            landed = at(i, LANDED * 2 * U // RING, LANDED * (r_at // RING + 1))
                            dve_ada(dve, a, u + UPFRONT, at(i, 2 * U, r_at), r_at, landed)

                        def take(up, n0, i, u, U):
                            b = (up.o0 + u) % 2
                            dve.wait_ge(gated, at(i, U, n0 + u + 1))
                            dve.wait_ge(hid_l, at(i, U, n0 + u + 1))
                            nc.vector.tensor_tensor(hid[:, b], act_out[:, b], out_bank(up, u, 1)[:, 0:L], ALU.mult).then_inc(dve_took, 1)
                        for up, n0 in zip(ups, first_pair):
                            dve_pairs(dve, up, lambda i, u, U: take(up, n0, i, u, U), between if up.name == "up1a" else None)
                            if up.name == "up1a":
                                dve_mod(dve, 2 * UPFRONT, 2 * (UPFRONT + BESIDE_UP), UPFRONT + BESIDE_UP)
                        link(dve, "dve", nc.vector.tensor_scalar(gain_col[:], mod[:, 8 * gate:8 * gate + 8], 0.5, None, ALU.mult))

                        def residual(i, u, U):
                            outputs_ready(dve, down, i, u, U)
                            for j in range(2):
                                k = 2 * u + j
                                ins = nc.vector.scalar_tensor_tensor(
                                    out=h1[:, k], in0=out_bank(down, u, j)[:, 0:L], scalar=gain_col[:, k:k + 1], in1=h1[:, k],
                                    op0=ALU.mult, op1=ALU.add)
                            ins.then_inc(dve_took, 1)
                        dve_pairs(dve, down, residual)

                    @block.tensor
                    def _(pe):
                        def after(i, u, U):
                            a = at(i, U, u + UPFRONT)
                            pe_ada(pe, at(i, 2 * U, ups[0].r0 + 2 * u + 1), a, u + UPFRONT, at(i, 2 * U, 2 * (u + UPFRONT)))
                        for up in ups:
                            pe_pairs(pe, up, x_hi, x_lo, L, after if up.name == "up1a" else None, norm if up is ups[0] else None)
                        pe_pairs(pe, down, hid_hi, hid_lo, L, lambda i, u, U: then.total(pe, u - 1, sq) if u else None,
                                 tile_ready=lambda k: pe.wait_ge(hid_l, k + 3))
                        then.total(pe, 3, sq)

        norm_mix = Norm(h1, T1, *modulation("norm_mix", 3, 4))
        swiglu([S["up1a"], S["up1b"]], S["down1"], 2, norm_ffn1, norm_mix)


        mix = ExitStack()
        ya_hi = sb("ya_hi", [P, CA // P, T1], F32R, mix)
        ya_lo = sb("ya_lo", [P, CA // P, T1], F32R, mix)
        o_sum = sb("o_sum", [P, HEADS, T1], c=mix)
        gdn = ExitStack()
        qkv = sb("qkv", [P, 3 * HEADS, T1], c=gdn)
        beta = sb("beta", [P, 2, 2, HEADS], c=gdn)
        g_log = sb("g_log", [P, 2, 2, HEADS], c=gdn)
        conv = ExitStack()
        mid_m = sb("mid_m", [P, DT, T1], c=conv)
        cab = sb("cab", [P, CA // P, T1], c=conv)
        cac = sb("cac", [P, CA // P, T1], c=conv)
        PAD1 = T1 + 2
        cav = sb("cav", [P, CA // P, PAD1], c=conv)
        ya = sb("ya", [P, CA // P, T1], c=conv)
        PAD5 = T1 + 4
        win = sb("win", [P, 2, 2, PAD5], c=conv)
        wsum = sb("wsum", [P, 2, 2, T1], c=conv)
        w_ba = sb("w_ba", [P, DT, 32], c=conv)
        w_ba_hi = sb("w_ba_hi", [P, DT, 32], F32R, conv)
        w_ba_lo = sb("w_ba_lo", [P, DT, 32], F32R, conv)
        heads_row = sb("heads_row", [1, 2, 2, HEADS], c=conv)
        heads_all = sb("heads_all", [P, 2, 2, HEADS], c=conv)
        ba = sb("ba", [P, 2, 4 * HEADS], c=conv)
        sp_t = sb("sp_t", [P, 6, 2, 2 * HEADS], c=conv)
        small = sem("mix_small")
        ca_act, cv_ready, conv_step, conv_done = sem("ca_act"), sem("cv_ready"), sem("conv_step"), sem("conv_done")
        qkv_in, qkv_out, ba_sem, ba_hi_done, ba_act = (sem(x) for x in ("qkv_in", "qkv_out", "ba_sem", "ba_hi_done", "ba_act"))
        ya_done, pads, ba_exp, tap_done = sem("ya_done"), sem("pads"), sem("ba_exp"), sem("tap_done")

        def conv_w(i, u, U, tap, j):
            v, row = vcol["conv_dn"]
            first = row + 24 * tap + 2 * u + j
            return vec[:, v, first:first + 1] if i is None else vec[:, v, bass.ds(i * (2 * U) + first, 1)]

        with nc.Block() as block:
            @block.sync
            def _(sp):
                sp.dma_start(w_ba[:], w_in[:, gate0 - 32:gate0].rearrange("(k p) n -> p k n", p=P)).then_inc(small, 16)
                for k, name in enumerate(("dt_bias_fwd", "dt_bias_bwd", "a_log_fwd", "a_log_bwd")):
                    sp.dma_start(heads_row[:, k // 2, k % 2], t[name]).then_inc(small, 16)
                load_to(sp, S["qkv"].r0 + 12 + RING)

            @block.scalar
            def _(act):
                def copy_to(dst, name):
                    sec = S[name]

                    def take(i, u, U):
                        outputs_ready(act, sec, i, u, U)
                        for j in range(2):
                            ins = nc.scalar.activation(dst[:, 2 * u + j], out_bank(sec, u, j)[:, 0:T1], ACT.Copy)
                        ins.then_inc(act_took, 1)
                    return take
                norm_mix.on_act(act, mid_m, lambda: split_hi_ahead(act, S["ca_b"]))
                act_pairs(act, S["ca_b"], copy_to(cab, "ca_b"), ahead=True)
                act_pairs(act, S["ca_c"], copy_to(cac, "ca_c"))
                act_pairs(act, S["ca_v"], lambda i, u, U: None)
                act.wait_ge(small, 80)
                nc.scalar.activation(w_ba_hi[:], w_ba[:], ACT.Copy).then_inc(ba_hi_done, 1)
                sec = S["qkv"]
                act.wait_ge(pads, 1)

                def silu(n, b):
                    act.wait_ge(conv_done, n + 1)
                    nc.scalar.activation(qkv[:, bass.ds(n * 2, 2)], wsum[:, b], ACT.Silu).then_inc(qkv_out, 1)

                def take(i, u, U):
                    b = u % 2
                    outputs_ready(act, sec, i, u, U)
                    for j in range(2):
                        ins = nc.scalar.activation(win[:, b, j, 2:2 + T1], out_bank(sec, u, j)[:, 0:T1], ACT.Copy)
                    ins.then_inc(act_took, 1)
                    taken(act, sec, i, u, U)
                    for j in range(2):
                        ins = nc.scalar.activation(wsum[:, b, j], win[:, b, j, 0:T1], ACT.Copy, scale=conv_w(i, u, U, 0, j))
                    ins.then_inc(tap_done, 1)
                    if i is not None or u:
                        silu(at(i, U, u - 1), (u - 1) % 2)
                act_pairs(act, sec, take, peeled=2)
                silu(sec.pairs - 1, (sec.pairs - 1) % 2)
                act.wait_ge(ya_done, 1)
                nc.scalar.activation(ya_hi[:], ya[:], ACT.Copy).then_inc(ya_done, 1)
                act.wait_ge(ba_sem, 1)
                nc.scalar.activation(heads_all[:], banks[6][:, 128:160].rearrange("p (a b c) -> p a b c", a=2, b=2), ACT.Copy).then_inc(ba_act, 1)
                nc.scalar.activation(ba[:, 0], banks[6][:, 0:32], ACT.Copy)
                nc.scalar.activation(ba[:, 1], banks[6][:, 32:64], ACT.Copy).then_inc(ba_act, 1)
                act.wait_ge(ba_act, 2)
                nc.scalar.activation(beta[:], ba[:, :, 0:16].rearrange("p c (d h) -> p c d h", d=2), ACT.Sigmoid)
                nc.scalar.activation(heads_all[:, 1], heads_all[:, 1], ACT.Exp).then_inc(ba_act, 1)
                act.wait_ge(ba_exp, 1)
                nc.scalar.activation(sp_t[:, 2], sp_t[:, 1], ACT.Exp, scale=-1.0).then_inc(ba_act, 1)

            @block.vector
            def _(dve):
                nc.vector.memset(cav[:], 0.0).then_inc(cv_ready, 1)
                nc.vector.memset(win[:], 0.0).then_inc(pads, 1)
                norm_mix.on_dve(dve, mid_m)
                dve_pairs(dve, S["ca_b"], lambda i, u, U: None)
                dve_pairs(dve, S["ca_c"], lambda i, u, U: None)
                dve.wait_ge(cv_ready, 1)
                sec = S["ca_v"]

                def product(i, u, U):
                    outputs_ready(dve, S["ca_v"], i, u, U)
                    taken(dve, S["ca_c"], None, 1, 0)
                    for j in range(2):
                        k = 2 * u + j
                        ins = nc.vector.tensor_tensor(cav[:, k, 1:1 + T1], out_bank(S["ca_v"], u, j)[:, 0:T1], cac[:, k], ALU.mult)
                    ins.then_inc(dve_took, 1)
                dve_pairs(dve, sec, product)
                taken(dve, sec, None, 1, 0)
                for tap in range(3):
                    for k in range(4):
                        w = col("conv_a", 4 * tap + k)
                        if tap == 0:
                            ins = nc.vector.tensor_scalar(ya[:, k], cav[:, k, 0:T1], w, None, ALU.mult)
                        else:
                            ins = nc.vector.scalar_tensor_tensor(out=ya[:, k], in0=cav[:, k, tap:tap + T1], scalar=w, in1=ya[:, k],
                                                                 op0=ALU.mult, op1=ALU.add)
                    link(dve, "dve", ins)
                nc.vector.tensor_tensor(ya[:], ya[:], cab[:], ALU.mult).then_inc(ya_done, 1)
                dve.wait_ge(ba_hi_done, 1)
                nc.vector.tensor_tensor(w_ba_lo[:], w_ba[:], w_ba_hi[:].bitcast(F32), ALU.subtract).then_inc(ba_hi_done, 1)
                sec = S["qkv"]

                def taps(i, u, U):
                    b, n = u % 2, at(i, U, u)
                    dve.wait_ge(tap_done, at(i, U, u + 1))
                    for k in range(8):
                        tap, j = 1 + k // 2, k % 2
                        if k >= 2:
                            dve.wait_ge(conv_step, n * 7 + (k - 1))
                        nc.vector.scalar_tensor_tensor(out=wsum[:, b, j], in0=win[:, b, j, tap:tap + T1], scalar=conv_w(i, u, U, tap, j),
                                                       in1=wsum[:, b, j], op0=ALU.mult, op1=ALU.add).then_inc(conv_done if k == 7 else conv_step, 1)
                dve_pairs(dve, sec, taps)
                dve.wait_ge(ya_done, 2)
                nc.vector.tensor_tensor(ya_lo[:], ya[:], ya_hi[:].bitcast(F32), ALU.subtract)
                dve.wait_ge(ba_act, 3)
                al, x, neg = sp_t[:, 0], sp_t[:, 0], sp_t[:, 1]
                bias = heads_all[:, 0].rearrange("p d h -> p (d h)")[:, None, :].broadcast_to([P, 2, 2 * HEADS])
                rate = heads_all[:, 1].rearrange("p d h -> p (d h)")[:, None, :].broadcast_to([P, 2, 2 * HEADS])
                link(dve, "dve", nc.vector.tensor_tensor(x, ba[:, :, 16:32], bias, ALU.add))
                link(dve, "dve", nc.vector.tensor_scalar(neg, x, -1.0, None, ALU.mult))
                nc.vector.tensor_tensor(neg, neg, x, ALU.max).then_inc(ba_exp, 1)
                dve.wait_ge(ba_act, 4)
                e, s, s2, poly = sp_t[:, 2], sp_t[:, 3], sp_t[:, 4], sp_t[:, 5]
                link(dve, "dve", nc.vector.tensor_scalar(s, e, 2.0, None, ALU.add))
                link(dve, "dve", nc.vector.reciprocal(s, s))
                link(dve, "dve", nc.vector.tensor_tensor(s, s, e, ALU.mult))
                link(dve, "dve", nc.vector.tensor_tensor(s2, s, s, ALU.mult))
                link(dve, "dve", nc.vector.tensor_scalar(poly, s2, 2.0 / 19, 2.0 / 17, ALU.mult, ALU.add))
                for k in (15, 13, 11, 9, 7, 5, 3, 1):
                    link(dve, "dve", nc.vector.tensor_tensor(poly, poly, s2, ALU.mult))
                    link(dve, "dve", nc.vector.tensor_scalar(poly, poly, 2.0 / k, None, ALU.add))
                link(dve, "dve", nc.vector.tensor_tensor(poly, poly, s, ALU.mult))
                link(dve, "dve", nc.vector.scalar_tensor_tensor(out=poly, in0=x, scalar=0.0, in1=poly, op0=ALU.max, op1=ALU.add))
                nc.vector.scalar_tensor_tensor(out=g_log[:].rearrange("p c d h -> p c (d h)"), in0=poly, scalar=-1.0, in1=rate,
                                               op0=ALU.mult, op1=ALU.mult)

            @block.tensor
            def _(pe):
                for name in ("ca_b", "ca_c", "ca_v", "qkv"):
                    pe_pairs(pe, S[name], x_hi, x_lo, T1, norm=norm_mix if name == "ca_b" else None)
                pe.wait_ge(ba_hi_done, 2)
                for c in range(2):
                    out = banks[6][:, 32 * c:32 * c + 32]
                    for k in range(DT):
                        rows = slice(c * P, (c + 1) * P)
                        nc.tensor.matmul(out, x_hi[:, k, rows], w_ba_hi[:, k], start=k == 0, stop=False)
                        nc.tensor.matmul(out, x_lo[:, k, rows], w_ba_hi[:, k], start=False, stop=False)
                        nc.tensor.matmul(out, x_hi[:, k, rows], w_ba_lo[:, k], start=False, stop=k == DT - 1)
                mm = nc.tensor.matmul(banks[6][:, 128:160], const("ones")[0:1], heads_row[:].rearrange("p a b c -> p (a b c)"),
                                      start=True, stop=True)
                mm.then_inc(ba_sem, 1)
        conv.close()

        k_rows = sb("k_rows", [P, 2, HEADS, P], c=gdn)
        v_rows = sb("v_rows", [P, 2, HEADS, P], c=gdn)
        g_cum = sb("g_cum", [P, 2, 2, HEADS], c=gdn)
        g_end = sb("g_end", [P, 2, 2, HEADS], c=gdn)
        g_exp = sb("g_exp", [P, 2, 2, HEADS], c=gdn)
        a_t = sb("a_t", [P, 2, HEADS, P], c=gdn)
        inv = sb("inv", [P, 2, HEADS, P], c=gdn)
        inv_t = sb("inv_t", [P, 2, HEADS, P], c=gdn)
        attn_t = sb("attn_t", [P, 2, HEADS, P], c=gdn)
        prod = sb("prod", [P, 2, HEADS, P], c=gdn)
        dec_t = prod
        q_exp = sb("q_exp", [P, HEADS, P], c=gdn)
        sq = attn_t[:, 0].rearrange("p (a x) n -> p a (x n)", a=4)
        rt = prod[:].rearrange("p c (a x) n -> p (c a) (x n)", a=4).rearrange("p (a b) n -> p a b n", b=2)
        rt_y = [k_rows[:, 0, 4 * b:4 * b + 4].rearrange("p (a x) n -> p a (x n)", a=2) for b in range(2)]
        state, k_end, v_new = inv[:, 0], inv[:, 1], prod
        l2_sq, l2_sum, l2_ms, l2_y, l2_done = (sem(x) for x in ("l2_sq", "l2_sum", "l2_ms", "l2_y", "l2_done"))
        rows_ready, rows_taken, cum_ready, cum_taken = (sem(x) for x in ("rows_ready", "rows_taken", "cum_ready", "cum_taken"))
        with nc.Block() as block:
            @block.scalar
            def _(act):
                def root(q):
                    act.wait_ge(l2_ms, q + 1)
                    if q >= 2:
                        act.wait_ge(l2_done, q - 1)
                    nc.scalar.activation(rt_y[q % 2], rt[:, q % 2], ACT.Abs_reciprocal_sqrt).then_inc(l2_y, 1)
                for q in range(8):
                    if q >= 2:
                        act.wait_ge(l2_sum, q - 1)
                    nc.scalar.activation(sq[:, 2 * (q % 2):2 * (q % 2) + 2], qkv[:, 2 * q:2 * q + 2], ACT.Square).then_inc(l2_sq, 1)
                    if q:
                        root(q - 1)
                root(7)
                for q in range(8):
                    act.wait_ge(rows_ready, q + 1)
                    dst, c, hh = (k_rows, v_rows)[q // 4], (q // 2) % 2, 4 * (q % 2)
                    nc.scalar.activation(dst[:, c, hh:hh + 4], banks[q % 4][:].rearrange("p (h n) -> p h n", h=4), ACT.Copy).then_inc(rows_taken, 1)

            @block.tensor
            def _(pe):
                for d, name in enumerate(("upto", "from")):
                    for c in range(2):
                        mm = nc.tensor.matmul(banks[6][:, 16 * d + 8 * c:16 * d + 8 * c + 8], const(name), g_log[:, c, d], start=True, stop=True)
                        mm = nc.tensor.matmul(banks[6][:, 32 + 16 * d + 8 * c:40 + 16 * d + 8 * c], const("ones"), g_log[:, c, d], start=True, stop=True)
                mm.then_inc(cum_ready, 1)
                for q in range(8):
                    pe.wait_ge(l2_sq, q + 1)
                    if q >= 2:
                        pe.wait_ge(l2_ms, q - 1)
                    nc.tensor.matmul(banks[4 + q % 2][:].rearrange("p (a b) -> p a b", a=2), const("ones"), sq[:, 2 * (q % 2):2 * (q % 2) + 2], start=True, stop=True).then_inc(l2_sum, 1)
                pe.wait_ge(l2_done, 8)
                for q in range(8):
                    if q >= 4:
                        pe.wait_ge(rows_taken, q - 3)
                    base, c, hh = (8, 16)[q // 4], (q // 2) % 2, 4 * (q % 2)
                    for k in range(4):
                        mm = nc.tensor.transpose(banks[q % 4][:, k * P:(k + 1) * P], qkv[:, base + hh + k, c * P:(c + 1) * P], ident)
                    mm.then_inc(rows_ready, 1)

            @block.vector
            def _(dve):
                dve.wait_ge(cum_ready, 1)
                flat = lambda x: x.rearrange("p d c h -> p (d c h)")
                link(dve, "dve", nc.vector.tensor_copy(flat(g_cum[:]), banks[6][:, 0:32]))
                nc.vector.tensor_tensor(flat(g_end[:]), banks[6][:, 32:64], flat(g_cum[:]), ALU.subtract).then_inc(cum_taken, 1)
                for q in range(9):
                    if q < 8:
                        dve.wait_ge(l2_sum, q + 1)
                        s = float(P) if q < 4 else 1.0
                        nc.vector.tensor_scalar(rt[:, q % 2], banks[4 + q % 2][:].rearrange("p (a b) -> p a b", a=2), EPS, s, ALU.add, ALU.mult).then_inc(l2_ms, 1)
                    if q:
                        p = q - 1
                        inverse_root(dve, l2_y, p + 1, rt[:, p % 2], rt_y[p % 2], rt[:, 2], rt[:, 3])
                        nc.vector.tensor_tensor(qkv[:, 2 * p:2 * p + 2], qkv[:, 2 * p:2 * p + 2], rt[:, 3], ALU.mult).then_inc(l2_done, 1)
        with nc.Block() as block:
            @block.scalar
            def _(act):
                nc.scalar.activation(g_end[:], g_end[:], ACT.Exp)
                nc.scalar.activation(g_exp[:], g_cum[:], ACT.Exp).then_inc(cum_taken, 1)

            @block.vector
            def _(dve):
                dve.wait_ge(cum_taken, 2)
                nc.vector.tensor_scalar(g_exp[:], g_exp[:], -1.0, None, ALU.mult)


        gb_ready, gb_taken, dec_min, dec_exp, gram_ready, a_done, at_done = (
            sem(x) for x in ("gb_ready", "gb_taken", "dec_min", "dec_exp", "gram_ready", "a_done", "at_done"))
        z_ready, z_done, s_ready, s_done, ks_ready, r_done, o_ready, o_done, qe_ready, qe_done, ke_done = (
            sem(x) for x in ("z_ready", "z_done", "s_ready", "s_done", "ks_ready", "r_done", "o_ready", "o_done", "qe_ready", "qe_done", "ke_done"))
        H2 = HEADS // 2

        def heads4(bank):
            return bank[:].rearrange("p (h n) -> p h n", h=4)

        def joined(x, l, side):
            return x.rearrange("p h (n two b) -> p h n two b", two=2, b=1 << l)[:, :, :, side]

        inverses = [0, 0, 0]

        def grow_inverse(a_t, inv, inv_t, prod, nh, C, flip, slabs=None):
            even, odd = (0, 1) if flip == 0 else (1, 0)
            levels, half = C.bit_length() - 1, C // 2
            L0, Y0, X0 = inverses
            inverses[2] += 2 * (levels - 2)
            inverses[0] += 2 * levels
            inverses[1] += 2 * levels + 2
            level_cols = const("levels").rearrange("p (l f n) -> p l f n", l=LEVELS, f=2)

            def rows_of(side):
                halves = [slice(0, half), slice(half, C)] if half >= 32 else [slice(0, C)]
                return halves if side is None or half < 32 else [halves[side]]

            def by_head(bank, b=None, rows=slice(0, C)):
                v = bank[rows, 0:nh * half]
                return v.rearrange("p (h n b) -> p h n b", h=nh, b=b) if b else v.rearrange("p (h n) -> p h n", h=nh)
            with nc.Block() as block:
                @block.gpsimd
                def _(pool):
                    for l in range(levels):
                        for c in range(2):
                            if l:
                                pool.wait_ge(y_done, Y0 + 2 * l + c + 1)
                            nc.gpsimd.memset(prod[0:C, c], 0.0).then_inc(p_zero, 1)

                @block.tensor
                def _(pe):
                    def product(bank, c, lhs, rhs, done, rows):
                        for k in range(nh):
                            for m in rows:
                                mm = nc.tensor.matmul(bank[m, k * half:(k + 1) * half], lhs[0:C, c, k, m], rhs(c, k), start=True, stop=True)
                        mm.then_inc(done, 1)
                    for l in range(levels):
                        n, last = L0 + 2 * l, l == levels - 1
                        for c in range(2):
                            pe.wait_ge(y_done, Y0 + 2 * l + c + 1)
                            product(banks[c], c, a_t, lambda c, k: joined(inv[0:C, c, k:k + 1], l, even)[:, 0], p_ready, rows_of(odd) if last else rows_of(None))
                        if slabs and l:
                            pe_ada(pe, slabs[0] + l - 1, slabs[1] + l - 1, slabs[1] + l - 1, 2 * (slabs[1] + l - 1))
                        for c in range(2):
                            pe.wait_ge(p_done, n + c + 1)
                            if 0 < l < levels - 1:
                                product(banks[2 + c], c, inv_t, lambda c, k: joined(prod[0:C, c, k:k + 1], l, even)[:, 0], xu_ready, rows_of(None))
                            product(banks[4 + c], c, prod, lambda c, k: joined(inv_t[0:C, c, k:k + 1], l, odd)[:, 0], yu_ready, rows_of(even) if last else rows_of(None))
                    if slabs:
                        pe_ada(pe, slabs[0] + levels - 1, slabs[1] + levels - 1, slabs[1] + levels - 1, 2 * (slabs[1] + levels - 1))

                if slabs:
                    @block.sync
                    def _(sp):
                        load_to(sp, slabs[0] + BESIDE_GDN + RING)

                @block.vector
                def _(dve):
                    def steps_of(l, quarter):
                        if slabs:
                            r, a = slabs[0] + l, slabs[1] + l
                            dve_ada(dve, a, a, r, r, LANDED * (r // RING + 1), 2 * quarter, 2 * quarter + 2)
                    eye = ident[0:C, 0:C][:, None, :].broadcast_to([C, nh, C])
                    for c in range(2):
                        nc.vector.tensor_copy(inv[0:C, c], eye).then_inc(x_done, 1)
                        nc.vector.tensor_copy(inv_t[0:C, c], eye).then_inc(y_done, 1)
                    for l in range(levels):
                        n, b, last = L0 + 2 * l, 1 << l, l == levels - 1
                        rows_p, rows_y = (rows_of(odd)[-1], rows_of(even)[0]) if last and half >= 32 else (slice(0, C), slice(0, C))
                        for c in range(2):
                            dve.wait_ge(p_ready, n + c + 1)
                            dve.wait_ge(p_zero, n + c + 1)
                            mask = level_cols[rows_p, l, flip, 0:half].rearrange("p (n b) -> p n b", b=b)[:, None].broadcast_to([rows_p.stop - rows_p.start, nh, half // b, b])
                            nc.vector.tensor_tensor(joined(prod[rows_p, c], l, even), by_head(banks[c], b, rows_p), mask, ALU.mult).then_inc(p_done, 1)
                            steps_of(l, c)
                        for c in range(2):
                            part = joined(inv[0:C, c], l, even)
                            if l == 0:
                                dve.wait_ge(p_done, n + c + 1)
                                nc.vector.tensor_tensor(part, part, joined(prod[0:C, c], l, even), ALU.subtract).then_inc(x_done, 1)
                            elif not last:
                                dve.wait_ge(xu_ready, X0 + 2 * (l - 1) + c + 1)
                                nc.vector.tensor_tensor(part, part, by_head(banks[2 + c], b), ALU.subtract).then_inc(x_done, 1)
                            dve.wait_ge(yu_ready, n + c + 1)
                            part = joined(inv_t[rows_y, c], l, odd)
                            nc.vector.tensor_tensor(part, part, by_head(banks[4 + c], b, rows_y), ALU.subtract).then_inc(y_done, 1)
                            steps_of(l, 2 + c)
                    if slabs:
                        dve_mod(dve, 2 * slabs[1], 2 * (slabs[1] + BESIDE_GDN), slabs[1] + BESIDE_GDN)

        def gb_bank(q):
            return banks[(0, 1, 6, 7)[q]]

        def gdn_direction(d):
            tri, neg = (("upto", "neg_upto"), ("from", "neg_from"))[d]
            first = d
            D4 = 4 * d
            with nc.Block() as block:
                @block.tensor
                def _(pe):
                    for q in range(4):
                        c, hh = q // 2, H2 * (q % 2)
                        for k in range(4):
                            g = g_log[:, c, d, hh + k:hh + k + 1].broadcast_to([P, P])
                            mm = nc.tensor.matmul(gb_bank(q)[:, k * P:(k + 1) * P], g, const(tri), start=True, stop=True)
                        mm.then_inc(gb_ready, 1)
                    for q in range(4):
                        c, hh = q // 2, H2 * (q % 2)
                        if q >= 2:
                            pe.wait_ge(at_done, D4 + q - 1)
                        for k in range(4):
                            kt = qkv[:, HEADS + hh + k, c * P:(c + 1) * P]
                            qt = qkv[:, hh + k, c * P:(c + 1) * P]
                            nc.tensor.matmul(banks[2 + q % 2][:, k * P:(k + 1) * P], kt, kt, start=True, stop=True)
                            mm = nc.tensor.matmul(banks[4 + q % 2][:, k * P:(k + 1) * P], kt, qt, start=True, stop=True)
                        mm.then_inc(gram_ready, 1)

                @block.vector
                def _(dve):
                    for q in range(4):
                        c, hh = q // 2, H2 * (q % 2)
                        dve.wait_ge(gb_ready, D4 + q + 1)
                        for k in range(4):
                            ins = nc.vector.scalar_tensor_tensor(
                                out=dec_t[:, c, hh + k], in0=gb_bank(q)[:, k * P:(k + 1) * P], scalar=g_cum[:, d, c, hh + k:hh + k + 1],
                                in1=const(neg), op0=ALU.subtract, op1=ALU.add)
                        ins.then_inc(gb_taken, 1)
                    for q in range(4):
                        c, hh = q // 2, H2 * (q % 2)
                        dve.wait_ge(dec_exp, D4 + q + 1)
                        dve.wait_ge(gram_ready, D4 + q + 1)
                        for k in range(4):
                            nc.vector.scalar_tensor_tensor(
                                out=a_t[:, c, hh + k], in0=banks[2 + q % 2][:, k * P:(k + 1) * P], scalar=beta[:, c, d, hh + k:hh + k + 1],
                                in1=dec_t[:, c, hh + k], op0=ALU.mult, op1=ALU.mult)
                        nc.vector.tensor_tensor(attn_t[:, c, hh:hh + 4], heads4(banks[4 + q % 2]), dec_t[:, c, hh:hh + 4], ALU.mult).then_inc(at_done, 1)

                @block.scalar
                def _(act):
                    for q in range(4):
                        c, hh = q // 2, H2 * (q % 2)
                        act.wait_ge(gb_taken, D4 + q + 1)
                        nc.scalar.activation(dec_t[:, c, hh:hh + 4], dec_t[:, c, hh:hh + 4], ACT.Exp).then_inc(dec_exp, 1)
                        if c != first:
                            act.wait_ge(gb_ready, D4 + 4)
                            if q % 2 == 1:
                                for half in range(2):
                                    nc.scalar.activation(q_exp[:, 4 * half:4 * half + 4], heads4(gb_bank(2 * c + half)), ACT.Exp).then_inc(qe_ready, 1)

                @block.gpsimd
                def _(pool):
                    pool.wait_ge(qe_ready, 2 * (d + 1))
                    nc.gpsimd.tensor_tensor(q_exp[:], q_exp[:], qkv[:, 0:HEADS, (1 - first) * P:(2 - first) * P], ALU.mult).then_inc(qe_done, 1)

            grow_inverse(a_t, inv, inv_t, prod, HEADS, P, d, (S["gates0"].r0 + 1 + BESIDE_GDN * d, UPFRONT + BESIDE_UP + BESIDE_GDN * d))
            second = 1 - first
            with nc.Block() as block:
                @block.tensor
                def _(pe):
                    def eight(bank0, lhs, rhs, ready, start=True, stop=True):
                        for k in range(HEADS):
                            mm = nc.tensor.matmul(banks[bank0 + k // 4][:, (k % 4) * P:(k % 4 + 1) * P], lhs(k), rhs(k), start=start, stop=stop)
                            if k % 4 == 3 and ready:
                                mm.then_inc(ready, 1)
                    H = 2 * d
                    eight(0, lambda k: inv_t[:, first, k], lambda k: v_rows[:, first, k], z_ready)
                    for half in range(2):
                        pe.wait_ge(z_done, 2 * H + half + 1)
                        pe.wait_ge(ke_done, H + half + 1)
                        for k in range(4 * half, 4 * half + 4):
                            mm = nc.tensor.matmul(banks[2 + half][:, (k % 4) * P:(k % 4 + 1) * P], k_end[:, k], v_new[:, first, k], start=True, stop=True)
                        mm.then_inc(s_ready, 1)
                    for half in range(2):
                        pe.wait_ge(s_done, H + half + 1)
                        for k in range(4 * half, 4 * half + 4):
                            kt = qkv[:, HEADS + k, second * P:(second + 1) * P]
                            mm = nc.tensor.matmul(banks[4 + half][:, (k % 4) * P:(k % 4 + 1) * P], kt, state[:, k], start=True, stop=True)
                        mm.then_inc(ks_ready, 1)
                    eight(6, lambda k: v_new[:, first, k], lambda k: attn_t[:, first, k], o_ready)
                    for half in range(2):
                        pe.wait_ge(r_done, H + half + 1)
                        for k in range(4 * half, 4 * half + 4):
                            mm = nc.tensor.matmul(banks[half][:, (k % 4) * P:(k % 4 + 1) * P], inv_t[:, second, k], v_new[:, second, k], start=True, stop=True)
                        mm.then_inc(z_ready, 1)
                    for half in range(2):
                        pe.wait_ge(z_done, 2 * H + 2 + half + 1)
                        for k in range(4 * half, 4 * half + 4):
                            out = banks[2 + half][:, (k % 4) * P:(k % 4 + 1) * P]
                            nc.tensor.matmul(out, state[:, k], q_exp[:, k], start=True, stop=False)
                            mm = nc.tensor.matmul(out, v_new[:, second, k], attn_t[:, second, k], start=False, stop=True)
                        mm.then_inc(o_ready, 1)

                @block.gpsimd
                def _(pool):
                    for half in range(2):
                        hs = slice(4 * half, 4 * half + 4)
                        end = g_end[:, d, first, hs][:, :, None].broadcast_to([P, 4, P])
                        nc.gpsimd.tensor_tensor(k_end[:, hs], k_rows[:, first, hs], end, ALU.mult).then_inc(ke_done, 1)

                @block.scalar
                def _(act):
                    for half in range(2):
                        act.wait_ge(s_ready, 2 * d + half + 1)
                        nc.scalar.activation(state[:, 4 * half:4 * half + 4], heads4(banks[2 + half]), ACT.Copy).then_inc(s_done, 1)

                @block.vector
                def _(dve):
                    def betas(c, half):
                        return beta[:, c, d, 4 * half:4 * half + 4][:, :, None].broadcast_to([P, 4, P])

                    def z_to_v(c, half):
                        nc.vector.tensor_tensor(v_new[:, c, 4 * half:4 * half + 4], heads4(banks[half]), betas(c, half), ALU.mult).then_inc(z_done, 1)

                    def outputs(c, half, bank):
                        o = o_sum[:, 4 * half:4 * half + 4, c * P:(c + 1) * P]
                        if d == 0:
                            nc.vector.tensor_copy(o, heads4(bank)).then_inc(o_done, 1)
                        else:
                            nc.vector.tensor_tensor(o, o, heads4(bank), ALU.add).then_inc(o_done, 1)
                    for half in range(2):
                        dve.wait_ge(z_ready, 4 * d + half + 1)
                        z_to_v(first, half)
                    for half in range(2):
                        dve.wait_ge(ks_ready, 2 * d + half + 1)
                        for k in range(4 * half, 4 * half + 4):
                            ins = nc.vector.scalar_tensor_tensor(
                                out=v_new[:, second, k], in0=banks[4 + half][:, (k % 4) * P:(k % 4 + 1) * P],
                                scalar=g_exp[:, d, second, k:k + 1], in1=v_rows[:, second, k], op0=ALU.mult, op1=ALU.add)
                        ins.then_inc(r_done, 1)
                    for half in range(2):
                        dve.wait_ge(o_ready, 4 * d + half + 1)
                        outputs(first, half, banks[6 + half])
                    for half in range(2):
                        dve.wait_ge(z_ready, 4 * d + 2 + half + 1)
                        z_to_v(second, half)
                    for half in range(2):
                        dve.wait_ge(o_ready, 4 * d + 2 + half + 1)
                        outputs(second, half, banks[2 + half])

        gdn_direction(0)
        gdn_direction(1)
        gdn.close()

        fin = ExitStack()
        norm_ffn2 = Norm(h1, T1, *modulation("norm_ffn2", 6, 7))
        sq_f = sb("sq_f", [P, DT, T1], c=fin)
        osq = sb("osq", [P, 4, T1], c=fin)
        ort = sb("ort", [P, 4, 2, T1], c=fin)
        zt = sb("zt", [P, 2, 2, T1], c=fin)
        yb_hi = sb("yb_hi", [P, HEADS, T1], F32R, fin)
        yb_lo = sb("yb_lo", [P, HEADS, T1], F32R, fin)
        gate = sb("gate", [P, 2 * DT, T1], c=fin)
        merged = gate[:, 0:DT]
        tmp_b = sb("tmp_b", [P, 2, 2, T1], c=fin)
        on_sq, on_sum, on_ms, on_y, on_done = (sem(x) for x in ("on_sq", "on_sum", "on_ms", "on_y", "on_done"))
        z_act, yb_done, yb_h, m_done, m_h, m_l, tb_done = (sem(x) for x in ("z_act", "yb_done", "yb_h", "m_done", "m_h", "m_l", "tb_done"))
        with nc.Block() as block:
            @block.sync
            def _(sp):
                load_to(sp, S["w_out"].r0 + 4 + RING)

            @block.scalar
            def _(act):
                def sigmoid(sec, n0, u):
                    n = n0 + u
                    outputs_ready(act, sec, None, u, 0)
                    for j in range(2):
                        ins = nc.scalar.activation(gate[:, 2 * n + j], out_bank(sec, u, j)[:, 0:T1], ACT.Sigmoid)
                    ins.then_inc(act_took, 1)
                    if n < 4:
                        if n >= 2:
                            act.wait_ge(on_sum, n - 1)
                        nc.scalar.activation(osq[:, 2 * (n % 2):2 * (n % 2) + 2], o_sum[:, 2 * n:2 * n + 2], ACT.Square).then_inc(on_sq, 1)
                    if 1 <= n <= 4:
                        act.wait_ge(on_ms, n)
                        nc.scalar.activation(ort[:, 1], ort[:, 0], ACT.Abs_reciprocal_sqrt).then_inc(on_y, 1)
                for m, (n0, _) in enumerate(gate_parts):
                    sec = S[f"gates{m}"]
                    act_pairs(act, sec, lambda i, u, U: sigmoid(sec, n0, u))

                def silu_z(i, u, U):
                    outputs_ready(act, S["z"], i, u, U)
                    if u >= 2:
                        act.wait_ge(yb_done, u - 1)
                    for j in range(2):
                        ins = nc.scalar.activation(zt[:, u % 2, j], out_bank(S["z"], u, j)[:, 0:T1], ACT.Silu)
                    ins.then_inc(act_took, 1)
                act_pairs(act, S["z"], silu_z)
                act.wait_ge(yb_done, 4)
                nc.scalar.activation(yb_hi[:], o_sum[:], ACT.Copy).then_inc(yb_h, 1)
                act_pairs(act, S["a_out"], lambda i, u, U: None)

                def high(i, u, U):
                    act.wait_ge(m_done, u + 1)
                    nc.scalar.activation(x_hi[:, 2 * u:2 * u + 2, 0:T1], merged[:, 2 * u:2 * u + 2], ACT.Copy).then_inc(m_h, 1)
                act_pairs(act, S["b_out"], high)

                def square(i, u, U):
                    taken(act, S["w_out"], None, u, 0)
                    norm_ffn2.square(act, u, sq_f)
                act_pairs(act, S["w_out"], square)

            @block.tensor
            def _(pe):
                def head_sums(n):
                    if 1 <= n <= 4:
                        q = n - 1
                        pe.wait_ge(on_sq, q + 1)
                        if q >= 2:
                            pe.wait_ge(on_ms, q - 1)
                        nc.tensor.matmul(banks[4 + q % 2][:].rearrange("p (a b) -> p a b", a=2), const("ones"), osq[:, 2 * (q % 2):2 * (q % 2) + 2], start=True, stop=True).then_inc(on_sum, 1)
                for m, (n0, _) in enumerate(gate_parts):
                    pe_pairs(pe, S[f"gates{m}"], x_hi, x_lo, T1, lambda i, u, U: head_sums(n0 + u))
                pe_pairs(pe, S["z"], x_hi, x_lo, T1)
                pe_pairs(pe, S["a_out"], ya_hi, ya_lo, T1)
                pe.wait_ge(yb_h, 2)
                pe_pairs(pe, S["b_out"], yb_hi, yb_lo, T1)
                pe_pairs(pe, S["w_out"], x_hi, x_lo, T1, lambda i, u, U: norm_ffn2.total(pe, u - 1, sq_f) if u else None,
                         tile_ready=lambda k: pe.wait_ge(m_l, k // 2 + 1))
                norm_ffn2.total(pe, 3, sq_f)

            @block.vector
            def _(dve):
                def norm_pair(n):
                    if 1 <= n <= 4:
                        q = n - 1
                        dve.wait_ge(on_sum, q + 1)
                        nc.vector.tensor_scalar(ort[:, 0], banks[4 + q % 2][:].rearrange("p (a b) -> p a b", a=2), 1.0 / P, EPS, ALU.mult, ALU.add).then_inc(on_ms, 1)
                        inverse_root(dve, on_y, q + 1, ort[:, 0], ort[:, 1], ort[:, 2], ort[:, 3])
                        link(dve, "dve", nc.vector.scalar_tensor_tensor(out=o_sum[:, 2 * q:2 * q + 2], in0=o_sum[:, 2 * q:2 * q + 2],
                                                                        scalar=col("dn_norm", 0), in1=ort[:, 3], op0=ALU.mult, op1=ALU.mult))
                for m, (n0, _) in enumerate(gate_parts):
                    dve_pairs(dve, S[f"gates{m}"], lambda i, u, U: norm_pair(n0 + u))

                def times_z(i, u, U):
                    taken(dve, S["z"], None, u, 0)
                    nc.vector.tensor_tensor(o_sum[:, 2 * u:2 * u + 2], o_sum[:, 2 * u:2 * u + 2], zt[:, u % 2], ALU.mult).then_inc(yb_done, 1)
                dve_pairs(dve, S["z"], times_z)
                dve.wait_ge(yb_h, 1)
                nc.vector.tensor_tensor(yb_lo[:], o_sum[:], yb_hi[:].bitcast(F32), ALU.subtract).then_inc(yb_h, 1)

                def gated_a(i, u, U):
                    outputs_ready(dve, S["a_out"], i, u, U)
                    taken(dve, S["gates2"], None, 3, 0)
                    for j in range(2):
                        k = 2 * u + j
                        ins = nc.vector.tensor_tensor(gate[:, k], gate[:, k], out_bank(S["a_out"], u, j)[:, 0:T1], ALU.mult)
                    ins.then_inc(dve_took, 1)
                dve_pairs(dve, S["a_out"], gated_a)

                def gated_b(i, u, U):
                    outputs_ready(dve, S["b_out"], i, u, U)
                    for j in range(2):
                        k = 2 * u + j
                        ins = nc.vector.tensor_tensor(tmp_b[:, u % 2, j], gate[:, DT + k], out_bank(S["b_out"], u, j)[:, 0:T1], ALU.mult)
                    ins.then_inc(dve_took, 1)
                    taken(dve, S["b_out"], None, u, 0)
                    nc.vector.tensor_tensor(merged[:, 2 * u:2 * u + 2], merged[:, 2 * u:2 * u + 2], tmp_b[:, u % 2], ALU.add).then_inc(m_done, 1)
                    dve.wait_ge(m_h, u + 1)
                    nc.vector.tensor_tensor(x_lo[:, 2 * u:2 * u + 2, 0:T1], merged[:, 2 * u:2 * u + 2], x_hi[:, 2 * u:2 * u + 2, 0:T1].bitcast(F32), ALU.subtract).then_inc(m_l, 1)
                dve_pairs(dve, S["b_out"], gated_b)

                def residual(i, u, U):
                    outputs_ready(dve, S["w_out"], i, u, U)
                    for j in range(2):
                        k = 2 * u + j
                        ins = nc.vector.scalar_tensor_tensor(out=h1[:, k], in0=out_bank(S["w_out"], u, j)[:, 0:T1], scalar=mod[:, 40 + k:41 + k],
                                                             in1=h1[:, k], op0=ALU.mult, op1=ALU.add)
                    ins.then_inc(dve_took, 1)
                dve_pairs(dve, S["w_out"], residual)
        fin.close()
        mix.close()
        norm_final = Norm(h1, T1, lambda k: col("norm_final", k), dst=h1)
        swiglu([S["up2"]], S["down2"], 8, norm_ffn2, norm_final)

        def g_row(layer, k):
            return lambda ft: col("norm_g_2", (layer * 4 + k) * DT + ft)
        norm_in = Norm(h, T2, g_row(0, 0))
        with ExitStack() as c:
            sq = sb("sq_in", [P, DT, T2], c=c)
            with nc.Block() as block:
                @block.scalar
                def _(act):
                    norm_final.on_act(act)
                    for u in range(4):
                        norm_final.wait_scaled(act, 2 * u + 1)
                        norm_in.square(act, u, sq)

                @block.vector
                def _(dve):
                    norm_final.on_dve(dve)

                @block.tensor
                def _(pe):
                    for u in range(4):
                        norm_in.total(pe, u, sq)

        end_of_stage()
        rw = ExitStack()
        Y = sb("Y", [P, SHIFTED + 4, T2 + 1], c=rw)
        ys = Y[:, :, 1:T2 + 1]
        r_t, k_t, v_t = ys[:, 0:4], ys[:, 4:8], ys[:, 8:12]
        pool_u = ys[:, 14:18]
        log_w = sb("log_w", [P, RW, T2], c=rw)
        log_g = sb("log_g", [P, RW, T2], c=rw)
        nb_t = sb("nb_t", [P, RW, T2], c=rw)
        gate_t = sb("gate_t", [P, RW, T2], c=rw)
        kk_t = sb("kk_t", [P, RW, T2], c=rw)
        e1 = sb("e1", [P, RW, T2], c=rw)
        v_rw = sb("v_rw", [P, 3, 512], c=rw)
        g_fin = sb("g_fin", [P, RW, 5], c=rw)
        state_bd = sb("state_bd", [P, RW, P], c=rw)
        o_rows = sb("o_rows", [P, 3, 512], c=rw)
        pre = ExitStack()
        mid_e = sb("mid_e", [P, DT, T2], c=pre)
        w_up = sb("w_up", [P, 512], c=pre)
        g_up = sb("g_up", [P, 512], c=pre)
        low = sb("low", [P, 2, T2], c=pre)
        shift = sb("shift", [P, 2, 2, T2], c=pre)
        reset = sb("reset", [P, RW, T2], c=pre)
        e2 = sb("e2", [P, RW, T2], c=pre)
        e3 = sb("e3", [P, RW, T2], c=pre)
        names = ("ev_small", "y_zero", "sh_sub", "sh_done", "lo_act", "lo_mm", "lo_out", "a_mm", "a_out", "g_mm", "g_out",
                 "kk_sq", "kk_sum", "kk_ms", "kk_y", "kk_ok", "bon", "bon_mm", "vr_mm", "vr_out", "ex", "ex_done", "reset_ok")
        q = {n: sem(n) for n in names}
        with nc.Block() as block:
            @block.sync
            def _(sp):
                sp.dma_start(w_up[0:64], t["ev_w_up_2"][0]).then_inc(q["ev_small"], 16)
                sp.dma_start(w_up[64:P], t["ev_a_up_2"][0]).then_inc(q["ev_small"], 16)
                sp.dma_start(g_up[:], t["ev_g_up_2"][0]).then_inc(q["ev_small"], 16)
                load_to(sp, S["ev_u"].r0 + 2 + RING)

            @block.scalar
            def _(act):
                def copy(sec, first):
                    def take(i, u, U):
                        outputs_ready(act, sec, i, u, U)
                        for j in range(2):
                            k = first + 2 * u + j
                            ins = nc.scalar.activation(ys[:, k], out_bank(sec, u, j)[:, 0:T2], ACT.Copy)
                        ins.then_inc(act_took, 1)
                    return take
                norm_in.on_act(act, mid_e, lambda: split_hi_ahead(act, S["ev_s"]))
                act.wait_ge(q["y_zero"], 1)
                act_pairs(act, S["ev_s"], copy(S["ev_s"], 0), ahead=True)
                act_pairs(act, S["ev_u"], copy(S["ev_u"], SHIFTED))
                act.wait_ge(q["sh_done"], 7)
                nc.scalar.activation(low[0:64, 0], ys[0:64, 12], ACT.Tanh)
                nc.scalar.activation(low[64:P, 0], ys[64:P, 12], ACT.Copy)
                nc.scalar.activation(low[:, 1], ys[:, 13], ACT.Sigmoid).then_inc(q["lo_act"], 1)
                for k in range(RW):
                    act.wait_ge(q["lo_mm"], k + 1)
                    nc.scalar.activation(log_w[:, k], banks[k][:, 0:T2], ACT.Sigmoid, bias=col("ev_w0_2", k)).then_inc(q["lo_out"], 1)
                for k in range(RW):
                    act.wait_ge(q["a_mm"], k + 1)
                    nc.scalar.activation(nb_t[:, k], banks[4 + k][:, 0:T2], ACT.Sigmoid, bias=col("ev_a0_2", k)).then_inc(q["a_out"], 1)
                for k in range(RW):
                    act.wait_ge(q["g_mm"], k + 1)
                    nc.scalar.activation(gate_t[:, k], banks[k][:, 0:T2], ACT.Copy).then_inc(q["g_out"], 1)
                act.wait_ge(q["kk_ok"], 1)
                nc.scalar.activation(e1[:], kk_t[:], ACT.Square).then_inc(q["kk_sq"], 1)
                act.wait_ge(q["ex"], 1)
                nc.scalar.activation(g_fin[:], g_fin[:], ACT.Exp)
                nc.scalar.activation(reset[:], log_g[:], ACT.Exp, scale=-1.0).then_inc(q["ex_done"], 1)
                act.wait_ge(q["ex_done"], 1)
                nc.scalar.activation(log_g[:], log_g[:], ACT.Exp).then_inc(q["ex_done"], 1)
                nc.scalar.activation(log_w[:], log_w[:], ACT.Exp).then_inc(q["ex_done"], 1)
                act.wait_ge(q["kk_ms"], 1)
                nc.scalar.activation(e2[:], e1[:], ACT.Abs_reciprocal_sqrt).then_inc(q["kk_y"], 1)
                for c in range(3):
                    act.wait_ge(q["vr_mm"], c + 1)
                    C = min(P, T2 - c * P)
                    nc.scalar.activation(v_rw[0:C, c], banks[c][0:C], ACT.Copy).then_inc(q["vr_out"], 1)

            @block.vector
            def _(dve):
                nc.vector.memset(Y[:, :, 0:1], 0.0).then_inc(q["y_zero"], 1)
                link(dve, "dve", nc.vector.memset(reset[:], 1.0))
                nc.vector.memset(reset[:, :, 0:T2:64], 0.0).then_inc(q["reset_ok"], 1)
                norm_in.on_dve(dve, mid_e)
                dve.wait_ge(q["y_zero"], 1)

                def shifted(i, u, U):
                    b = u % 2
                    taken(dve, S["ev_s"], None, u, 0)
                    link(dve, "dve", nc.vector.tensor_tensor(shift[:, b], Y[:, 2 * u:2 * u + 2, 0:T2], ys[:, 2 * u:2 * u + 2], ALU.subtract))
                    for j in range(2):
                        k = 2 * u + j
                        ins = nc.vector.scalar_tensor_tensor(out=ys[:, k], in0=shift[:, b, j], scalar=col("ev_mu_2", k), in1=ys[:, k],
                                                             op0=ALU.mult, op1=ALU.add)
                    ins.then_inc(q["sh_done"], 1)
                dve_pairs(dve, S["ev_s"], shifted)
                dve_pairs(dve, S["ev_u"], lambda i, u, U: None)
                dve.wait_ge(q["sh_done"], 7)
                for k in range(RW):
                    ins = nc.vector.tensor_scalar(kk_t[:, k], k_t[:, k], col("ev_k_k_2", k), None, ALU.mult)
                ins.then_inc(q["kk_ok"], 1)
                dve.wait_ge(q["lo_out"], 4)
                link(dve, "dve", nc.vector.tensor_scalar(log_w[:], log_w[:], -float(np.exp(-0.5)), None, ALU.mult))
                dve.wait_ge(q["reset_ok"], 1)
                flat = lambda x: x[:].rearrange("p a b -> p (a b)")
                link(dve, "dve", nc.vector.tensor_tensor_scan(flat(log_g), flat(reset), flat(log_w), 0.0, ALU.mult, ALU.add))
                nc.vector.tensor_copy(g_fin[:, :, 0:4], log_g[:, :, 63:T2:64])
                nc.vector.tensor_copy(g_fin[:, :, 4:5], log_g[:, :, T2 - 1:T2])
                nc.vector.tensor_tensor(log_w[:], log_g[:], log_w[:], ALU.subtract).then_inc(q["ex"], 1)
                dve.wait_ge(q["a_out"], 4)
                for k in range(RW):
                    ins = nc.vector.tensor_scalar(e3[:, k], nb_t[:, k], -1.0, col("ev_k_a_2", k), ALU.add, ALU.mult)
                link(dve, "dve", ins)
                link(dve, "dve", nc.vector.scalar_tensor_tensor(out=k_t, in0=e3[:], scalar=1.0, in1=k_t, op0=ALU.add, op1=ALU.mult))
                for k in range(RW):
                    dve.wait_ge(q["kk_sum"], k + 1)
                    ins = nc.vector.tensor_scalar(e1[:, k], banks[4 + k][:, 0:T2], 1e-24, None, ALU.max)
                ins.then_inc(q["kk_ms"], 1)
                inverse_root(dve, q["kk_y"], 1, e1[:], e2[:], e3[:], e3[:])
                link(dve, "dve", nc.vector.tensor_tensor(kk_t[:], kk_t[:], e3[:], ALU.mult))
                link(dve, "dve", nc.vector.scalar_tensor_tensor(out=nb_t[:], in0=kk_t[:], scalar=-1.0, in1=nb_t[:], op0=ALU.mult, op1=ALU.mult))
                for k in range(RW):
                    ins = nc.vector.scalar_tensor_tensor(out=e3[:, k], in0=r_t[:, k], scalar=col("ev_r_k_2", k), in1=k_t[:, k], op0=ALU.mult, op1=ALU.mult)
                ins.then_inc(q["bon"], 1)
                dve.wait_ge(q["ex_done"], 3)
                nc.vector.tensor_tensor(kk_t[:], kk_t[:], log_w[:], ALU.mult)
                nc.vector.tensor_tensor(nb_t[:], nb_t[:], reset[:], ALU.mult)
                dve.wait_ge(q["bon"], 1)
                nc.vector.tensor_tensor(r_t, r_t, log_g[:], ALU.mult)
                dve.wait_ge(q["vr_mm"], 3)
                for k in range(RW):
                    dve.wait_ge(q["bon_mm"], k + 1)
                    nc.vector.tensor_tensor(v_t[:, k], v_t[:, k], banks[4 + k][:, 0:T2], ALU.mult)

            @block.gpsimd
            def _(pool):
                pool.wait_ge(q["bon"], 1)
                pool.wait_ge(q["ex_done"], 1)
                nc.gpsimd.tensor_tensor(k_t, k_t, reset[:], ALU.mult)

            @block.tensor
            def _(pe):
                pe_pairs(pe, S["ev_s"], x_hi, x_lo, T2, norm=norm_in)
                pe_pairs(pe, S["ev_u"], x_hi, x_lo, T2)
                pe.wait_ge(q["ev_small"], 48)
                pe.wait_ge(q["lo_act"], 1)
                taken(pe, S["ev_u"], None, 1, 0)
                for k in range(RW):
                    nc.tensor.matmul(banks[k][:, 0:T2], w_up[0:64, k * P:(k + 1) * P], low[0:64, 0], start=True, stop=True).then_inc(q["lo_mm"], 1)
                for k in range(RW):
                    nc.tensor.matmul(banks[4 + k][:, 0:T2], w_up[64:P, k * P:(k + 1) * P], low[64:P, 0], start=True, stop=True).then_inc(q["a_mm"], 1)
                for k in range(RW):
                    pe.wait_ge(q["lo_out"], k + 1)
                    nc.tensor.matmul(banks[k][:, 0:T2], g_up[:, k * P:(k + 1) * P], low[:, 1], start=True, stop=True).then_inc(q["g_mm"], 1)
                pe.wait_ge(q["kk_sq"], 1)
                for k in range(RW):
                    pe.wait_ge(q["a_out"], k + 1)
                    nc.tensor.matmul(banks[4 + k][:, 0:T2], const("halves"), e1[:, k], start=True, stop=True).then_inc(q["kk_sum"], 1)
                pe.wait_ge(q["g_out"], 4)
                for c in range(3):
                    C = min(P, T2 - c * P)
                    for k in range(RW):
                        mm = nc.tensor.transpose(banks[c][0:C, k * P:(k + 1) * P], v_t[:, k, c * P:c * P + C], ident)
                    mm.then_inc(q["vr_mm"], 1)
                pe.wait_ge(q["bon"], 1)
                for k in range(RW):
                    nc.tensor.matmul(banks[4 + k][:, 0:T2], const("halves"), e3[:, k], start=True, stop=True).then_inc(q["bon_mm"], 1)
        pre.close()

        ch = ExitStack()
        rb_at, ak_t, rb_t, rk_t, rinv, rinv_t, rprod = (sb(n, [P, 2, RW, P], c=ch) for n in ("rb_at", "ak_t", "rb_t", "rk_t", "rinv", "rinv_t", "rprod"))
        hats = sb("hats", [P, 2, RW, 64], c=ch)
        rows_kb = sb("rows_kb", [P, 2, 512], c=ch)
        rhs_r = sb("rhs_r", [P, 512], c=ch)
        w_r = sb("w_r", [P, 512], c=ch)
        w_end = sb("w_end", [P, RW, 1], c=ch)
        names = ("hat", "gr", "gr_out", "gr_act", "hat2", "kb_mm", "kb_out", "rr", "rr_out", "ww", "ww_out", "oo", "oo_out", "st", "st_out", "bd0")
        m = {n: sem("c_" + n) for n in names}

        def rwkv_chunk(c):
            C = min(P, T2 - c * P)
            cols, c0, c1 = slice(c * P, c * P + C), slice(c * P, c * P + 64), slice(c * P + 64, c * P + P)
            two = C == P
            f_a, f_b = (g_fin[:, :, min(2 * c + x, 4):min(2 * c + x, 4) + 1] for x in range(2))
            pairs = [(nb_t, kk_t), (k_t, kk_t), (nb_t, r_t), (k_t, r_t)]
            with nc.Block() as block:
                @block.gpsimd
                def _(pool):
                    if two:
                        nc.gpsimd.tensor_tensor(hats[:, 0], nb_t[:, :, c0], f_a.broadcast_to([P, RW, 64]), ALU.mult)
                        nc.gpsimd.tensor_tensor(hats[:, 1], k_t[:, :, c0], f_a.broadcast_to([P, RW, 64]), ALU.mult).then_inc(m["hat"], 1)

                @block.tensor
                def _(pe):
                    def whole(x):
                        left, right = pairs[x]
                        for par in range(2):
                            ps = slice(64 * par, 64 * par + 64)
                            for k in range(RW):
                                mm = nc.tensor.matmul(banks[2 * x + par][0:C, k * P:k * P + C], left[ps, k, cols], right[ps, k, cols], start=True, stop=True)
                            if not two:
                                mm.then_inc(m["gr"], 1)

                    def across(x):
                        if not two:
                            return
                        pe.wait_ge(m["hat"], c + 1)
                        for par in range(2):
                            ps = slice(64 * par, 64 * par + 64)
                            for k in range(RW):
                                mm = nc.tensor.matmul(banks[2 * x + par][0:64, k * P + 64:k * P + P], hats[ps, x % 2, k], pairs[x][1][ps, k, c1], start=True, stop=True)
                            mm.then_inc(m["gr"], 1)
                    whole(0)
                    whole(1)
                    across(0)
                    whole(2)
                    across(1)
                    whole(3)
                    across(2)
                    across(3)

                @block.scalar
                def _(act):
                    for par in range(2):
                        act.wait_ge(m["gr"], 8 * c + par + 1)
                        nc.scalar.activation(rb_at[0:C, par, :, 0:C], heads4(banks[par])[0:C, :, 0:C], ACT.Copy, scale=-1.0).then_inc(m["gr_act"], 1)

                @block.vector
                def _(dve):
                    for x, (dst, mask) in enumerate(((ak_t, "before"), (rb_t, "upto"), (rk_t, "upto"))):
                        for par in range(2):
                            dve.wait_ge(m["gr"], 8 * c + 2 * x + 2 + par + 1)
                            nc.vector.tensor_tensor(dst[0:C, par, :, 0:C], heads4(banks[2 * x + 2 + par])[0:C, :, 0:C],
                                                    const(mask)[0:C, 0:C][:, None, :].broadcast_to([C, RW, C]), ALU.mult).then_inc(m["gr_out"], 1)
            grow_inverse(rb_at[:, :, :, 0:C], rinv[:, :, :, 0:C], rinv_t[:, :, :, 0:C], rprod[:, :, :, 0:C], RW, C, 0)
            has_state, makes_state = c > 0, c < 2
            with nc.Block() as block:
                @block.vector
                def _(dve):
                    if two:
                        fb = f_b.broadcast_to([P, RW, 64])
                        fa = f_a.broadcast_to([P, RW, 64])
                        if has_state:
                            for x in (kk_t[:], r_t):
                                nc.vector.tensor_tensor(x[:, :, c1], x[:, :, c1], fa, ALU.mult)
                        nc.vector.tensor_tensor(w_end[:], f_a, f_b, ALU.mult)
                        for n, x in enumerate((nb_t[:], k_t)):
                            nc.vector.tensor_tensor(x[:, :, c0], hats[:, n], fb, ALU.mult)
                            ins = nc.vector.tensor_tensor(x[:, :, c1], x[:, :, c1], fb, ALU.mult)
                        ins.then_inc(m["hat2"], 1)
                        if c == 0:
                            nc.vector.memset(state_bd[:], 0.0).then_inc(m["bd0"], 1)
                            dve.wait_ge(m["bd0"], 1)
                    dve.wait_ge(m["rr"], c + 1)
                    nc.vector.tensor_copy(rhs_r[0:C], banks[0][0:C]).then_inc(m["rr_out"], 1)
                    dve.wait_ge(m["ww"], c + 1)
                    nc.vector.tensor_copy(w_r[0:C], banks[1][0:C]).then_inc(m["ww_out"], 1)
                    if makes_state:
                        dve.wait_ge(m["st"], c + 1)
                        dve.wait_ge(m["oo"], c + 1)
                        for par in range(2):
                            ps = slice(64 * par, 64 * par + 64)
                            s = state_bd[ps, :, ps]
                            new = heads4(banks[3])[ps, :, ps]
                            if c:
                                link(dve, "dve", nc.vector.tensor_tensor(s, s, w_end[ps].broadcast_to([64, RW, 64]), ALU.mult))
                                link(dve, "dve", nc.vector.tensor_tensor(s, s, new, ALU.add))
                            else:
                                link(dve, "dve", nc.vector.tensor_copy(s, new))

                @block.scalar
                def _(act):
                    if makes_state:
                        for n in range(2):
                            act.wait_ge(m["kb_mm"], 2 * c + n + 1)
                            nc.scalar.activation(rows_kb[:, n], banks[4 + n][:], ACT.Copy).then_inc(m["kb_out"], 1)
                    act.wait_ge(m["oo"], c + 1)
                    nc.scalar.activation(o_rows[0:C, c], banks[2][0:C], ACT.Copy).then_inc(m["oo_out"], 1)

                @block.tensor
                def _(pe):
                    if has_state and two:
                        pe.wait_ge(m["hat2"], c + 1)
                    def head(x, k, par):
                        return x[0:C, par, k, 0:C]
                    def of(x, k, par):
                        return x[0:C, k * P + 64 * par:k * P + 64 * par + 64]
                    for k in range(RW):
                        if has_state:
                            nc.tensor.matmul(banks[0][0:C, k * P:(k + 1) * P], kk_t[:, k, cols], state_bd[:, k], start=True, stop=False, skip_group_check=True)
                        for par in range(2):
                            mm = nc.tensor.matmul(of(banks[0], k, par), head(ak_t, k, par), of(v_rw[:, c], k, par), start=not has_state, stop=True, skip_group_check=True)
                    mm.then_inc(m["rr"], 1)
                    if makes_state:
                        pe.wait_ge(m["hat2"], c + 1)
                        for n, x in enumerate((nb_t, k_t)):
                            for k in range(RW):
                                mm = nc.tensor.transpose(banks[4 + n][:, k * P:(k + 1) * P], x[:, k, cols], ident)
                            mm.then_inc(m["kb_mm"], 1)
                    pe.wait_ge(m["rr_out"], c + 1)
                    for k in range(RW):
                        for par in range(2):
                            mm = nc.tensor.matmul(of(banks[1], k, par), head(rinv_t, k, par), of(rhs_r, k, par), start=True, stop=True)
                    mm.then_inc(m["ww"], 1)
                    pe.wait_ge(m["ww_out"], c + 1)
                    if makes_state:
                        pe.wait_ge(m["kb_out"], 2 * c + 2)
                        for k in range(RW):
                            ks = slice(k * P, (k + 1) * P)
                            nc.tensor.matmul(banks[3][:, ks], rows_kb[:, 0, ks], w_r[:, ks], start=True, stop=False)
                            mm = nc.tensor.matmul(banks[3][:, ks], rows_kb[:, 1, ks], v_rw[:, c, ks], start=False, stop=True)
                        mm.then_inc(m["st"], 1)
                    for k in range(RW):
                        if has_state:
                            nc.tensor.matmul(banks[2][0:C, k * P:(k + 1) * P], r_t[:, k, cols], state_bd[:, k], start=True, stop=False, skip_group_check=True)
                        for par in range(2):
                            nc.tensor.matmul(of(banks[2], k, par), head(rb_t, k, par), of(w_r, k, par), start=not has_state, stop=False, skip_group_check=True)
                            mm = nc.tensor.matmul(of(banks[2], k, par), head(rk_t, k, par), of(v_rw[:, c], k, par), start=False, stop=True, skip_group_check=True)
                    mm.then_inc(m["oo"], 1)

        for c in range(3):
            rwkv_chunk(c)
        ch.close()

        po = ExitStack()
        dev = sb("dev", [P, 3, 512], c=po)
        dev2 = sb("dev2", [P, 3, 512], c=po)
        gn = sb("gn", [P, 6, 3, HEADS], c=po)
        sum_a, sum_b, diff = (sb(n, [P, 4, T2], c=po) for n in ("sum_a", "sum_b", "diff"))
        head16 = sb("head16", [P, 4, 16], c=po)
        pool_w = sb("pool_w", [P, 4, P], c=po)
        cat = sb("cat", [P, DT, T2], c=po)
        names = ("pw", "d2", "ms", "y", "nrm", "tr", "o_done", "pl", "pl_mm", "cat_h", "cat_l", "z_done")
        g = {n: sem("g_" + n) for n in names}
        heads8 = lambda x: x.rearrange("p (h n) -> p h n", h=HEADS)
        with nc.Block() as block:
            @block.sync
            def _(sp):
                sp.dma_start(pool_w[:], t["ev_pool_w_2"][0].rearrange("g c d -> c g d")).then_inc(g["pw"], 16)

            @block.scalar
            def _(act):
                for c in range(3):
                    C = min(P, T2 - c * P)
                    act.wait_ge(g["d2"], c + 1)
                    nc.scalar.activation(dev2[0:C, c], dev[0:C, c], ACT.Square).then_inc(g["y"], 1)
                for c in range(3):
                    C = min(P, T2 - c * P)
                    act.wait_ge(g["ms"], c + 1)
                    nc.scalar.activation(gn[0:C, 3, c], gn[0:C, 2, c], ACT.Abs_reciprocal_sqrt).then_inc(g["y"], 1)
                for k in range(4):
                    act.wait_ge(g["pl_mm"], k + 1)
                    nc.scalar.activation(cat[:, 4 + k], banks[4 + k][:, 0:T2], ACT.Identity, scale=col("ev_pool_scale_2", k)).then_inc(g["z_done"], 1)
                act.wait_ge(g["z_done"], 4)
                nc.scalar.activation(x_hi[:, 4:8], cat[:, 4:8], ACT.Copy).then_inc(g["cat_h"], 1)
                act.wait_ge(g["o_done"], 1)
                nc.scalar.activation(x_hi[:, 0:4], cat[:, 0:4], ACT.Copy).then_inc(g["cat_h"], 1)

            @block.vector
            def _(dve):
                for c in range(3):
                    C = min(P, T2 - c * P)
                    link(dve, "dve", nc.vector.reduce_sum(gn[0:C, 0, c], heads8(o_rows[0:C, c]), AX.X))
                    link(dve, "dve", nc.vector.tensor_scalar(gn[0:C, 0, c], gn[0:C, 0, c], 1.0 / 64, None, ALU.mult))
                    mean = gn[0:C, 0, c][:, :, None].broadcast_to([C, HEADS, 64])
                    nc.vector.tensor_tensor(heads8(dev[0:C, c]), heads8(o_rows[0:C, c]), mean, ALU.subtract).then_inc(g["d2"], 1)
                u = pool_u
                nc.vector.tensor_copy(sum_a[:, :, 0:1], u[:, :, 0:1])
                link(dve, "dve", nc.vector.tensor_tensor(sum_a[:, :, 1:T2], u[:, :, 1:T2], u[:, :, 0:T2 - 1], ALU.add))
                nc.vector.tensor_copy(sum_b[:, 1:4, 0:2], sum_a[:, 1:4, 0:2])
                link(dve, "dve", nc.vector.tensor_tensor(sum_b[:, 1:4, 2:T2], sum_a[:, 1:4, 2:T2], sum_a[:, 1:4, 0:T2 - 2], ALU.add))
                nc.vector.tensor_copy(sum_a[:, 2:4, 0:4], sum_b[:, 2:4, 0:4])
                link(dve, "dve", nc.vector.tensor_tensor(sum_a[:, 2:4, 4:T2], sum_b[:, 2:4, 4:T2], sum_b[:, 2:4, 0:T2 - 4], ALU.add))
                nc.vector.tensor_copy(sum_b[:, 3:4, 0:8], sum_a[:, 3:4, 0:8])
                link(dve, "dve", nc.vector.tensor_tensor(sum_b[:, 3:4, 8:T2], sum_a[:, 3:4, 8:T2], sum_a[:, 3:4, 0:T2 - 8], ALU.add))
                counts = const("counts").rearrange("p (g n) -> p g n", g=4)
                sums = (sum_a, sum_b, sum_a, sum_b)
                for k, win in enumerate(WINDOWS):
                    nc.vector.tensor_tensor(head16[:, k], sums[k][:, k, 0:16], counts[:, k], ALU.mult)
                    ins = nc.vector.scalar_tensor_tensor(out=diff[:, k], in0=sums[k][:, k], scalar=1.0 / win, in1=u[:, k], op0=ALU.mult, op1=ALU.subtract)
                link(dve, "dve", ins)
                nc.vector.tensor_tensor(diff[:, :, 0:16], head16[:], u[:, :, 0:16], ALU.subtract).then_inc(g["pl"], 1)
                for c in range(3):
                    C = min(P, T2 - c * P)
                    dve.wait_ge(g["y"], c + 1)
                    link(dve, "dve", nc.vector.reduce_sum(gn[0:C, 1, c], heads8(dev2[0:C, c]), AX.X))
                    nc.vector.tensor_scalar(gn[0:C, 2, c], gn[0:C, 1, c], 1.0 / 64, GN_EPS, ALU.mult, ALU.add).then_inc(g["ms"], 1)
                for c in range(3):
                    C = min(P, T2 - c * P)
                    inverse_root(dve, g["y"], 3 + c + 1, gn[0:C, 2, c], gn[0:C, 3, c], gn[0:C, 4, c], gn[0:C, 5, c])
                    rstd = gn[0:C, 5, c][:, :, None].broadcast_to([C, HEADS, 64])
                    nc.vector.tensor_tensor(heads8(dev[0:C, c]), heads8(dev[0:C, c]), rstd, ALU.mult).then_inc(g["nrm"], 1)
                dve.wait_ge(g["tr"], 1)
                for k in range(RW):
                    ins = nc.vector.tensor_scalar(cat[:, k], banks[k][:, 0:T2], col("ev_ln_w_2", k), col("ev_ln_b_2", k), ALU.mult, ALU.add)
                link(dve, "dve", ins)
                link(dve, "dve", nc.vector.tensor_tensor(cat[:, 0:4], cat[:, 0:4], v_t, ALU.add))
                nc.vector.tensor_tensor(cat[:, 0:4], cat[:, 0:4], gate_t[:], ALU.mult).then_inc(g["o_done"], 1)
                for n, half in enumerate((slice(4, 8), slice(0, 4))):
                    dve.wait_ge(g["cat_h"], n + 1)
                    if n:
                        dve.wait_ge(g["o_done"], 1)
                    nc.vector.tensor_tensor(x_lo[:, half], cat[:, half], x_hi[:, half].bitcast(F32), ALU.subtract).then_inc(g["cat_l"], 1)

            @block.tensor
            def _(pe):
                pe.wait_ge(g["pw"], 16)
                pe.wait_ge(g["pl"], 1)
                for k in range(4):
                    nc.tensor.matmul(banks[4 + k][:, 0:T2], pool_w[:, k], diff[:, k], start=True, stop=True).then_inc(g["pl_mm"], 1)
                for c in range(3):
                    C = min(P, T2 - c * P)
                    pe.wait_ge(g["nrm"], c + 1)
                    for k in range(RW):
                        mm = nc.tensor.transpose(banks[k][:, c * P:c * P + C], dev[0:C, c, k * P:(k + 1) * P], ident[0:C, 0:C])
                mm.then_inc(g["tr"], 1)
        po.close()
        rw.close()

        def plain(sec, xh, xl, dst, before=None, norm=None, then=None):
            with ExitStack() as c, nc.Block() as block:
                uid[0] += 1
                tile = lambda name: sb(f"{name}{uid[0]}", [P, DT, T2], c=c)
                mid = tile("mid") if before or norm else None
                sq = tile("sq") if norm else None

                @block.sync
                def _(sp):
                    load_to(sp, sec.r0 + sec.pairs * sec.g + RING)

                @block.scalar
                def _(act):
                    if before:
                        before.on_act(act, mid, lambda: split_hi_ahead(act, sec))

                    def take(i, u, U):
                        outputs_ready(act, sec, i, u, U)
                        for j in range(2):
                            d = dst[:, 2 * u + j] if i is None else dst[:, bass.ds(i * (2 * U) + (2 * u + j), 1)]
                            b = out_bank(sec, u, j)
                            ins = nc.scalar.activation(d, b[:, 0:T2] if i is None else b[:, None, 0:T2], ACT.Copy)
                        ins.then_inc(act_took, 1)
                        if norm:
                            taken(act, sec, None, u, 0)
                            norm.square(act, u, sq)
                    act_pairs(act, sec, take, ahead=before is not None)
                    if norm:
                        norm.on_act(act)
                    if then:
                        for u in range(4):
                            norm.wait_tile(act, 2 * u + 1)
                            then.square(act, u, sq)

                @block.vector
                def _(dve):
                    if before:
                        before.on_dve(dve, mid)
                    dve_pairs(dve, sec, lambda i, u, U: None)
                    if norm:
                        norm.on_dve(dve, mid)

                @block.tensor
                def _(pe):
                    pe_pairs(pe, sec, xh, xl, T2, (lambda i, u, U: norm.total(pe, u - 1, sq) if u else None) if norm else None, before)
                    if norm:
                        norm.total(pe, 3, sq)
                    if then:
                        for u in range(4):
                            then.total(pe, u, sq)

        def mixer_out(sec, layer, tag):
            with ExitStack() as c:
                out = sb(f"mixed{tag}", [P, DT, T2], c=c)
                norm, then = Norm(out, T2, g_row(layer, 1), add_to=h), Norm(h, T2, g_row(layer, 2))
                plain(sec, x_hi, x_lo, out, norm=norm, then=then)
            return then

        def mlp(up, down, layer, before, make_then):
            whole = ExitStack()
            out = sb(f"down_out{layer}", [P, DT, T2], c=whole)
            norm = Norm(out, T2, g_row(layer, 3), add_to=h)
            then = make_then()
            with ExitStack() as c:
                hid_hi = sb(f"mh_hi{layer}", [P, FF2T, T2], F32R, c)
                hid_lo = sb(f"mh_lo{layer}", [P, FF2T, T2], F32R, c)
                in_up = ExitStack()
                relu = sb(f"relu{layer}", [P, 2, 2, T2], c=in_up)
                sq = sb(f"relu2{layer}", [P, 2, 2, T2], c=in_up)
                mid = sb(f"mid_up{layer}", [P, DT, T2], c=in_up)
                s_sq, s_hi, s_lo = (sem(f"{x}{layer}") for x in ("mlp_sq", "mlp_hi", "mlp_lo"))
                with nc.Block() as block:
                    @block.sync
                    def _(sp):
                        load_to(sp, up.r0 + up.pairs + RING)

                    @block.scalar
                    def _(act):
                        def take(i, u, U):
                            b, n = u % 2, at(i, U, u)
                            outputs_ready(act, up, i, u, U)
                            for j in range(2):
                                ins = nc.scalar.activation(relu[:, b, j], out_bank(up, u, j)[:, 0:T2], ACT.Relu)
                            ins.then_inc(act_took, 1)
                            taken(act, up, i, u, U)
                            act.wait_ge(s_lo, n + 1)
                            nc.scalar.activation(sq[:, b], relu[:, b], ACT.Square).then_inc(s_sq, 1)
                            act.wait_ge(s_sq, n + 1)
                            nc.scalar.activation(hid_hi[:, bass.ds(n * 2, 2)], sq[:, b], ACT.Copy).then_inc(s_hi, 1)
                        before.on_act(act, mid, lambda: split_hi_ahead(act, up))
                        act_pairs(act, up, take, ahead=True)

                    @block.vector
                    def _(dve):
                        dve.sem_inc(s_lo, 2)
                        before.on_dve(dve, mid)

                        def low_part(i, u, U):
                            b, n = u % 2, at(i, U, u)
                            dve.wait_ge(s_hi, n + 1)
                            nc.vector.tensor_tensor(hid_lo[:, bass.ds(n * 2, 2)], sq[:, b], hid_hi[:, bass.ds(n * 2, 2)].bitcast(F32), ALU.subtract).then_inc(s_lo, 1)
                        dve_pairs(dve, up, low_part)

                    @block.tensor
                    def _(pe):
                        pe_pairs(pe, up, x_hi, x_lo, T2, norm=before)
                in_up.close()
                plain(down, hid_hi, hid_lo, out, norm=norm, then=then)
            whole.close()
            return then

        before_mlp = mixer_out(S["ev_out"], 0, "0")
        before_attention = mlp(S["mlp1_0"], S["mlp2_0"], 0, before_mlp, lambda: Norm(h, T2, g_row(1, 0)))

        end_of_stage()
        LAM_INIT = float(0.8 - 0.6 * np.exp(-0.3))
        at_ = ExitStack()
        yq = sb("yq", [P, 3 * HEADS, T2], c=at_)
        plain(S["od_in"], x_hi, x_lo, yq, before=before_attention)
        turning = sb("turning", [P, P + 2 * T2], c=at_)
        rotate, cos_t, sin_t = turning[:, 0:P], turning[:, P:P + T2], turning[:, P + T2:P + 2 * T2]
        o_at = sb("o_at", [P, HEADS, T2], c=at_)
        v_at = sb("v_at", [P, 3, HEADS, P], c=at_)
        rot_a = sb("rot_a", [P, 2, T2], c=at_)
        lam_row = sb("lam_row", [1, 4, 64], c=at_)
        lam_p = sb("lam_p", [1, 2, 64], c=at_)
        lam_s = sb("lam_s", [1, 4], c=at_)
        lam = sb("lam", [P, 1], c=at_)
        names = ("turn", "lam", "lam_x", "lam_e", "lam_mm", "rot", "rot_a", "rot_d", "vr", "vr_out")
        a = {n: sem("a_" + n) for n in names}
        with nc.Block() as block:
            @block.sync
            def _(sp):
                sp.dma_start(lam_row[:], t["od_lambda_2"]).then_inc(a["lam"], 16)
                sp.dma_start(turning[:], t["turning"]).then_inc(a["turn"], 16)

            @block.tensor
            def _(pe):
                pe.wait_ge(a["turn"], 16)
                for k in range(2 * HEADS):
                    if k >= 4:
                        pe.wait_ge(a["rot_d"], k - 3)
                    nc.tensor.matmul(banks[k % 4][:, 0:T2], rotate, yq[:, k], start=True, stop=True).then_inc(a["rot"], 1)
                for n in range(6):
                    c, half = n // 2, n % 2
                    C = min(P, T2 - c * P)
                    if n >= 2:
                        pe.wait_ge(a["vr_out"], n - 1)
                    for k in range(4):
                        mm = nc.tensor.transpose(banks[4 + n % 2][0:C, k * P:(k + 1) * P], yq[:, 16 + 4 * half + k, c * P:c * P + C], ident)
                    mm.then_inc(a["vr"], 1)
                pe.wait_ge(a["lam_x"], 2)
                nc.tensor.matmul(banks[6][:, 0:1], const("ones")[0:1], lam_s[0:1, 3:4], start=True, stop=True).then_inc(a["lam_mm"], 1)

            @block.vector
            def _(dve):
                dve.wait_ge(a["lam"], 16)
                link(dve, "dve", nc.vector.tensor_tensor(lam_p[:], lam_row[:, 0:4:2], lam_row[:, 1:4:2], ALU.mult))
                nc.vector.reduce_sum(lam_s[:, 0:2], lam_p[:], AX.X).then_inc(a["lam_x"], 1)
                dve.wait_ge(a["lam_e"], 1)
                link(dve, "dve", nc.vector.tensor_tensor(lam_s[:, 2:3], lam_s[:, 1:2], lam_s[:, 0:1], ALU.subtract))
                nc.vector.tensor_scalar(lam_s[:, 3:4], lam_s[:, 2:3], -LAM_INIT, None, ALU.add).then_inc(a["lam_x"], 1)
                for k in range(2 * HEADS):
                    dve.wait_ge(a["rot"], k + 1)
                    link(dve, "dve", nc.vector.tensor_tensor(rot_a[:, k % 2], banks[k % 4][:, 0:T2], sin_t, ALU.mult))
                    dve.wait_ge(a["rot_a"], k + 1)
                    nc.vector.tensor_tensor(yq[:, k], yq[:, k], rot_a[:, k % 2], ALU.add).then_inc(a["rot_d"], 1)
                dve.wait_ge(a["lam_mm"], 1)
                nc.vector.tensor_copy(lam[:], banks[6][:, 0:1])

            @block.gpsimd
            def _(pool):
                for k in range(2 * HEADS):
                    pool.wait_ge(a["rot"], k + 1)
                    nc.gpsimd.tensor_tensor(yq[:, k], yq[:, k], cos_t, ALU.mult).then_inc(a["rot_a"], 1)

            @block.scalar
            def _(act):
                act.wait_ge(a["lam_x"], 1)
                nc.scalar.activation(lam_s[:, 0:2], lam_s[:, 0:2], ACT.Exp).then_inc(a["lam_e"], 1)
                for n in range(6):
                    c, half = n // 2, n % 2
                    C = min(P, T2 - c * P)
                    act.wait_ge(a["vr"], n + 1)
                    nc.scalar.activation(v_at[0:C, c, 4 * half:4 * half + 4], heads4(banks[4 + n % 2])[0:C], ACT.Copy).then_inc(a["vr_out"], 1)

        prob = sb("prob", [P, 2, 2, T2], c=at_)
        attn = sb("attn", [P, 2, T2], c=at_)
        attn_tr = sb("attn_tr", [P, 2, 3, P], c=at_)
        smx = sb("smx", [P, 2, 10], c=at_)
        units = [(head, qt) for head in range(HEADS) for qt in range(3)]
        names = ("sc", "mask", "max", "nmax", "exp", "p0", "attn", "tr", "tr_out", "pv", "o_out")
        u_ = {n: sem("u_" + n) for n in names}
        with nc.Block() as block:
            def dims(n):
                head, qt = units[n]
                C = min(P, T2 - qt * P)
                return head, qt, C, qt * P + C

            @block.tensor
            def _(pe):
                for n in range(len(units) + 3):
                    if n < len(units):
                        head, qt, C, K = dims(n)
                        if n >= 2:
                            pe.wait_ge(u_["exp"], n - 1)
                        for comp in range(2):
                            ps = slice(64 * comp, 64 * comp + 64)
                            mm = nc.tensor.matmul(banks[2 * (n % 2) + comp][0:C, 0:K], yq[ps, head, qt * P:qt * P + C], yq[ps, HEADS + head, 0:K], start=True, stop=True)
                        mm.then_inc(u_["sc"], 1)
                    if 2 <= n < len(units) + 2:
                        m = n - 2
                        head, qt, C, K = dims(m)
                        pe.wait_ge(u_["attn"], m + 1)
                        if m >= 2:
                            pe.wait_ge(u_["tr_out"], m - 1)
                        for kt in range(qt + 1):
                            R = min(P, T2 - kt * P)
                            mm = nc.tensor.transpose(banks[4 + m % 2][0:R, kt * P:kt * P + C], attn[0:C, m % 2, kt * P:kt * P + R], ident[0:C, 0:C])
                        mm.then_inc(u_["tr"], 1)
                    if n >= 3:
                        head, qt, C, K = dims(n - 3)
                        pe.wait_ge(u_["tr_out"], n - 2)
                        if qt == 0 and head >= 2:
                            pe.wait_ge(u_["o_out"], head - 1)
                        for kt in range(qt + 1):
                            R = min(P, T2 - kt * P)
                            mm = nc.tensor.matmul(banks[6 + head % 2][:, qt * P:qt * P + C], v_at[0:R, kt, head], attn_tr[0:R, (n - 3) % 2, kt, 0:C], start=kt == 0, stop=kt == qt)
                        mm.then_inc(u_["pv"], 1)

            @block.vector
            def _(dve):
                scale = 64 ** -0.5

                def outputs(n):
                    if n >= 0 and units[n][1] == 2:
                        head = units[n][0]
                        dve.wait_ge(u_["pv"], n + 1)
                        nc.vector.tensor_copy(o_at[:, head], banks[6 + head % 2][:, 0:T2]).then_inc(u_["o_out"], 1)

                for n in range(len(units) + 1):
                    now, before = n < len(units), n > 0
                    if now:
                        head, qt, C, K = dims(n)
                        b = n % 2
                        dve.wait_ge(u_["sc"], n + 1)
                        for comp in range(2):
                            diag = banks[2 * b + comp][0:C, qt * P:qt * P + C]
                            ins = nc.vector.tensor_tensor(diag, diag, const("neg_from")[0:C, 0:C], ALU.add)
                        masked = mark("dve", ins)
                    if before:
                        _, _, C1, K1 = dims(n - 1)
                        b1 = (n - 1) % 2
                        m_ = smx[0:C1, b1]
                        dve.wait_ge(u_["exp"], n)
                        inverse = mark("dve", nc.vector.reciprocal(m_[:, 6:8], m_[:, 4:6]))
                    if now:
                        dve.wait_ge(step["dve"], masked)
                        for comp in range(2):
                            ins = nc.vector.reduce_max(smx[0:C, b, comp:comp + 1], banks[2 * b + comp][0:C, 0:K], AX.X)
                        top = mark("dve", ins)
                    if before:
                        dve.wait_ge(step["dve"], inverse)
                        weight = mark("dve", nc.vector.tensor_tensor(m_[:, 8:9], m_[:, 7:8], lam[0:C1], ALU.mult))
                        if n >= 3:
                            dve.wait_ge(u_["tr"], n - 2)
                        first = mark("dve", nc.vector.tensor_scalar(attn[0:C1, b1, 0:K1], prob[0:C1, b1, 0, 0:K1], m_[:, 6:7], None, ALU.mult))
                    if now:
                        dve.wait_ge(step["dve"], top)
                        nc.vector.tensor_scalar(smx[0:C, b, 2:4], smx[0:C, b, 0:2], -scale, None, ALU.mult).then_inc(u_["nmax"], 1)
                    if before:
                        dve.wait_ge(step["dve"], max(first, weight))
                        nc.vector.scalar_tensor_tensor(out=attn[0:C1, b1, 0:K1], in0=prob[0:C1, b1, 1, 0:K1], scalar=m_[:, 8:9], in1=attn[0:C1, b1, 0:K1],
                                                       op0=ALU.mult, op1=ALU.add).then_inc(u_["attn"], 1)
                    outputs(n - 4)
                for n in range(len(units) - 3, len(units)):
                    outputs(n)

            @block.scalar
            def _(act):
                def tr_copy(n):
                    head, qt, C, K = dims(n)
                    act.wait_ge(u_["tr"], n + 1)
                    if n >= 2:
                        act.wait_ge(u_["pv"], n - 1)
                    for kt in range(qt + 1):
                        R = min(P, T2 - kt * P)
                        ins = nc.scalar.activation(attn_tr[0:R, n % 2, kt, 0:C], banks[4 + n % 2][0:R, kt * P:kt * P + C], ACT.Copy)
                    ins.then_inc(u_["tr_out"], 1)
                for n in range(len(units)):
                    head, qt, C, K = dims(n)
                    b = n % 2
                    act.wait_ge(u_["nmax"], n + 1)
                    if n >= 2:
                        act.wait_ge(u_["attn"], n - 1)
                    for comp in range(2):
                        ins = nc.scalar.activation(prob[0:C, b, comp, 0:K], banks[2 * b + comp][0:C, 0:K], ACT.Exp, bias=smx[0:C, b, 2 + comp:3 + comp],
                                                   scale=64 ** -0.5, accum_out=smx[0:C, b, 4 + comp:5 + comp])
                    ins.then_inc(u_["exp"], 1)
                    if n >= 2:
                        tr_copy(n - 2)
                tr_copy(len(units) - 2)
                tr_copy(len(units) - 1)

        asq = sb("asq", [P, 2, T2], c=at_)
        art = sb("art", [P, 2, 4, T2], c=at_)
        names = ("sq", "sum", "ms", "y", "mid", "hi")
        b_ = {n: sem("b_" + n) for n in names}
        sub_w = sb("sub_w", [P, 1], c=at_)
        with nc.Block() as block:
            @block.scalar
            def _(act):
                def high(k):
                    act.wait_ge(b_["mid"], k + 1)
                    nc.scalar.activation(x_hi[:, k], o_at[:, k], ACT.Copy).then_inc(b_["hi"], 1)

                def root(k):
                    act.wait_ge(b_["ms"], k + 1)
                    if k >= 2:
                        act.wait_ge(b_["mid"], k - 1)
                    nc.scalar.activation(art[:, k % 2, 1], art[:, k % 2, 0], ACT.Abs_reciprocal_sqrt).then_inc(b_["y"], 1)
                for k in range(HEADS):
                    if k >= 2:
                        act.wait_ge(b_["sum"], k - 1)
                    nc.scalar.activation(asq[:, k % 2], o_at[:, k], ACT.Square).then_inc(b_["sq"], 1)
                    if k:
                        root(k - 1)
                    if k >= 2:
                        high(k - 2)
                root(HEADS - 1)
                high(HEADS - 2)
                high(HEADS - 1)

            @block.tensor
            def _(pe):
                for k in range(HEADS):
                    pe.wait_ge(b_["sq"], k + 1)
                    if k >= 2:
                        pe.wait_ge(b_["ms"], k - 1)
                    nc.tensor.matmul(banks[4 + k % 2][:, 0:T2], const("ones"), asq[:, k % 2], start=True, stop=True).then_inc(b_["sum"], 1)

            @block.vector
            def _(dve):
                link(dve, "dve", nc.vector.tensor_scalar(sub_w[:], col("od_subln_w_2", 0), 1.0 - LAM_INIT, None, ALU.mult))

                def low(k):
                    dve.wait_ge(b_["hi"], k + 1)
                    nc.vector.tensor_tensor(x_lo[:, k], o_at[:, k], x_hi[:, k].bitcast(F32), ALU.subtract)
                for n in range(HEADS + 1):
                    if n < HEADS:
                        dve.wait_ge(b_["sum"], n + 1)
                        nc.vector.tensor_scalar(art[:, n % 2, 0], banks[4 + n % 2][:, 0:T2], 1.0 / P, 1e-5, ALU.mult, ALU.add).then_inc(b_["ms"], 1)
                    if n == 0:
                        continue
                    k = n - 1
                    s_ = art[:, k % 2]
                    inverse_root(dve, b_["y"], k + 1, s_[:, 0], s_[:, 1], s_[:, 2], s_[:, 3])
                    nc.vector.scalar_tensor_tensor(out=o_at[:, k], in0=o_at[:, k], scalar=sub_w[:], in1=s_[:, 3], op0=ALU.mult, op1=ALU.mult).then_inc(b_["mid"], 1)
                    if k >= 2:
                        low(k - 2)
                low(HEADS - 2)
                low(HEADS - 1)
        at_.close()
        before_mlp = mixer_out(S["od_out"], 1, "1")
        mlp(S["mlp1_1"], S["mlp2_1"], 1, before_mlp, lambda: None)

        out_rows = sb("out_rows", [P, 2, D])
        f_tr, f_out, stored = sem("f_tr"), sem("f_out"), sem("stored")
        with nc.Block() as block:
            @block.tensor
            def _(pe):
                for n in range(4):
                    c, half = n // 2, n % 2
                    for k in range(4):
                        mm = nc.tensor.transpose(banks[n][:, k * P:(k + 1) * P], h[:, 4 * half + k, META + c * P:META + (c + 1) * P], ident)
                    mm.then_inc(f_tr, 1)

            @block.vector
            def _(dve):
                for n in range(4):
                    dve.wait_ge(f_tr, n + 1)
                    nc.vector.tensor_copy(out_rows[:, n // 2, 512 * (n % 2):512 * (n % 2) + 512], banks[n][:]).then_inc(f_out, 1)

            @block.sync
            def _(sp):
                rows = t["out"][0].rearrange("(c p) d -> p c d", p=P)
                for n in range(4):
                    cols = slice(512 * (n % 2), 512 * (n % 2) + 512)
                    sp.wait_ge(f_out, n + 1)
                    sp.dma_start(rows[:, n // 2, cols], out_rows[:, n // 2, cols]).then_inc(stored, 16)
                sp.wait_ge(stored, 64)


IN_NAMES = (
    "x", "c", "w_ada", "b_ada", "norm_ffn1", "w_ffn1_up", "w_ffn1_down", "norm_mix", "w_in", "conv_a",
    "conv_dn", "a_log_fwd", "dt_bias_fwd", "a_log_bwd", "dt_bias_bwd", "dn_norm", "w_a_out",
    "w_b_out", "w_out", "norm_ffn2", "w_ffn2_up", "w_ffn2_down", "norm_final", "meta_2",
    "norm_g_2", "mlp_w1_2", "mlp_w2_2", "ev_w_in_2", "ev_mu_2", "ev_w0_2", "ev_w_up_2", "ev_a0_2",
    "ev_a_up_2", "ev_g_up_2", "ev_k_k_2", "ev_k_a_2", "ev_r_k_2", "ev_ln_w_2", "ev_ln_b_2",
    "ev_pool_w_2", "ev_pool_scale_2", "ev_w_out_2", "od_w_in_2", "od_lambda_2", "od_subln_w_2",
    "od_w_out_2",
)


def kernel(**inputs):
    import concourse.bacc as bacc
    from concourse.bass_utils import run_bass_kernel_spmd

    nc = bacc.Bacc("TRN2", target_bir_lowering=False, num_devices=1)
    const_np, place, turning = constants()
    arrays = {name: np.ascontiguousarray(inputs[name]) for name in IN_NAMES}
    arrays["const"], arrays["turning"] = const_np, turning
    t = {name: nc.dram_tensor("in_" + name, a.shape, mybir.dt.from_np(a.dtype), kind="ExternalInput").ap()
         for name, a in arrays.items()}
    t["out"] = nc.dram_tensor("out_0", (1, T1, D), F32, kind="ExternalOutput").ap()
    build(nc, t, const_np, place)
    result = run_bass_kernel_spmd(nc, [{"in_" + name: a for name, a in arrays.items()}], core_ids=[0])
    return result.results[0]["out_0"]
```
